# Optimizing a Trainium2 kernel written in Bass

```python
import jax
import jax.numpy as jnp
from jax import lax
import numpy as np

D_MODEL = 1024
BATCH = 1
SEQ = 1024
DEPTH = 1

GRID_W = 64
CTX_LEN = 256
D_CONV = 512
N_NA_HEADS = 8
HEAD_DIM = 64
D_NA = N_NA_HEADS * HEAD_DIM
D_MIX = D_CONV + D_NA
D_IN = 2 * D_CONV + 3 * D_NA
CONV_WIDTH = 31
NA_ROWS = 8
NA_COLS = 16
NA_Q_COLS = 16
NA_KEY_COLS = 2 * NA_COLS
PEER_HEADS = 8
PEER_KEYS = 128
N_EXPERTS = PEER_KEYS * PEER_KEYS
PEER_DK = 256
PEER_TOPK = 16
PEER_CHUNK = 128
N_MOD = 6
EPS = 1e-6
NEG_INF = -1e30

kernel_name = "hybrid_conv_natten_peer_dit_block"

def rms_norm(x, g):
    xf = x.astype(jnp.float32)
    y = xf * lax.rsqrt(jnp.mean(xf * xf, axis=-1, keepdims=True) + EPS)
    return y.astype(x.dtype) * g

def layer_norm(x, g, b):
    xf = x.astype(jnp.float32)
    mu = jnp.mean(xf, axis=-1, keepdims=True)
    var = jnp.mean(jnp.square(xf - mu), axis=-1, keepdims=True)
    return ((xf - mu) * lax.rsqrt(var + EPS)).astype(x.dtype) * g + b

def conformer_conv(u, conv_w, conv_b, cn_g, cn_b):
    a, gate = jnp.split(u, 2, axis=-1)
    h = a * jax.nn.sigmoid(gate)
    h = lax.conv_general_dilated(
        h, conv_w[:, None, :].astype(h.dtype), window_strides=(1,),
        padding=[(CONV_WIDTH // 2, CONV_WIDTH // 2)],
        dimension_numbers=("NWC", "WIO", "NWC"), feature_group_count=D_CONV) + conv_b
    return jax.nn.silu(layer_norm(h, cn_g, cn_b))

def _na_tables(rows):
    wr = min(NA_ROWS, rows)
    ncb = GRID_W // NA_Q_COLS
    r = np.arange(rows)
    row_start = np.clip(r - wr // 2, 0, rows - wr)
    key_rows = row_start[:, None] + np.arange(wr)[None, :]
    j = np.arange(ncb)
    col_start = np.clip(j * NA_Q_COLS - NA_COLS // 2, 0, GRID_W - NA_KEY_COLS)
    key_cols = col_start[:, None] + np.arange(NA_KEY_COLS)[None, :]
    key_idx = key_rows[:, None, :, None] * GRID_W + key_cols[None, :, None, :]
    q_cols = j[:, None] * NA_Q_COLS + np.arange(NA_Q_COLS)[None, :]
    win_start = np.clip(q_cols - NA_COLS // 2, 0, GRID_W - NA_COLS)
    kc = key_cols[:, None, :]
    col_ok = (kc >= win_start[..., None]) & (kc < win_start[..., None] + NA_COLS)
    dr = key_rows - r[:, None] + NA_ROWS - 1
    dc = np.clip(kc - q_cols[..., None] + NA_COLS - 1, 0, 2 * NA_COLS - 2)
    return key_idx.reshape(rows, ncb, wr * NA_KEY_COLS).astype(np.int32), col_ok, dr, dc, wr

def neighbourhood_attention(q, k, v, k_ctx, v_ctx, rpb):
    b, l = q.shape[0], q.shape[1]
    rows = l // GRID_W
    ncb = GRID_W // NA_Q_COLS
    key_idx, col_ok, dr, dc, wr = _na_tables(rows)
    n_keys = wr * NA_KEY_COLS
    bias = rpb.astype(jnp.float32)[:, dr[:, None, None, :, None], dc[None, :, :, None, :]]
    bias = jnp.where(col_ok[None, None, :, :, None, :], bias, NEG_INF)
    bias = bias.reshape(N_NA_HEADS, rows, ncb, NA_Q_COLS, n_keys).transpose(1, 0, 2, 3, 4)
    q_rows = q.reshape(b, rows, ncb, NA_Q_COLS, N_NA_HEADS, HEAD_DIM).transpose(1, 0, 2, 3, 4, 5)
    scale = HEAD_DIM ** -0.5

    def row_fn(args):
        q_r, idx_r, bias_r = args
        kb = k[:, idx_r]
        vb = v[:, idx_r]
        s_loc = jnp.einsum("bjqhd,bjkhd->bhjqk", q_r, kb).astype(jnp.float32) * scale + bias_r
        s_ctx = jnp.einsum("bjqhd,bchd->bhjqc", q_r, k_ctx).astype(jnp.float32) * scale
        p = jax.nn.softmax(jnp.concatenate([s_loc, s_ctx], axis=-1), axis=-1).astype(v.dtype)
        return (jnp.einsum("bhjqk,bjkhd->bjqhd", p[..., :n_keys], vb)
                + jnp.einsum("bhjqc,bchd->bjqhd", p[..., n_keys:], v_ctx))

    o = lax.map(row_fn, (q_rows, jnp.asarray(key_idx), bias))
    return o.transpose(1, 0, 2, 3, 4, 5).reshape(b, l, D_NA)

def context_attention(q, k, v):
    b, lc = q.shape[0], q.shape[1]
    s = jnp.einsum("bqhd,bkhd->bhqk", q, k).astype(jnp.float32) * HEAD_DIM ** -0.5
    p = jax.nn.softmax(s, axis=-1).astype(v.dtype)
    return jnp.einsum("bhqk,bkhd->bqhd", p, v).reshape(b, lc, D_NA)

def split_heads(t):
    return t.reshape(t.shape[0], t.shape[1], N_NA_HEADS, HEAD_DIM)

def token_mixer(h_lat, h_ctx, w_in, conv_w, conv_b, cn_g, cn_b, rpb, w_out, with_ctx):
    p_lat = h_lat @ w_in
    q, k, v = [split_heads(t) for t in jnp.split(p_lat[..., 2 * D_CONV:], 3, axis=-1)]
    q_c, k_c, v_c = [split_heads(t) for t in jnp.split(h_ctx @ w_in[:, 2 * D_CONV:], 3, axis=-1)]
    conv_lat = conformer_conv(p_lat[..., :2 * D_CONV], conv_w, conv_b, cn_g, cn_b)
    na_lat = neighbourhood_attention(q, k, v, k_c, v_c, rpb)
    y_lat = jnp.concatenate([conv_lat, na_lat], axis=-1) @ w_out
    if not with_ctx:
        return y_lat, None
    conv_ctx = conformer_conv(h_ctx @ w_in[:, :2 * D_CONV], conv_w, conv_b, cn_g, cn_b)
    y_ctx = jnp.concatenate([conv_ctx, context_attention(q_c, k_c, v_c)], axis=-1) @ w_out
    return y_lat, y_ctx

def peer_ffn(h, w_q, sub_keys, u_emb, v_emb):
    shape = h.shape
    chunks = h.reshape(-1, PEER_CHUNK, D_MODEL)

    def chunk_fn(hc):
        n = hc.shape[0]
        qh = (hc @ w_q).reshape(n, PEER_HEADS, 2, PEER_DK // 2)
        s = jnp.einsum("nhpd,hpkd->nhpk", qh, sub_keys).astype(jnp.float32)
        s1, i1 = lax.top_k(s[:, :, 0], PEER_TOPK)
        s2, i2 = lax.top_k(s[:, :, 1], PEER_TOPK)
        cand_s = (s1[..., :, None] + s2[..., None, :]).reshape(n, PEER_HEADS, PEER_TOPK * PEER_TOPK)
        cand_i = (i1[..., :, None] * PEER_KEYS + i2[..., None, :]).reshape(n, PEER_HEADS, PEER_TOPK * PEER_TOPK)
        top_s, pos = lax.top_k(cand_s, PEER_TOPK)
        idx = jnp.take_along_axis(cand_i, pos, axis=-1)
        g = jax.nn.softmax(top_s, axis=-1).astype(hc.dtype)
        act = jax.nn.gelu(jnp.einsum("nd,nhkd->nhk", hc, u_emb[idx]))
        return jnp.einsum("nhk,nhkd->nd", g * act, v_emb[idx])

    return lax.map(chunk_fn, chunks).reshape(shape)

def setup_inputs(seed: int = 0) -> dict:
    key = jax.random.key(seed)
    ks = jax.random.split(key, 21)

    def nrm(k, shape, scale):
        return jax.random.normal(k, shape, jnp.float32) * scale

    L = DEPTH
    return {
        "x": nrm(ks[0], (BATCH, SEQ, D_MODEL), 1.0),
        "c": nrm(ks[1], (BATCH, D_MODEL), 1.0),
        "ctx": nrm(ks[2], (BATCH, CTX_LEN, D_MODEL), 1.0),
        "c_ctx": nrm(ks[3], (D_MODEL,), 1.0),
        "w_ada": nrm(ks[4], (L, D_MODEL, N_MOD * D_MODEL), 0.5 * D_MODEL ** -0.5),
        "b_ada": nrm(ks[5], (L, N_MOD * D_MODEL), 0.01),
        "g_pre_mix": 1.0 + nrm(ks[6], (L, D_MODEL), 0.01),
        "g_post_mix": 1.0 + nrm(ks[7], (L, D_MODEL), 0.01),
        "g_pre_ffn": 1.0 + nrm(ks[8], (L, D_MODEL), 0.01),
        "g_post_ffn": 1.0 + nrm(ks[9], (L, D_MODEL), 0.01),
        "w_in": nrm(ks[10], (L, D_MODEL, D_IN), D_MODEL ** -0.5),
        "conv_w": nrm(ks[11], (L, CONV_WIDTH, D_CONV), CONV_WIDTH ** -0.5),
        "conv_b": nrm(ks[12], (L, D_CONV), 0.01),
        "conv_norm_g": 1.0 + nrm(ks[13], (L, D_CONV), 0.01),
        "conv_norm_b": nrm(ks[14], (L, D_CONV), 0.01),
        "na_rpb": nrm(ks[15], (L, N_NA_HEADS, 2 * NA_ROWS - 1, 2 * NA_COLS - 1), 0.1),
        "w_out": nrm(ks[16], (L, D_MIX, D_MODEL), D_MIX ** -0.5),
        "peer_wq": nrm(ks[17], (L, D_MODEL, PEER_HEADS * PEER_DK), D_MODEL ** -0.5),
        "peer_keys": nrm(ks[18], (L, PEER_HEADS, 2, PEER_KEYS, PEER_DK // 2), (PEER_DK // 2) ** -0.5),
        "peer_u": nrm(ks[19], (L, N_EXPERTS, D_MODEL), D_MODEL ** -0.5),
        "peer_v": nrm(ks[20], (L, N_EXPERTS, D_MODEL), D_MODEL ** -0.5),
    }

def reference(x, c, ctx, c_ctx, w_ada, b_ada, g_pre_mix, g_post_mix, g_pre_ffn, g_post_ffn,
              w_in, conv_w, conv_b, conv_norm_g, conv_norm_b, na_rpb, w_out,
              peer_wq, peer_keys, peer_u, peer_v):
    x_lat, x_ctx = x, ctx
    for layer in range(DEPTH):
        with_ctx = layer < DEPTH - 1
        mod_lat = jax.nn.silu(c) @ w_ada[layer] + b_ada[layer]
        mod_ctx = jax.nn.silu(c_ctx) @ w_ada[layer] + b_ada[layer]
        sh1, sc1, gt1, sh2, sc2, gt2 = jnp.split(mod_lat[:, None, :], N_MOD, axis=-1)
        csh1, csc1, cgt1, csh2, csc2, cgt2 = jnp.split(mod_ctx, N_MOD, axis=-1)

        h_lat = rms_norm(x_lat, g_pre_mix[layer]) * (1.0 + sc1) + sh1
        h_ctx = rms_norm(x_ctx, g_pre_mix[layer]) * (1.0 + csc1) + csh1
        y_lat, y_ctx = token_mixer(h_lat, h_ctx, w_in[layer], conv_w[layer], conv_b[layer],
                                   conv_norm_g[layer], conv_norm_b[layer], na_rpb[layer],
                                   w_out[layer], with_ctx)
        x_lat = x_lat + gt1 * rms_norm(y_lat, g_post_mix[layer])

        h_lat = rms_norm(x_lat, g_pre_ffn[layer]) * (1.0 + sc2) + sh2
        f_lat = peer_ffn(h_lat, peer_wq[layer], peer_keys[layer], peer_u[layer], peer_v[layer])
        x_lat = x_lat + gt2 * rms_norm(f_lat, g_post_ffn[layer])

        if with_ctx:
            x_ctx = x_ctx + cgt1 * rms_norm(y_ctx, g_post_mix[layer])
            h_ctx = rms_norm(x_ctx, g_pre_ffn[layer]) * (1.0 + csc2) + csh2
            f_ctx = peer_ffn(h_ctx, peer_wq[layer], peer_keys[layer], peer_u[layer], peer_v[layer])
            x_ctx = x_ctx + cgt2 * rms_norm(f_ctx, g_post_ffn[layer])
    return x_lat


_drawn_inputs = setup_inputs


def setup_inputs(seed=0):
    import zlib

    import numpy as np

    out = dict(_drawn_inputs(seed))
    spreads = {}
    factors = {'g_pre_mix': 2.968,
     'g_post_mix': 3.194,
     'g_post_ffn': 8.0,
     'conv_norm_g': 2.877,
     'conv_norm_b': 3.53,
     'na_rpb': 3.279}
    for name, (base, spread) in spreads.items():
        noise = np.random.default_rng([zlib.crc32(name.encode()), seed]).standard_normal(out[name].shape)
        drawn = base * np.exp(spread * noise) if base else spread * noise
        out[name] = jnp.asarray(drawn.astype(out[name].dtype))
    for name, factor in factors.items():
        out[name] = (out[name] * factor).astype(out[name].dtype)
    return out
```

```python
from contextlib import ExitStack

import concourse.bass as bass
from concourse import mybir

F32 = mybir.dt.float32
BF16 = mybir.dt.bfloat16
U32 = mybir.dt.uint32
I32 = mybir.dt.int32
ALU = mybir.AluOpType
ACT = mybir.ActivationFunctionType
AX_X = mybir.AxisListType.X

P = 128
D = 1024
KD = D // P
SEQ = 1024
NT = SEQ // P
CTX = 256
CT = CTX // P
HALF = 512
NH = SEQ // HALF
N_MOD = 6
MODT = N_MOD * KD
D_CONV = 512
CC = D_CONV // P
TAPS = 31
PAD = TAPS // 2
HEADS = 8
HD = 64
D_NA = HEADS * HD
CA = D_NA // P
GRID_W = 64
ROWS = SEQ // GRID_W
WIN_R = 8
WIN_C = 16
PAIRS = ROWS // 2
EDGE_ROWS = [7, 5, 3, 1]
T_ROWS = 14
IN_ROWS = 9
BIAS_R = T_ROWS + IN_ROWS
EPS = 1e-6
NEG = -1e30
PH = 8
PK = 128
TOPK = 16
SUB = 2 * PH
EXPERTS = PK * PK
GROUP = 4
GROUPS = PK // GROUP

V_BADA = 0
V_GPRE1 = V_BADA + MODT
V_GPOST1 = V_GPRE1 + KD
V_GPRE2 = V_GPOST1 + KD
V_GPOST2 = V_GPRE2 + KD
V_CONVB = V_GPOST2 + KD
V_CNG = V_CONVB + CC
V_CNB = V_CNG + CC
V_CONVW = V_CNB + CC
V_COND = V_CONVW + CC * TAPS
V_END = V_COND + 2 * KD


class Count:

    def __init__(self, sem):
        self.sem, self.n = sem, 0

    def up(self, instruction):
        self.n += 1
        instruction.then_inc(self.sem, 1)
        return self.n

    def then_wait(self, engine, instruction):
        engine.wait_ge(self.sem, self.up(instruction))


def modulation(nc, io, keep):
    with ExitStack() as ctx:
        def sb(name, shape, dt=F32):
            return ctx.enter_context(nc.sbuf_tensor(f"modulation_{name}", shape, dt))

        def sem(name):
            return ctx.enter_context(nc.semaphore(f"modulation_{name}"))

        CH = 4
        NCH = MODT // CH
        RING = 3
        TT = NT + CT
        x_sb = sb("x_sb", [P, TT, D])
        w_sb = sb("w_ada_sb", [P, RING, KD, CH * P])
        silu_c = sb("silu_c", [P, KD, 2])
        square = sb("square", [P, 2, D])
        ssq = sb("ssq", [P, TT])
        std = sb("std", [P, TT])
        rstd = sb("rstd", [P, TT])
        gs1 = sb("gs1", [P, KD])
        cgs1 = sb("cgs1", [P, KD])
        cmod = sb("cmod", [P, 2 * KD])
        gate_col = sb("gate_col", [P, 2 * KD])
        diag = sb("diag", [P, 2 * KD, P])
        ones = sb("ones", [P, P])
        mod1_ps = ctx.enter_context(nc.psum_tensor("mod1_ps", [P, HALF], F32))
        mod2_ps = ctx.enter_context(nc.psum_tensor("mod2_ps", [P, HALF], F32))
        tr_ps = [ctx.enter_context(nc.psum_tensor(f"tr_ps{i}", [P, HALF], F32)) for i in range(4)]
        row_ps = [ctx.enter_context(nc.psum_tensor(f"row_ps{i}", [P, HALF], F32)) for i in range(2)]

        vec_in = sem("vec_in")
        x_in = [sem(f"x_in{t}") for t in range(TT)]
        w_in = [sem(f"w_ada_in{i}") for i in range(RING)]
        silu_done = sem("silu_done")
        ssq_done = sem("ssq_done")
        std_done = sem("std_done")
        xn_done = sem("xn_done")
        mod1_mm = sem("mod1_mm")
        chunk_used = sem("chunk_used")
        mod_done = sem("mod_done")
        dve = sem("dve")
        tr_done = sem("tr_done")
        act_evac = sem("act_evac")
        dve_evac = sem("dve_evac")
        diag_done = sem("diag_done")
        row_mm = sem("row_mm")
        ones_set = sem("ones_set")
        row_out = sem("row_out")

        vec, ident, hT, hcT, mod, gs2, rows1, rows2 = (
            keep[n] for n in ("vec", "ident", "hT", "hcT", "mod", "gs2", "rows1", "rows2"))
        mod_src = io["w_ada"].rearrange("(k p) c -> p k c", p=P)
        turns = [("x", 4 * q, 4, k) for q in range(NT // 4) for k in range(KD)] + [("c", NT, CT, k) for k in range(KD)]

        block = ctx.enter_context(nc.Block())

        @block.sync
        def _(sp):
            sp.dma_start(vec[:], io["vec"]).then_inc(vec_in, 16)
            sp.dma_start(ident[:], io["ident"]).then_inc(vec_in, 16)
            for n in range(NCH):
                if n >= RING:
                    sp.wait_ge(chunk_used, n - RING + 1)
                sp.dma_start(w_sb[:, n % RING], mod_src[:, :, n * CH * P:(n + 1) * CH * P]).then_inc(w_in[n % RING], 16)

        @block.scalar
        def _(act):
            for t in range(TT):
                src = io["x"][t * P:(t + 1) * P, :] if t < NT else io["ctx"][(t - NT) * P:(t - NT + 1) * P, :]
                act.dma_start(x_sb[:, t, :], src).then_inc(x_in[t], 16)
            act.wait_ge(vec_in, 32)
            nc.scalar.activation(silu_c[:].rearrange("p k c -> p (k c)"), vec[:, V_COND:V_END],
                                 ACT.Silu).then_inc(silu_done, 1)
            for t in range(TT):
                act.wait_ge(x_in[t], 16)
                if t >= 2:
                    act.wait_ge(ssq_done, t - 1)
                nc.scalar.activation(square[:, t % 2, :], x_sb[:, t, :], ACT.Square,
                                     accum_out=ssq[:, t:t + 1]).then_inc(ssq_done, 1)
            act.wait_ge(dve, 1)
            nc.scalar.activation(std[:], std[:], ACT.Sqrt).then_inc(std_done, 1)
            act.wait_ge(mod_done, 1)
            for n, (which, t0, nt, k) in enumerate(turns):
                if n % 2 == 0:
                    act.wait_ge(tr_done, n + 1)
                    dst = hT[:, k, t0 * P:(t0 + nt) * P] if which == "x" else hcT[:, k, :]
                    g, sh = (gs1, mod) if which == "x" else (cgs1, cmod)
                    nc.scalar.activation(dst, tr_ps[n % 4][:, 0:nt * P], ACT.Identity, bias=sh[:, k:k + 1],
                                         scale=g[:, k:k + 1]).then_inc(act_evac, 1)

        @block.gpsimd
        def _(pool):
            nc.gpsimd.memset(keep["eps"][:], EPS)
            nc.gpsimd.memset(ones[:], 1.0).then_inc(ones_set, 1)

        @block.tensor
        def _(pe):
            pe.wait_ge(silu_done, 1)

            def turn(n):
                which, t0, nt, k = turns[n]
                if n % 4 == 0:
                    pe.wait_ge(xn_done, t0 + nt)
                if n >= 4:
                    pe.wait_ge(act_evac if n % 2 == 0 else dve_evac, (n - 4) // 2 + 1)
                for j in range(nt):
                    last = nc.tensor.transpose(tr_ps[n % 4][:, j * P:(j + 1) * P], x_sb[:, t0 + j, k * P:(k + 1) * P],
                                               ident[:])
                last.then_inc(tr_done, 1)

            for n in range(NCH):
                pe.wait_ge(w_in[n % RING], 16 * (n // RING + 1))
                for c in range(CH):
                    m = n * CH + c
                    out = mod1_ps[:, 2 * m:2 * m + 2] if m < 2 * KD else mod2_ps[:, 2 * m:2 * m + 2]
                    for k in range(KD):
                        last = nc.tensor.matmul(out, w_sb[:, n % RING, k, c * P:(c + 1) * P], silu_c[:, k, :],
                                                start=(k == 0), stop=(k == KD - 1))
                last.then_inc(chunk_used, 1)
                if n >= 3:
                    for i in range(3 * (n - 3), min(3 * (n - 2), len(turns))):
                        turn(i)
            assert 3 * (NCH - 3) >= len(turns)
            pe.wait_ge(ones_set, 1)
            for g in range(4):
                pe.wait_ge(diag_done, 4 * g + 4)
                if g >= 2:
                    pe.wait_ge(row_out, g - 1)
                for j in range(4):
                    last = nc.tensor.matmul(row_ps[g % 2][:, j * P:(j + 1) * P], ones[:], diag[:, 4 * g + j, :],
                                            start=True, stop=True)
                last.then_inc(row_mm, 1)

        @block.vector
        def _(v):
            c = Count(dve)
            v.wait_ge(ssq_done, TT)
            c.up(nc.vector.tensor_scalar(std[:], ssq[:], 1.0 / D, EPS, ALU.mult, ALU.add))
            v.wait_ge(std_done, 1)
            c.then_wait(v, nc.vector.reciprocal(rstd[:], std[:]))
            for t in range(TT):
                nc.vector.tensor_scalar(x_sb[:, t, :], x_sb[:, t, :], rstd[:, t:t + 1], None,
                                        ALU.mult).then_inc(xn_done, 1)
            v.wait_ge(chunk_used, 2 * KD // CH)
            both = mod1_ps[:, 0:4 * KD].rearrange("p (m c) -> p m c", c=2)
            nc.vector.tensor_tensor(mod[:, 0:2 * KD], both[:, :, 0], vec[:, V_BADA:V_BADA + 2 * KD], ALU.add)
            c.then_wait(v, nc.vector.tensor_tensor(cmod[:], both[:, :, 1], vec[:, V_BADA:V_BADA + 2 * KD], ALU.add))
            g1 = vec[:, V_GPRE1:V_GPRE1 + KD]
            nc.vector.scalar_tensor_tensor(gs1[:], mod[:, KD:2 * KD], 1.0, g1, ALU.add, ALU.mult)
            nc.vector.scalar_tensor_tensor(cgs1[:], cmod[:, KD:2 * KD], 1.0, g1, ALU.add, ALU.mult).then_inc(mod_done, 1)
            v.wait_ge(mod_done, 1)
            for n, (which, t0, nt, k) in enumerate(turns):
                if n % 2 == 1:
                    v.wait_ge(tr_done, n + 1)
                    dst = hT[:, k, t0 * P:(t0 + nt) * P] if which == "x" else hcT[:, k, :]
                    g, sh = (gs1, mod) if which == "x" else (cgs1, cmod)
                    nc.vector.tensor_scalar(dst, tr_ps[n % 4][:, 0:nt * P], g[:, k:k + 1], sh[:, k:k + 1],
                                            ALU.mult, ALU.add).then_inc(dve_evac, 1)
            v.wait_ge(chunk_used, NCH)
            c.then_wait(v, nc.vector.tensor_tensor(
                mod[:, 2 * KD:], mod2_ps[:, 4 * KD:2 * MODT].rearrange("p (m c) -> p m c", c=2)[:, :, 0],
                vec[:, V_BADA + 2 * KD:V_BADA + MODT], ALU.add))
            nc.vector.scalar_tensor_tensor(gs2[:], mod[:, 4 * KD:5 * KD], 1.0, vec[:, V_GPRE2:V_GPRE2 + KD],
                                           ALU.add, ALU.mult)
            nc.vector.tensor_tensor(gate_col[:, 0:KD], mod[:, 2 * KD:3 * KD], vec[:, V_GPOST1:V_GPOST1 + KD], ALU.mult)
            c.then_wait(v, nc.vector.tensor_tensor(gate_col[:, KD:], mod[:, 5 * KD:6 * KD],
                                                   vec[:, V_GPOST2:V_GPOST2 + KD], ALU.mult))
            for k in range(2 * KD):
                nc.vector.tensor_scalar(diag[:, k, :], ident[:], gate_col[:, k:k + 1], None,
                                        ALU.mult).then_inc(diag_done, 1)
            for g in range(4):
                v.wait_ge(row_mm, g + 1)
                nc.vector.tensor_copy((rows1 if g < NH else rows2)[:, g % NH, :], row_ps[g % 2][:]).then_inc(row_out, 1)


def projection(nc, io, keep):
    with ExitStack() as ctx:
        def sb(name, shape, dt=F32):
            return ctx.enter_context(nc.sbuf_tensor(f"projection_{name}", shape, dt))

        def sem(name):
            return ctx.enter_context(nc.semaphore(f"projection_{name}"))

        vec, hT, hcT, conv, qT, kT, kcT, v_sb, vc_sb = (
            keep[n] for n in ("vec", "hT", "hcT", "conv", "qT", "kT", "kcT", "v_sb", "vc_sb"))
        RING = 4
        w_sb = sb("w_in_sb", [P, RING, KD, P])
        wv_sb = sb("wv_sb", [P, KD, D_NA])
        glu = sb("glu", [P, 2, SEQ + 2 * PAD])
        odd = sb("odd", [P, SEQ])
        sig = sb("sig", [P, 2, SEQ])
        square = sig[:].rearrange("p a (b n) -> p (a b) n", n=HALF)
        mean_w = sb("mean_w", [P, P])
        rstd_row = sb("rstd_row", [P, SEQ])
        BANKS = 8
        bank = [ctx.enter_context(nc.psum_tensor(f"proj_ps{i}", [P, HALF], F32)) for i in range(BANKS)]

        w_in = [sem(f"w_in{i}") for i in range(RING)]
        wv_in = sem("wv_in")
        piece_mm = sem("piece_mm")
        act_read = sem("act_read")
        dve_read = sem("dve_read")
        dve = sem("dve")
        glu_zero = sem("glu_zero")
        conv_done = sem("conv_done")
        sq_done = sem("sq_done")
        normed = sem("normed")
        mean_set = sem("mean_set")

        order = [t for c in range(CC) for t in (CC + c, c)] + list(range(2 * CC, 2 * CC + 2 * CA))
        kind_of = lambda t: "value" if t < CC else "gate" if t < 2 * CC else "q" if t < 2 * CC + CA else "k"
        pieces = []
        for t in order:
            pieces += [(kind_of(t), t % CC, h) for h in range(NH)]
            if kind_of(t) == "k":
                pieces.append(("kc", t % CC, 0))
        pieces += [("v", t, 0) for t in range(NT)] + [("vc", t, 0) for t in range(CT)]
        pieces += [("mean", 0, h) for h in range(NH)] + [("var", 0, h) for h in range(NH)]
        number = {p: n for n, p in enumerate(pieces)}
        by_dve = [p for p in pieces if p[0] in ("value", "mean")]
        by_act = [p for p in pieces if p not in by_dve]

        def last_piece(t):
            return number[("kc", t % CC, 0) if kind_of(t) == "k" else (kind_of(t), t % CC, NH - 1)]

        def wait_read(eng, p):
            if p in by_dve:
                eng.wait_ge(dve_read, by_dve.index(p) + 1)
            else:
                eng.wait_ge(act_read, by_act.index(p) + 1)

        block = ctx.enter_context(nc.Block())

        @block.sync
        def _(sp):
            for i, t in enumerate(order):
                if i >= RING:
                    sp.wait_ge(piece_mm, last_piece(order[i - RING]) + 1)
                sp.dma_start(w_sb[:, i % RING], io["w_in_t"][t]).then_inc(w_in[i % RING], 16)
                if i == RING - 1:
                    sp.dma_start(wv_sb[:], io["w_v"].rearrange("(k p) c -> p k c", p=P)).then_inc(wv_in, 16)

        @block.gpsimd
        def _(pool):
            nc.gpsimd.memset(mean_w[:], 1.0 / D_CONV).then_inc(mean_set, 1)
            nc.gpsimd.memset(glu[:, :, 0:PAD], 0.0)
            nc.gpsimd.memset(glu[:, :, PAD + SEQ:], 0.0).then_inc(glu_zero, 1)

        @block.tensor
        def _(pe):
            def make(n, terms, width=HALF):
                if n >= BANKS:
                    wait_read(pe, pieces[n - BANKS])
                for i, (w, m) in enumerate(terms):
                    last = nc.tensor.matmul(bank[n % BANKS][:, 0:width], w, m, start=(i == 0), stop=(i == len(terms) - 1))
                return last.then_inc(piece_mm, 1)

            for i, t in enumerate(order):
                pe.wait_ge(w_in[i % RING], 16 * (i // RING + 1))
                w = w_sb[:, i % RING]
                for h in range(NH):
                    last = make(number[(kind_of(t), t % CC, h)],
                                [(w[:, k, :], hT[:, k, h * HALF:(h + 1) * HALF]) for k in range(KD)])
                if kind_of(t) == "k":
                    last = make(number[("kc", t % CC, 0)], [(w[:, k, :], hcT[:, k, :]) for k in range(KD)], CTX)
            pe.wait_ge(wv_in, 16)
            for t in range(NT):
                make(number[("v", t, 0)], [(hT[:, k, t * P:(t + 1) * P], wv_sb[:, k, :]) for k in range(KD)])
            for t in range(CT):
                make(number[("vc", t, 0)], [(hcT[:, k, t * P:(t + 1) * P], wv_sb[:, k, :]) for k in range(KD)])
            pe.wait_ge(mean_set, 1)
            pe.wait_ge(conv_done, CC)
            for h in range(NH):
                make(number[("mean", 0, h)], [(mean_w[:], conv[:, c, h * HALF:(h + 1) * HALF]) for c in range(CC)])
            for h in range(NH):
                pe.wait_ge(sq_done, CC * (h + 1))
                make(number[("var", 0, h)], [(mean_w[:], square[:, c, :]) for c in range(CC)])

        @block.scalar
        def _(act):
            for n, (kind, i, h) in enumerate(pieces):
                cols = slice(h * HALF, (h + 1) * HALF)
                src = bank[n % BANKS][:]
                if (kind, i, h) in by_dve:
                    continue
                if kind == "var":
                    for c in range(CC):
                        act.wait_ge(dve_read, by_dve.index(("mean", 0, h)) + 1)
                        if h > 0:
                            act.wait_ge(piece_mm, number[("var", 0, h - 1)] + 1)
                        nc.scalar.activation(square[:, c, :], conv[:, c, cols], ACT.Square).then_inc(sq_done, 1)
                act.wait_ge(piece_mm, n + 1)
                if kind == "gate":
                    if i >= 2:
                        act.wait_ge(dve_read, by_dve.index(("value", i - 2, NH - 1)) + 1)
                    ins = nc.scalar.activation(sig[:, i % 2, cols], src, ACT.Sigmoid)
                elif kind == "q":
                    ins = nc.scalar.activation(qT[:, i, cols], src, ACT.Copy, scale=HD ** -0.5)
                elif kind == "k":
                    ins = nc.scalar.copy(kT[:, i, cols], src)
                elif kind == "kc":
                    ins = nc.scalar.copy(kcT[:, i, :], src[:, 0:CTX])
                elif kind == "v":
                    ins = nc.scalar.copy(v_sb[:, i, :], src)
                elif kind == "vc":
                    ins = nc.scalar.copy(vc_sb[:, i, :], src)
                else:
                    ins = nc.scalar.activation(rstd_row[:, cols], src, ACT.Sqrt, bias=keep["eps"][:, 0:1])
                ins.then_inc(act_read, 1)
            for c in range(CC):
                act.wait_ge(normed, c + 1)
                nc.scalar.activation(conv[:, c, :], conv[:, c, :], ACT.Silu, bias=vec[:, V_CNB + c:V_CNB + c + 1],
                                     scale=vec[:, V_CNG + c:V_CNG + c + 1])

        @block.vector
        def _(v):
            ch = Count(dve)
            v.wait_ge(glu_zero, 1)

            def gated(c):
                for h in range(NH):
                    v.wait_ge(piece_mm, number[("value", c, h)] + 1)
                    v.wait_ge(act_read, by_act.index(("gate", c, h)) + 1)
                    cols = slice(h * HALF, (h + 1) * HALF)
                    nc.vector.tensor_tensor(glu[:, c % 2, PAD + h * HALF:PAD + (h + 1) * HALF],
                                            bank[number[("value", c, h)] % BANKS][:], sig[:, c % 2, cols],
                                            ALU.mult).then_inc(dve_read, 1)

            def depthwise(c):
                v.wait_ge(dve_read, by_dve.index(("value", c, NH - 1)) + 1)
                made = []
                for tap in range(TAPS):
                    w = vec[:, V_CONVW + c * TAPS + tap:V_CONVW + c * TAPS + tap + 1]
                    src = glu[:, c % 2, tap:tap + SEQ]
                    acc = conv[:, c, :] if tap % 2 == 0 else odd[:]
                    if tap >= 2:
                        v.wait_ge(dve, made[tap - 2])
                    if tap == 1 and c >= 1:
                        v.wait_ge(conv_done, c)
                    if tap == 0:
                        ins = nc.vector.tensor_scalar(acc, src, w, vec[:, V_CONVB + c:V_CONVB + c + 1], ALU.mult, ALU.add)
                    elif tap == 1:
                        ins = nc.vector.tensor_scalar(acc, src, w, None, ALU.mult)
                    else:
                        ins = nc.vector.scalar_tensor_tensor(acc, src, w, acc, ALU.mult, ALU.add)
                    made.append(ch.up(ins))
                v.wait_ge(dve, made[-1])
                nc.vector.tensor_tensor(conv[:, c, :], conv[:, c, :], odd[:], ALU.add).then_inc(conv_done, 1)

            gated(0)
            gated(1)
            for c in range(CC):
                depthwise(c)
                if c + 2 < CC:
                    gated(c + 2)
            v.wait_ge(conv_done, CC)
            for h in range(NH):
                n = number[("mean", 0, h)]
                v.wait_ge(piece_mm, n + 1)
                for c in range(CC):
                    cols = slice(h * HALF, (h + 1) * HALF)
                    ins = nc.vector.tensor_tensor(conv[:, c, cols], conv[:, c, cols], bank[n % BANKS][:], ALU.subtract)
                ins.then_inc(dve_read, 1)
            v.wait_ge(act_read, len(by_act))
            ch.then_wait(v, nc.vector.reciprocal(rstd_row[:], rstd_row[:]))
            for c in range(CC):
                nc.vector.tensor_tensor(conv[:, c, :], conv[:, c, :], rstd_row[:], ALU.mult).then_inc(normed, 1)


def attention(nc, io, keep):
    with ExitStack() as ctx:
        def sb(name, shape, dt=F32):
            return ctx.enter_context(nc.sbuf_tensor(f"attention_{name}", shape, dt))

        def sem(name):
            return ctx.enter_context(nc.semaphore(f"attention_{name}"))

        ident, att, qT, kT, kcT, v_sb, vc_sb = (
            keep[n] for n in ("ident", "att", "qT", "kT", "kcT", "v_sb", "vc_sb"))
        bias = sb("bias", [P, HEADS, BIAS_R * GRID_W])
        LAT = IN_ROWS * GRID_W
        KB = (LAT + P - 1) // P
        KEYS = LAT + CTX
        score = sb("score", [P, 2, KEYS])
        probT = sb("probT", [P, 2, (KB + CT) * P])
        mask = probT[:].rearrange("p s k -> p (s k)")[:, 0:BIAS_R * GRID_W]
        top = sb("top", [P, 2, 2])
        neg_max = sb("neg_max", [P, 2])
        sums = sb("sums", [P, 2, 2])
        rsum = sb("rsum", [P, 2])
        heads_out = sb("heads_out", [P, 2, D_NA])
        s_ps = [ctx.enter_context(nc.psum_tensor(f"s_ps{i}", [P, 2 * HALF], F32)) for i in range(2)]
        pt_ps = ctx.enter_context(nc.psum_tensor("pt_ps", [P, 2 * HALF], F32))
        o_ps = ctx.enter_context(nc.psum_tensor("o_ps", [P, HALF], F32))
        ot_ps = ctx.enter_context(nc.psum_tensor("ot_ps", [P, HALF], F32))

        bias_in = [sem(f"bias_in{h}") for h in range(HEADS)]
        mask_in = sem("mask_in")
        bias_done = sem("bias_done")
        scores_mm = sem("scores_mm")
        biased = sem("biased")
        neg_done = sem("neg_done")
        exp_done = sem("exp_done")
        prob_turned = sem("prob_turned")
        probT_done = sem("probT_done")
        out_mm = sem("out_mm")
        out_done = sem("out_done")
        outT_mm = sem("outT_mm")
        outT_done = sem("outT_done")
        dve = sem("dve")

        plan = []
        for j in range(PAIRS):
            lo = min(max(2 * j - WIN_R // 2, 0), ROWS - WIN_R)
            hi = min(max(2 * j + 1 - WIN_R // 2, 0), ROWS - WIN_R)
            if lo == hi:
                plan.append((lo, WIN_R, EDGE_ROWS[j if j < 2 else j - PAIRS + 4] - 1))
            else:
                plan.append((lo, IN_ROWS, T_ROWS))
            assert lo % 2 == 0
        units = [(j, h) for j in range(PAIRS) for h in range(HEADS)]

        block = ctx.enter_context(nc.Block())

        @block.sync
        def _(sp):
            sp.dma_start(mask, io["mask"]).then_inc(mask_in, 16)
            for h in range(HEADS):
                src = io["rpb_t"][h]
                edge, inner = T_ROWS * GRID_W, IN_ROWS * GRID_W
                sp.dma_start(bias[0:GRID_W, h, 0:edge], src[:, 1:1 + T_ROWS, :].rearrange("q r c -> q (r c)")).then_inc(bias_in[h], 16)
                sp.dma_start(bias[GRID_W:P, h, 0:edge], src[:, 0:T_ROWS, :].rearrange("q r c -> q (r c)")).then_inc(bias_in[h], 16)
                sp.dma_start(bias[0:GRID_W, h, edge:edge + inner], src[:, 3:3 + IN_ROWS, :].rearrange("q r c -> q (r c)")).then_inc(bias_in[h], 16)
                sp.dma_start(bias[GRID_W:P, h, edge:edge + inner], src[:, 2:2 + IN_ROWS, :].rearrange("q r c -> q (r c)")).then_inc(bias_in[h], 16)

        @block.tensor
        def _(pe):
            def scores(u):
                j, h = units[u]
                r0, nr, _ = plan[j]
                if u >= 2:
                    pe.wait_ge(biased, u - 1)
                    pe.wait_ge(exp_done, u - 1)
                part = slice(HD * (h % 2), HD * (h % 2) + HD)
                q = qT[part, h // 2, j * P:(j + 1) * P]
                k0, nk = r0 * GRID_W, nr * GRID_W
                nc.tensor.matmul(s_ps[u % 2][:, 0:HALF], q, kT[part, h // 2, k0:k0 + HALF], start=True, stop=True)
                if nk > HALF:
                    nc.tensor.matmul(s_ps[u % 2][:, HALF:nk], q, kT[part, h // 2, k0 + HALF:k0 + nk],
                                     start=True, stop=True)
                nc.tensor.matmul(s_ps[u % 2][:, LAT:KEYS], q, kcT[part, h // 2, :], start=True,
                                 stop=True).then_inc(scores_mm, 1)

            def blocks(u):
                j, h = units[u]
                r0, nr, _ = plan[j]
                cols = slice(h * HD, (h + 1) * HD)
                out = []
                for b in range((nr * GRID_W + P - 1) // P):
                    n = min(P, nr * GRID_W - b * P)
                    out.append((b * P, n, v_sb[0:n, r0 * GRID_W // P + b, cols]))
                return out + [(LAT + b * P, P, vc_sb[:, b, cols]) for b in range(CT)]

            def values(u):
                j, h = units[u]
                pe.wait_ge(exp_done, u + 1)
                if u >= 1:
                    pe.wait_ge(probT_done, u)
                for b, (c, n, _) in enumerate(blocks(u)):
                    last = nc.tensor.transpose(pt_ps[0:n, b * P:(b + 1) * P], score[:, u % 2, c:c + n], ident[:])
                last.then_inc(prob_turned, 1)

            def outputs(u):
                j, h = units[u]
                pe.wait_ge(probT_done, u + 1)
                if u >= 1:
                    pe.wait_ge(out_done, u)
                bl = blocks(u)
                for b, (c, n, vals) in enumerate(bl):
                    last = nc.tensor.matmul(o_ps[:, 0:HD], probT[0:n, u % 2, b * P:(b + 1) * P], vals,
                                            start=(b == 0), stop=(b == len(bl) - 1))
                last.then_inc(out_mm, 1)

            def turned(j):
                pe.wait_ge(out_done, HEADS * (j + 1))
                if j >= 1:
                    pe.wait_ge(outT_done, j)
                for c in range(CA):
                    last = nc.tensor.transpose(ot_ps[:, c * P:(c + 1) * P], heads_out[:, j % 2, c * P:(c + 1) * P], ident[:])
                last.then_inc(outT_mm, 1)

            for u in range(len(units) + 2):
                if u < len(units):
                    scores(u)
                if 1 <= u <= len(units):
                    values(u - 1)
                if u >= 2:
                    outputs(u - 2)
                    if (u - 2) % HEADS == HEADS - 1:
                        turned((u - 2) // HEADS)

        @block.scalar
        def _(act):
            def probs(u):
                nk = plan[units[u][0]][1] * GRID_W
                act.wait_ge(neg_done, u + 1)
                if u >= 2:
                    act.wait_ge(prob_turned, u - 1)
                    act.wait_ge(out_done, u - 1)
                nc.scalar.activation(score[:, u % 2, 0:nk], score[:, u % 2, 0:nk], ACT.Exp,
                                     bias=neg_max[:, u % 2:u % 2 + 1], accum_out=sums[:, u % 2, 0:1])
                nc.scalar.activation(score[:, u % 2, LAT:KEYS], s_ps[u % 2][:, LAT:KEYS], ACT.Exp,
                                     bias=neg_max[:, u % 2:u % 2 + 1], accum_out=sums[:, u % 2, 1:2]).then_inc(exp_done, 1)

            def copy_probs(u):
                act.wait_ge(prob_turned, u + 1)
                if u == 0:
                    act.wait_ge(bias_done, HEADS)
                if u >= 2:
                    act.wait_ge(out_mm, u - 1)
                nb = (plan[units[u][0]][1] * GRID_W + P - 1) // P
                full = plan[units[u][0]][1] * GRID_W // P
                for a, b, n in ((0, full, P), (full, nb, GRID_W), (nb, nb + CT, P)):
                    if b > a:
                        ins = nc.scalar.copy(probT[0:n, u % 2, a * P:b * P], pt_ps[0:n, a * P:b * P])
                ins.then_inc(probT_done, 1)

            for u in range(len(units) + 1):
                if u < len(units):
                    probs(u)
                if u >= 1:
                    copy_probs(u - 1)

        @block.vector
        def _(v):
            ch = Count(dve)
            v.wait_ge(mask_in, 16)
            for h in range(HEADS):
                v.wait_ge(bias_in[h], 64)
                nc.vector.tensor_tensor(bias[:, h, :], bias[:, h, :], mask, ALU.add).then_inc(bias_done, 1)

            def biased_scores(u):
                j, h = units[u]
                _, nr, t0 = plan[j]
                nk = nr * GRID_W
                v.wait_ge(scores_mm, u + 1)
                if u < HEADS:
                    v.wait_ge(bias_done, h + 1)
                if u >= 2:
                    v.wait_ge(prob_turned, u - 1)
                    v.wait_ge(exp_done, u - 1)
                nc.vector.tensor_tensor_reduce(score[:, u % 2, 0:nk], s_ps[u % 2][:, 0:nk],
                                               bias[:, h, t0 * GRID_W:t0 * GRID_W + nk], 1.0, NEG,
                                               ALU.add, ALU.max, top[:, u % 2, 0:1])
                nc.vector.tensor_reduce(top[:, u % 2, 1:2], s_ps[u % 2][:, LAT:KEYS], AX_X,
                                        ALU.max).then_inc(biased, 1)
                v.wait_ge(biased, u + 1)
                nc.vector.tensor_reduce(neg_max[:, u % 2:u % 2 + 1], top[:, u % 2, :], AX_X, ALU.max,
                                        negate=True).then_inc(neg_done, 1)

            def normalise(u):
                j, h = units[u]
                v.wait_ge(exp_done, u + 1)
                ch.then_wait(v, nc.vector.tensor_reduce(rsum[:, u % 2:u % 2 + 1], sums[:, u % 2, :], AX_X, ALU.add))
                ch.then_wait(v, nc.vector.reciprocal(rsum[:, u % 2:u % 2 + 1], rsum[:, u % 2:u % 2 + 1]))
                v.wait_ge(out_mm, u + 1)
                if h == 0 and j >= 2:
                    v.wait_ge(outT_mm, j - 1)
                nc.vector.tensor_scalar(heads_out[:, j % 2, h * HD:(h + 1) * HD], o_ps[:, 0:HD],
                                        rsum[:, u % 2:u % 2 + 1], None, ALU.mult).then_inc(out_done, 1)

            def place(j):
                v.wait_ge(outT_mm, j + 1)
                nc.vector.tensor_copy(att[:, :, j * P:(j + 1) * P],
                                      ot_ps[:].rearrange("p (c n) -> p c n", c=CA)).then_inc(outT_done, 1)

            for u in range(len(units) + 2):
                if u < len(units):
                    biased_scores(u)
                if u >= 2:
                    if (u - 2) % HEADS == 0 and u > 2:
                        place((u - 2) // HEADS - 1)
                    normalise(u - 2)
            place(PAIRS - 1)


def output(nc, io, keep):
    with ExitStack() as ctx:
        def sb(name, shape, dt=F32):
            return ctx.enter_context(nc.sbuf_tensor(f"output_{name}", shape, dt))

        def sem(name):
            return ctx.enter_context(nc.semaphore(f"output_{name}"))

        ident, conv, att, hT, mod, gs2, rows1 = (
            keep[n] for n in ("ident", "conv", "att", "hT", "mod", "gs2", "rows1"))
        w_sb = sb("w_out_sb", [P, KD, D])
        x_sb = sb("x_res", [P, NT, D])
        square = sb("square", [P, 2, D])
        work = sb("work", [P, 2, D])
        ssq = sb("ssq", [P, 2, NT])
        std = sb("std", [P, 2, NT])
        rstd = sb("rstd", [P, 2, NT])
        y_ps = [ctx.enter_context(nc.psum_tensor(f"y_ps{i}", [P, D], F32)) for i in range(2)]
        t_ps = [ctx.enter_context(nc.psum_tensor(f"t_ps{i}", [P, D], F32)) for i in range(2)]

        w_in = [sem(f"w_out_in{k}") for k in range(KD)]
        x_in = [sem(f"x_res_in{t}") for t in range(NT)]
        y_mm = sem("y_mm")
        y_ssq = sem("y_ssq")
        y_ms = sem("y_ms")
        y_std = sem("y_std")
        x2_done = sem("x2_done")
        x2_out = sem("x2_out")
        x2_ssq = sem("x2_ssq")
        x2_ms = sem("x2_ms")
        x2_std = sem("x2_std")
        normed = sem("normed")
        t_mm = sem("t_mm")
        t_act = sem("t_act")
        t_dve = sem("t_dve")
        dve = sem("dve")

        block = ctx.enter_context(nc.Block())

        @block.sync
        def _(sp):
            for k in range(KD):
                sp.dma_start(w_sb[:, k, :], io["w_out"][k * P:(k + 1) * P, :]).then_inc(w_in[k], 16)
            for t in range(NT):
                sp.dma_start(x_sb[:, t, :], io["x"][t * P:(t + 1) * P, :]).then_inc(x_in[t], 16)
            for t in range(NT):
                sp.wait_ge(x2_done, t + 1)
                sp.dma_start(io["x2"][t * P:(t + 1) * P, :], x_sb[:, t, :]).then_inc(x2_out, 16)
            sp.wait_ge(x2_out, 16 * NT)

        @block.tensor
        def _(pe):
            def product(t):
                if t >= 2:
                    pe.wait_ge(x2_done, t - 1)
                for h in range(NH):
                    for k in range(KD):
                        if t == 0 and h == 0:
                            pe.wait_ge(w_in[k], 16)
                        last = nc.tensor.matmul(y_ps[t % 2][:, h * HALF:(h + 1) * HALF], (conv[:, k, :] if k < CC else att[:, k - CC, :])[:, t * P:(t + 1) * P],
                                                w_sb[:, k, h * HALF:(h + 1) * HALF], start=(k == 0), stop=(k == KD - 1))
                last.then_inc(y_mm, 1)

            def turn(t):
                pe.wait_ge(normed, t + 1)
                if t >= 2:
                    pe.wait_ge(t_act, t - 1)
                    pe.wait_ge(t_dve, t - 1)
                for k in range(KD):
                    last = nc.tensor.transpose(t_ps[t % 2][:, k * P:(k + 1) * P], work[:, t % 2, k * P:(k + 1) * P], ident[:])
                last.then_inc(t_mm, 1)

            for t in range(NT + 1):
                if t < NT:
                    product(t)
                if t >= 1:
                    turn(t - 1)

        @block.scalar
        def _(act):
            for t in range(NT):
                act.wait_ge(y_mm, t + 1)
                nc.scalar.activation(square[:, 0, :], y_ps[t % 2][:], ACT.Square,
                                     accum_out=ssq[:, 0, t:t + 1]).then_inc(y_ssq, 1)
                act.wait_ge(y_ms, t + 1)
                nc.scalar.activation(std[:, 0, t:t + 1], std[:, 0, t:t + 1], ACT.Sqrt).then_inc(y_std, 1)
                act.wait_ge(x2_done, t + 1)
                nc.scalar.activation(square[:, 1, :], x_sb[:, t, :], ACT.Square,
                                     accum_out=ssq[:, 1, t:t + 1]).then_inc(x2_ssq, 1)
                act.wait_ge(x2_ms, t + 1)
                nc.scalar.activation(std[:, 1, t:t + 1], std[:, 1, t:t + 1], ACT.Sqrt).then_inc(x2_std, 1)
                act.wait_ge(t_mm, t + 1)
                for k in range(KD // 2):
                    ins = nc.scalar.activation(hT[:, k, t * P:(t + 1) * P], t_ps[t % 2][:, k * P:(k + 1) * P],
                                               ACT.Identity, bias=mod[:, 3 * KD + k:3 * KD + k + 1], scale=gs2[:, k:k + 1])
                ins.then_inc(t_act, 1)

        @block.vector
        def _(v):
            ch = Count(dve)
            for t in range(NT):
                y = y_ps[t % 2]
                v.wait_ge(y_ssq, t + 1)
                nc.vector.tensor_scalar(std[:, 0, t:t + 1], ssq[:, 0, t:t + 1], 1.0 / D, EPS, ALU.mult,
                                        ALU.add).then_inc(y_ms, 1)
                v.wait_ge(y_std, t + 1)
                ch.then_wait(v, nc.vector.reciprocal(rstd[:, 0, t:t + 1], std[:, 0, t:t + 1]))
                if t >= 2:
                    v.wait_ge(t_mm, t - 1)
                ch.then_wait(v, nc.vector.scalar_tensor_tensor(work[:, t % 2, :], y[:], rstd[:, 0, t:t + 1],
                                                               rows1[:].rearrange("p a b -> p (a b)"),
                                                               ALU.mult, ALU.mult))
                v.wait_ge(x_in[t], 16)
                nc.vector.tensor_tensor(x_sb[:, t, :], x_sb[:, t, :], work[:, t % 2, :], ALU.add).then_inc(x2_done, 1)
                v.wait_ge(x2_ssq, t + 1)
                nc.vector.tensor_scalar(std[:, 1, t:t + 1], ssq[:, 1, t:t + 1], 1.0 / D, EPS, ALU.mult,
                                        ALU.add).then_inc(x2_ms, 1)
                v.wait_ge(x2_std, t + 1)
                ch.then_wait(v, nc.vector.reciprocal(rstd[:, 1, t:t + 1], std[:, 1, t:t + 1]))
                nc.vector.tensor_scalar(work[:, t % 2, :], x_sb[:, t, :], rstd[:, 1, t:t + 1], None,
                                        ALU.mult).then_inc(normed, 1)
                v.wait_ge(t_mm, t + 1)
                for k in range(KD // 2, KD):
                    ins = nc.vector.tensor_scalar(hT[:, k, t * P:(t + 1) * P], t_ps[t % 2][:, k * P:(k + 1) * P],
                                                  gs2[:, k:k + 1], mod[:, 3 * KD + k:3 * KD + k + 1], ALU.mult, ALU.add)
                ins.then_inc(t_dve, 1)


A_ROWS = 4
B_COLS = 4
CAND_A = A_ROWS * TOPK
CAND = CAND_A + (TOPK - A_ROWS) * B_COLS
LOWEST = -3.0e38
ROUTE_STEPS = 143


def routing(nc, io, keep):
    with ExitStack() as ctx:
        def sb(name, shape, dt=F32):
            return ctx.enter_context(nc.sbuf_tensor(f"routing_{name}", shape, dt))

        def sem(name):
            return ctx.enter_context(nc.semaphore(f"routing_{name}"))

        hT, route = keep["hT"], keep["route"]
        wq_sb = sb("wq_sb", [P, 2, KD, P])
        key_sb = sb("key_sb", [P, 2, PK])
        iota16 = sb("iota16", [P, TOPK])
        qh = sb("qh", [P, 2, SEQ])
        sc = sb("sc", [P, 2, NT, PK])
        rest = sb("rest", [P, 2, NT, PK])
        best = sb("best", [P, 2, NT, TOPK])
        at = sb("at", [P, 2, NT, TOPK], U32)
        atf = sb("atf", [P, 2, NT, TOPK])
        cand = sb("cand", [P, NT, CAND])
        cand_rest = sb("cand_rest", [P, NT, CAND])
        top = sb("top", [P, NT, TOPK])
        pos = sb("pos", [P, NT, TOPK], U32)
        shr = sb("shr", [P, 2, NT, TOPK], U32)
        low = sb("low", [P, 2, NT, TOPK], U32)
        late = sb("late", [P, NT, TOPK])
        diff = sb("diff", [P, 2, NT, TOPK])
        rank = sb("rank", [P, 2, NT, TOPK])
        hot = sb("hot", [P, 2, NT * TOPK, TOPK])
        gate = sb("gate", [P, NT, TOPK])
        gsum = sb("gsum", [P, NT])
        q_ps = [ctx.enter_context(nc.psum_tensor(f"q_ps{i}", [P, NH * HALF], F32)) for i in range(2)]
        s_ps = [ctx.enter_context(nc.psum_tensor(f"sc_ps{i}", [P, NT, PK], F32)) for i in range(2)]

        w_in = [sem(f"wq_in{i}") for i in range(2)]
        key_in = [sem(f"key_in{i}") for i in range(2)]
        iota_in = sem("iota_in")
        q_mm = sem("q_mm")
        q_out = sem("q_out")
        s_mm = sem("s_mm")
        s_out = sem("s_out")
        found = sem("found")
        shifted = sem("shifted")
        exp_done = sem("gate_exp")
        dve = sem("dve")

        block = ctx.enter_context(nc.Block())

        @block.sync
        def _(sp):
            sp.dma_start(iota16[:], io["iota"][:, 0:TOPK]).then_inc(iota_in, 16)
            for s in range(2):
                sp.dma_start(wq_sb[:, s], io["wq_t"][s]).then_inc(w_in[s], 16)
                sp.dma_start(key_sb[:, s], io["keys_t"][s]).then_inc(key_in[s], 16)
            with sp.Fori(1, PH) as h:
                for s in range(2):
                    sp.wait_ge(q_mm, 2 * h + s - 1)
                    sp.dma_start(wq_sb[:, s], io["wq_t"][2 * h + s]).then_inc(w_in[s], 16)
                    sp.wait_ge(s_mm, 2 * h + s + 1)
                    sp.dma_start(key_sb[:, s], io["keys_t"][2 * h + s]).then_inc(key_in[s], 16)

        @block.tensor
        def _(pe):
            pe.sem_inc(q_out, 2)
            pe.sem_inc(s_out, 2)
            pe.sem_inc(s_mm, 2)
            with pe.Fori(0, PH) as h:
                for s in range(2):
                    pe.wait_ge(w_in[s], 16 * h + 16)
                    pe.wait_ge(q_out, 2 * h + s + 1)
                    for half in range(NH):
                        for k in range(KD):
                            last = nc.tensor.matmul(q_ps[s][:, half * HALF:(half + 1) * HALF], wq_sb[:, s, k, :],
                                                    hT[:, k, half * HALF:(half + 1) * HALF], start=(k == 0),
                                                    stop=(k == KD - 1))
                    last.then_inc(q_mm, 1)
                for s in range(2):
                    pe.wait_ge(q_out, 2 * h + s + 3)
                    pe.wait_ge(key_in[s], 16 * h + 16)
                    pe.wait_ge(s_out, 2 * h + s + 1)
                    for t in range(NT):
                        last = nc.tensor.matmul(s_ps[s][:, t, :], qh[:, s, t * P:(t + 1) * P], key_sb[:, s, :],
                                                start=True, stop=True)
                    last.then_inc(s_mm, 1)

        @block.scalar
        def _(act):
            with act.Fori(0, PH) as h:
                for s in range(2):
                    act.wait_ge(q_mm, 2 * h + s + 1)
                    act.wait_ge(s_mm, 2 * h + s + 1)
                    nc.scalar.copy(qh[:, s, :], q_ps[s][:]).then_inc(q_out, 1)
                for s in range(2):
                    act.wait_ge(s_mm, 2 * h + s + 3)
                    act.wait_ge(found, 2 * h + s + 1)
                    nc.scalar.copy(sc[:, s], s_ps[s][:]).then_inc(s_out, 1)
                act.wait_ge(shifted, h + 1)
                nc.scalar.activation(gate[:], gate[:], ACT.Exp).then_inc(exp_done, 1)

        @block.vector
        def _(v):
            v.wait_ge(iota_in, 16)
            v.sem_inc(found, 2)
            with v.Fori(0, PH) as h:
                c = Count(dve)

                def ready():
                    v.wait_ge(dve, ROUTE_STEPS * h + c.n)
                    v.nop(nofuse=True)

                for s in range(2):
                    v.wait_ge(s_out, 2 * h + s + 3)
                    v.nop(nofuse=True)
                    for t in range(NT):
                        c.up(nc.vector.max(best[:, s, t, 0:8], sc[:, s, t, :]))
                    ready()
                    for t in range(NT):
                        c.up(nc.vector.match_replace(rest[:, s, t, :], best[:, s, t, 0:8], sc[:, s, t, :], LOWEST))
                    for t in range(NT):
                        c.up(nc.vector.max_index(at[:, s, t, 0:8], best[:, s, t, 0:8], sc[:, s, t, :]))
                    ready()
                    v.sem_inc(found, 1)
                    for t in range(NT):
                        c.up(nc.vector.max(best[:, s, t, 8:16], rest[:, s, t, :]))
                    ready()
                    for t in range(NT):
                        c.up(nc.vector.max_index(at[:, s, t, 8:16], best[:, s, t, 8:16], rest[:, s, t, :]))
                ready()
                c.up(nc.vector.tensor_copy(atf[:], at[:]))
                a, b = best[:, 0], best[:, 1]
                c.up(nc.vector.tensor_tensor(
                    cand[:, :, 0:CAND_A].rearrange("p t (a b) -> p t a b", b=TOPK),
                    a[:, :, 0:A_ROWS].unsqueeze(3).to_broadcast([P, NT, A_ROWS, TOPK]),
                    b.unsqueeze(2).to_broadcast([P, NT, A_ROWS, TOPK]), ALU.add))
                c.up(nc.vector.tensor_tensor(
                    cand[:, :, CAND_A:].rearrange("p t (a b) -> p t a b", b=B_COLS),
                    a[:, :, A_ROWS:].unsqueeze(3).to_broadcast([P, NT, TOPK - A_ROWS, B_COLS]),
                    b[:, :, 0:B_COLS].unsqueeze(2).to_broadcast([P, NT, TOPK - A_ROWS, B_COLS]), ALU.add))
                ready()
                for t in range(NT):
                    c.up(nc.vector.max(top[:, t, 0:8], cand[:, t, :]))
                ready()
                for t in range(NT):
                    c.up(nc.vector.match_replace(cand_rest[:, t, :], top[:, t, 0:8], cand[:, t, :], LOWEST))
                for t in range(NT):
                    c.up(nc.vector.max_index(pos[:, t, 0:8], top[:, t, 0:8], cand[:, t, :]))
                ready()
                for t in range(NT):
                    c.up(nc.vector.max(top[:, t, 8:16], cand_rest[:, t, :]))
                ready()
                nc.vector.tensor_tensor(gate[:], top[:], top[:, :, 0:1].to_broadcast([P, NT, TOPK]),
                                        ALU.subtract).then_inc(shifted, 1)
                for t in range(NT):
                    c.up(nc.vector.max_index(pos[:, t, 8:16], top[:, t, 8:16], cand_rest[:, t, :]))
                ready()
                c.up(nc.vector.tensor_scalar(shr[:, 0], pos[:], 4, None, ALU.logical_shift_right))
                c.up(nc.vector.tensor_scalar(shr[:, 1], pos[:], 2, None, ALU.logical_shift_right))
                c.up(nc.vector.tensor_scalar(low[:, 0], pos[:], TOPK - 1, None, ALU.bitwise_and))
                c.up(nc.vector.tensor_scalar(low[:, 1], pos[:], B_COLS - 1, None, ALU.bitwise_and))
                c.up(nc.vector.tensor_scalar(late[:], pos[:], float(CAND_A), None, ALU.is_ge))
                ready()
                c.up(nc.vector.scalar_tensor_tensor(diff[:, 0], shr[:, 1], float(CAND_A // B_COLS - A_ROWS), shr[:, 0],
                                                    ALU.subtract, ALU.subtract))
                c.up(nc.vector.tensor_tensor(diff[:, 1], low[:, 1], low[:, 0], ALU.subtract))
                ready()
                for s in range(2):
                    c.up(nc.vector.tensor_tensor(diff[:, s], diff[:, s], late[:], ALU.mult))
                ready()
                c.up(nc.vector.tensor_tensor(rank[:, 0], diff[:, 0], shr[:, 0], ALU.add))
                c.up(nc.vector.tensor_tensor(rank[:, 1], diff[:, 1], low[:, 0], ALU.add))
                ready()
                flat = [P, NT * TOPK, TOPK]
                for s in range(2):
                    c.up(nc.vector.tensor_tensor(
                        hot[:, s], rank[:, s].rearrange("p t k -> p (t k)").unsqueeze(2).to_broadcast(flat),
                        iota16[:].unsqueeze(1).to_broadcast(flat), ALU.is_equal))
                ready()
                for s in range(2):
                    hs = hot[:, s].rearrange("p (t k) m -> p t k m", k=TOPK)
                    c.up(nc.vector.tensor_tensor(hs, hs, atf[:, s].unsqueeze(2).to_broadcast([P, NT, TOPK, TOPK]),
                                                 ALU.mult))
                ready()
                for s in range(2):
                    c.up(nc.vector.tensor_reduce(route[:, s, :, bass.ts(h, TOPK)],
                                                 hot[:, s].rearrange("p (t k) m -> p t k m", k=TOPK), AX_X, ALU.add))
                v.wait_ge(exp_done, h + 1)
                c.up(nc.vector.tensor_reduce(gsum[:], gate[:], AX_X, ALU.add))
                ready()
                c.up(nc.vector.reciprocal(gsum[:], gsum[:]))
                ready()
                c.up(nc.vector.tensor_tensor(route[:, 2, :, bass.ts(h, TOPK)], gate[:],
                                             gsum[:].unsqueeze(2).to_broadcast([P, NT, TOPK]), ALU.mult))
                ready()
                assert c.n == ROUTE_STEPS, c.n


SLOT = 64
PERG = HALF // PK
HOTS = 8


def gates(nc, io, keep):
    with ExitStack() as ctx:
        def sb(name, shape, dt=F32):
            return ctx.enter_context(nc.sbuf_tensor(f"gates_{name}", shape, dt))

        def sem(name):
            return ctx.enter_context(nc.semaphore(f"gates_{name}"))

        ident, route = keep["ident"], keep["route"]
        iota = sb("iota_sb", [P, PK])
        routeT = sb("routeT", [P, 3, SEQ])
        row_hot = sb("row_hot", [P, HOTS, PK])
        col_hot = sb("col_hot", [P, HOTS, PK])
        table = sb("table", [P, 2, PK, SLOT])
        t_ps = [ctx.enter_context(nc.psum_tensor(f"rt_ps{i}", [P, 4, P], F32)) for i in range(2)]
        g_ps = [ctx.enter_context(nc.psum_tensor(f"g_ps{i}", [P, PERG, PK], F32)) for i in range(4)]

        iota_in = sem("iota_in")
        turned = sem("turned")
        routeT_done = sem("routeT_done")
        hot_done = sem("hot_done")
        g_mm = sem("g_mm")
        g_out = sem("g_out")
        table_out = [sem(f"table_out{i}") for i in range(2)]

        ITER = 2 * SLOT
        TURNS = SEQ // ITER
        jobs = [(c, q) for c in range(3) for q in range(NT // 4)]

        block = ctx.enter_context(nc.Block())

        @block.sync
        def _(sp):
            sp.dma_start(iota[:], io["iota"]).then_inc(iota_in, 16)
            for s in range(2):
                sp.sem_inc(table_out[s], 16)
            with sp.Fori(0, TURNS) as i:
                for s in range(2):
                    sp.wait_ge(g_out, (2 * i + s + 1) * (SLOT // PERG) + 4)
                    sp.dma_start(io["gates"][2 * i + s], table[:, s]).then_inc(table_out[s], 16)
            for s in range(2):
                sp.wait_ge(table_out[s], 16 * (TURNS + 1))

        @block.tensor
        def _(pe):
            for n, (c, q) in enumerate(jobs):
                if n >= 2:
                    pe.wait_ge(routeT_done, n - 1)
                for j in range(4):
                    last = nc.tensor.transpose(t_ps[n % 2][:, j, :], route[:, c, 4 * q + j, :], ident[:])
                last.then_inc(turned, 1)
            pe.sem_inc(g_out, 4)
            pe.sem_inc(g_mm, HOTS // PERG)
            with pe.Fori(0, TURNS) as i:
                for b in range(ITER // PERG):
                    pe.wait_ge(g_out, i * (ITER // PERG) + b + 1)
                    for j in range(PERG):
                        n = b * PERG + j
                        pe.wait_ge(hot_done, 2 * (i * ITER + n) + 2)
                        last = nc.tensor.matmul(g_ps[b % 4][:, j, :], col_hot[:, n % HOTS, :], row_hot[:, n % HOTS, :],
                                                start=True, stop=True)
                    last.then_inc(g_mm, 1)

        @block.scalar
        def _(act):
            with act.Fori(0, TURNS) as i:
                for b in range(ITER // PERG):
                    s, n = divmod(b * PERG, SLOT)
                    if n == 0:
                        act.wait_ge(table_out[s], 16 * i + 16)
                    act.wait_ge(g_mm, i * (ITER // PERG) + b + 1 + HOTS // PERG)
                    nc.scalar.copy(table[:, s, :, n:n + PERG].rearrange("p i n -> p n i"),
                                   g_ps[b % 4][:]).then_inc(g_out, 1)

        @block.vector
        def _(v):
            for n, (c, q) in enumerate(jobs):
                v.wait_ge(turned, n + 1)
                nc.vector.tensor_copy(routeT[:, c, q * HALF:(q + 1) * HALF],
                                      t_ps[n % 2][:].rearrange("p a b -> p (a b)")).then_inc(routeT_done, 1)
            v.wait_ge(routeT_done, len(jobs))
            v.wait_ge(iota_in, 16)
            with v.Fori(0, TURNS) as i:
                for n in range(ITER):
                    tok = i * ITER + n
                    if n % PERG == 0:
                        v.wait_ge(g_mm, i * (ITER // PERG) + n // PERG + 1)
                    nc.vector.tensor_scalar(col_hot[:, n % HOTS, :], iota[:], routeT[:, 1, bass.ds(tok, 1)], None,
                                            ALU.is_equal).then_inc(hot_done, 1)
                    nc.vector.tensor_scalar(row_hot[:, n % HOTS, :], iota[:], routeT[:, 0, bass.ds(tok, 1)],
                                            routeT[:, 2, bass.ds(tok, 1)], ALU.is_equal, ALU.mult).then_inc(hot_done, 1)



def experts(nc, io, keep):
    with ExitStack() as ctx:
        def sb(name, shape, dt=F32):
            return ctx.enter_context(nc.sbuf_tensor(f"experts_{name}", shape, dt))

        def sem(name):
            return ctx.enter_context(nc.semaphore(f"experts_{name}"))

        hT, rows2 = keep["hT"], keep["rows2"]
        acc = sb("acc", [P, NT, NH, HALF])
        u_raw = sb("u_raw", [P, 2, D])
        v_raw = sb("v_raw", [P, D])
        u_part = sb("u_part", [P, GROUP, 2, D], BF16)
        v_part = sb("v_part", [P, 2, GROUP, 2, D], BF16)
        w_part = sb("w_part", [P, 2, GROUP, 2, SEQ], BF16)
        CHUNKS = SEQ // SLOT
        g_sb = sb("g_sb", [P, 2, CHUNKS, GROUP * SLOT])
        ACTS = 4
        act_sb = sb("act_sb", [P, ACTS, HALF])
        h_part = hT[:].bitcast(BF16).rearrange("p k (s n) -> p k s n", s=2)
        stat = sb("stat", [P, 3, NT])
        whole = acc[:].rearrange("p t h n -> p t (h n)")
        a_ps = [ctx.enter_context(nc.psum_tensor(f"a_ps{i}", [P, HALF], F32)) for i in range(4)]
        b_ps = [ctx.enter_context(nc.psum_tensor(f"b_ps{i}", [P, HALF], F32)) for i in range(4)]

        zero_done = sem("zero_done")
        h_raw_done = sem("h_raw_done")
        h_hi_done = sem("h_hi_done")
        h_lo_done = sem("h_lo_done")
        u_in = [sem(f"u_in{i}") for i in range(2)]
        v_in = sem("v_in")
        g_in = [sem(f"g_in{i}") for i in range(2)]
        u_hi = sem("u_hi")
        u_lo = sem("u_lo")
        v_hi = sem("v_hi")
        v_lo = sem("v_lo")
        a_mm = sem("a_mm")
        gelu_done = sem("gelu_done")
        prod_done = sem("prod_done")
        w_hi = sem("w_hi")
        w_lo = sem("w_lo")
        b_mm = sem("b_mm")
        acc_done = sem("acc_done")
        f_ssq = sem("f_ssq")
        f_ms = sem("f_ms")
        f_std = sem("f_std")
        f_rstd = sem("f_rstd")
        f_norm = sem("f_norm")
        f_done = sem("f_done")
        out_done = sem("out_done")

        UA = 2 * GROUP
        UB = NH * NT

        def schedule(eng, a, b):
            a(0, 0)
            a(1, 1)
            b(0, 0)
            with eng.Fori(0, (GROUPS - 4) // 2) as it:
                for s in range(2):
                    a(2 * it + s + 2, s)
                    b(2 * it + s + 1, 1 - s)
            for g in range(GROUPS - 3, GROUPS - 1):
                a(g + 1, (g + 1) % 2)
                b(g, g % 2)
            b(GROUPS - 1, 1)

        def within(g, n):
            return isinstance(g, int) and g >= GROUPS - n

        def wait(eng, semaphore, value):
            if not isinstance(value, int) or value > 0:
                eng.wait_ge(semaphore, value)

        block = ctx.enter_context(nc.Block())

        @block.sync
        def _(sp):
            def load_g(g, s):
                wait(sp, w_lo, UA * (g - 1))
                sp.dma_start(g_sb[:, s], io["gates"][:, :, bass.ts(g, GROUP), :].rearrange("c j i n -> j c (i n)"))\
                  .then_inc(g_in[s], 16)

            def load_u(g, i):
                wait(sp, u_lo, GROUP * g + i - 1)
                sp.dma_start(u_raw[:, i % 2], io["u_t"][GROUP * g + i]).then_inc(u_in[i % 2], 16)

            def load_v(g):
                for i in range(GROUP):
                    wait(sp, v_lo, GROUP * g + i)
                    sp.dma_start(v_raw[:], io["v"][GROUP * g + i]).then_inc(v_in, 16)

            def a(g, s):
                if isinstance(g, int) and g == 0:
                    load_u(0, 0)
                    load_g(0, 0)
                for i in range(1, GROUP):
                    load_u(g, i)
                if isinstance(g, int) and g == 0:
                    load_u(1, 0)
                    load_g(1, 1)
                    load_v(0)

            def b(g, s):
                if not within(g, 2):
                    load_g(g + 2, s)
                if not within(g, 1):
                    load_v(g + 1)
                if not within(g, 2):
                    load_u(g + 2, 0)

            schedule(sp, a, b)
            for t in range(NT):
                if t == 0:
                    sp.wait_ge(u_lo, PK)
                if t >= 2:
                    sp.wait_ge(f_done, t - 1)
                    sp.wait_ge(out_done, 16 * (t - 1))
                sp.dma_start(u_raw[:, t % 2], io["x2"][t * P:(t + 1) * P, :]).then_inc(u_in[t % 2], 16)
                if t >= 1:
                    sp.wait_ge(f_done, t)
                    sp.dma_start(io["out"][(t - 1) * P:t * P, :], u_raw[:, (t - 1) % 2]).then_inc(out_done, 16)
            sp.wait_ge(f_done, NT)
            sp.dma_start(io["out"][(NT - 1) * P:NT * P, :], u_raw[:, (NT - 1) % 2]).then_inc(out_done, 16)
            sp.wait_ge(out_done, 16 * NT)

        @block.tensor
        def _(pe):
            pe.wait_ge(h_lo_done, KD)

            def a(g, s):
                for i in range(GROUP):
                    pe.wait_ge(u_lo, GROUP * g + i + 1)
                    for h in range(NH):
                        n = NH * i + h
                        wait(pe, gelu_done, UA * g + n - 3)
                        terms = [(wp, mp, k) for wp, mp in ((0, 0), (0, 1), (1, 0)) for k in range(KD)]
                        for m, (wp, mp, k) in enumerate(terms):
                            last = nc.tensor.matmul(a_ps[n % 4][:], u_part[:, i, wp, k * P:(k + 1) * P],
                                                    h_part[:, k, mp, h * HALF:(h + 1) * HALF], start=(m == 0),
                                                    stop=(m == len(terms) - 1))
                        last.then_inc(a_mm, 1)

            def b(g, s):
                pe.wait_ge(w_lo, UA * g + UA)
                pe.wait_ge(v_lo, GROUP * g + GROUP)
                for t in range(NT):
                    for h in range(NH):
                        n = NH * t + h
                        wait(pe, acc_done, UB * g + n - 3)
                        terms = [(i, wp, vp) for i in range(GROUP) for wp, vp in ((0, 0), (0, 1), (1, 0))]
                        for m, (i, wp, vp) in enumerate(terms):
                            last = nc.tensor.matmul(b_ps[n % 4][:], w_part[:, s, i, wp, t * P:(t + 1) * P],
                                                    v_part[:, s, i, vp, h * HALF:(h + 1) * HALF], start=(m == 0),
                                                    stop=(m == len(terms) - 1))
                        last.then_inc(b_mm, 1)

            schedule(pe, a, b)

        @block.scalar
        def _(act):
            for k in range(KD):
                act.wait_ge(h_raw_done, k + 1)
                nc.scalar.copy(h_part[:, k, 0, :], whole[:, k, :]).then_inc(h_hi_done, 1)

            def take_u(g, i):
                e = GROUP * g + i
                act.wait_ge(u_in[i % 2], 2 * 16 * g + 16 * (i // 2 + 1))
                wait(act, a_mm, NH * (e - GROUP) + NH)
                nc.scalar.copy(u_part[:, i, 0, :], u_raw[:, i % 2]).then_inc(u_hi, 1)

            def take_v(g, s):
                wait(act, b_mm, UB * (g - 1))
                for i in range(GROUP):
                    act.wait_ge(v_in, 16 * (GROUP * g + i + 1))
                    nc.scalar.copy(v_part[:, s, i, 0, :], v_raw[:]).then_inc(v_hi, 1)

            def round_w(g, s, n):
                act.wait_ge(prod_done, UA * g + n + 1)
                if n == 0:
                    wait(act, b_mm, UB * (g - 1))
                i, h = divmod(n, NH)
                nc.scalar.copy(w_part[:, s, i, 0, h * HALF:(h + 1) * HALF], act_sb[:, n % ACTS, :]).then_inc(w_hi, 1)

            def a(g, s):
                if isinstance(g, int) and g == 0:
                    take_u(0, 0)
                for i in range(GROUP):
                    for h in range(NH):
                        n = NH * i + h
                        if h == 0 and i + 1 < GROUP:
                            take_u(g, i + 1)
                        act.wait_ge(a_mm, UA * g + n + 1)
                        wait(act, w_lo, UA * g + n - ACTS + 1)
                        nc.scalar.activation(act_sb[:, n % ACTS, :], a_ps[n % 4][:],
                                             ACT.Gelu_apprx_tanh).then_inc(gelu_done, 1)
                        if n >= 1:
                            round_w(g, s, n - 1)
                round_w(g, s, UA - 1)
                if isinstance(g, int) and g == 0:
                    take_u(1, 0)
                    take_v(0, 0)

            def b(g, s):
                if not within(g, 1):
                    take_v(g + 1, 1 - s)
                if not within(g, 2):
                    take_u(g + 2, 0)

            schedule(act, a, b)
            act.wait_ge(acc_done, GROUPS * UB)
            for t in range(NT):
                if t >= 1:
                    act.wait_ge(f_ssq, t)
                nc.scalar.activation(g_sb[:, 0, 0:4, :].rearrange("p a b -> p (a b)"),
                                     whole[:, t, :], ACT.Square,
                                     accum_out=stat[:, 0, t:t + 1]).then_inc(f_ssq, 1)
            act.wait_ge(f_ms, 1)
            nc.scalar.activation(stat[:, 1, :], stat[:, 1, :], ACT.Sqrt).then_inc(f_std, 1)

        @block.gpsimd
        def _(pool):
            def take_u(g, i):
                pool.wait_ge(u_hi, GROUP * g + i + 1)
                nc.gpsimd.tensor_tensor(u_part[:, i, 1, :], u_raw[:, i % 2], u_part[:, i, 0, :],
                                        ALU.subtract).then_inc(u_lo, 1)

            def take_v(g, s):
                for i in range(GROUP):
                    pool.wait_ge(v_hi, GROUP * g + i + 1)
                    nc.gpsimd.tensor_tensor(v_part[:, s, i, 1, :], v_raw[:], v_part[:, s, i, 0, :],
                                            ALU.subtract).then_inc(v_lo, 1)

            def a(g, s):
                if isinstance(g, int) and g == 0:
                    take_u(0, 0)
                for i in range(1, GROUP):
                    take_u(g, i)
                if isinstance(g, int) and g == 0:
                    take_u(1, 0)
                    take_v(0, 0)

            def b(g, s):
                if not within(g, 1):
                    take_v(g + 1, 1 - s)
                if not within(g, 2):
                    take_u(g + 2, 0)

            schedule(pool, a, b)

        @block.vector
        def _(v):
            for k in range(KD):
                nc.vector.tensor_copy(whole[:, k, :], hT[:, k, :]).then_inc(h_raw_done, 1)
            for k in range(KD):
                v.wait_ge(h_hi_done, k + 1)
                nc.vector.tensor_tensor(h_part[:, k, 1, :], whole[:, k, :], h_part[:, k, 0, :],
                                        ALU.subtract).then_inc(h_lo_done, 1)
            v.wait_ge(h_lo_done, KD)
            nc.vector.memset(acc[:], 0.0).then_inc(zero_done, 1)
            v.wait_ge(zero_done, 1)

            def low_w(g, s, n):
                i, h = divmod(n, NH)
                v.wait_ge(w_hi, UA * g + n + 1)
                nc.vector.tensor_tensor(w_part[:, s, i, 1, h * HALF:(h + 1) * HALF], act_sb[:, n % ACTS, :],
                                        w_part[:, s, i, 0, h * HALF:(h + 1) * HALF], ALU.subtract).then_inc(w_lo, 1)

            def a(g, s):
                for n in range(UA):
                    i, h = divmod(n, NH)
                    v.wait_ge(gelu_done, UA * g + n + 1)
                    if n == 0:
                        v.wait_ge(g_in[s], 8 * (g - s) + 16)
                    cs = slice(h * CHUNKS // NH, (h + 1) * CHUNKS // NH)
                    nc.vector.tensor_tensor(act_sb[:, n % ACTS, :].rearrange("p (c n) -> p c n", n=SLOT),
                                            act_sb[:, n % ACTS, :].rearrange("p (c n) -> p c n", n=SLOT),
                                            g_sb[:, s, cs, i * SLOT:(i + 1) * SLOT], ALU.mult).then_inc(prod_done, 1)
                    if n >= 1:
                        low_w(g, s, n - 1)
                low_w(g, s, UA - 1)

            def b(g, s):
                for n in range(UB):
                    t, h = divmod(n, NH)
                    v.wait_ge(b_mm, UB * g + n + 1)
                    wait(v, acc_done, UB * g + n - UB + 1)
                    nc.vector.tensor_tensor(acc[:, t, h, :], acc[:, t, h, :], b_ps[n % 4][:], ALU.add)\
                        .then_inc(acc_done, 1)

            schedule(v, a, b)
            v.wait_ge(f_ssq, NT)
            nc.vector.tensor_scalar(stat[:, 1, :], stat[:, 0, :], 1.0 / D, EPS, ALU.mult, ALU.add).then_inc(f_ms, 1)
            v.wait_ge(f_std, 1)
            nc.vector.reciprocal(stat[:, 2, :], stat[:, 1, :]).then_inc(f_rstd, 1)
            v.wait_ge(f_rstd, 1)
            for t in range(NT):
                f = whole[:, t, :]
                nc.vector.scalar_tensor_tensor(f, f, stat[:, 2, t:t + 1], rows2[:].rearrange("p a b -> p (a b)"),
                                               ALU.mult, ALU.mult).then_inc(f_norm, 1)
                v.wait_ge(f_norm, t + 1)
                v.wait_ge(u_in[t % 2], 16 * (PK // 2 + t // 2 + 1))
                nc.vector.tensor_tensor(u_raw[:, t % 2], u_raw[:, t % 2], f, ALU.add).then_inc(f_done, 1)

def build(nc, io):
    with ExitStack() as ctx:
        def sb(stack, name, shape, dt=F32):
            return stack.enter_context(nc.sbuf_tensor(name, shape, dt))

        keep = {
            "vec": sb(ctx, "vec_sb", [P, V_END]),
            "ident": sb(ctx, "ident_sb", [P, P]),
            "mod": sb(ctx, "mod", [P, MODT]),
            "gs2": sb(ctx, "gs2", [P, KD]),
            "eps": sb(ctx, "eps", [P, 1]),
            "rows2": sb(ctx, "rows2", [P, NH, HALF]),
            "hT": sb(ctx, "hT", [P, KD, SEQ]),
        }
        with ExitStack() as mix:
            keep["rows1"] = sb(mix, "rows1", [P, NH, HALF])
            keep["conv"] = sb(mix, "conv", [P, CC, SEQ])
            keep["att"] = sb(mix, "att", [P, CA, SEQ])
            with ExitStack() as heads:
                keep["hcT"] = sb(heads, "hcT", [P, KD, CTX])
                modulation(nc, io, keep)
                for name, shape in (("qT", [P, CA, SEQ]), ("kT", [P, CA, SEQ]), ("kcT", [P, CA, CTX]),
                                    ("v_sb", [P, NT, D_NA]), ("vc_sb", [P, CT, D_NA])):
                    keep[name] = sb(heads, name, shape)
                projection(nc, io, keep)
                attention(nc, io, keep)
            output(nc, io, keep)
        with ExitStack() as chosen:
            keep["route"] = sb(chosen, "route", [P, 3, NT, PH * TOPK])
            routing(nc, io, keep)
            gates(nc, io, keep)
        experts(nc, io, keep)


def lay_out(a):
    import numpy as np

    def cols(v):
        return np.ascontiguousarray(v).reshape(-1, P).T

    arrays = {}
    arrays["x"] = a["x"][0]
    arrays["ctx"] = a["ctx"][0]
    cond = np.stack([cols(a["c"][0]), cols(a["c_ctx"])], axis=-1).reshape(P, 2 * KD)
    taps = a["conv_w"][0].reshape(TAPS, CC, P).transpose(2, 1, 0).reshape(P, CC * TAPS)
    arrays["vec"] = np.concatenate(
        [cols(a["b_ada"][0]), cols(a["g_pre_mix"][0]), cols(a["g_post_mix"][0]), cols(a["g_pre_ffn"][0]),
         cols(a["g_post_ffn"][0]), cols(a["conv_b"][0]), cols(a["conv_norm_g"][0]), cols(a["conv_norm_b"][0]), taps,
         cond], axis=1)
    arrays["w_ada"] = a["w_ada"][0]
    w_in = a["w_in"][0]
    nt = 2 * CC + 2 * CA
    arrays["w_in_t"] = w_in[:, :nt * P].reshape(KD, P, nt, P).transpose(2, 1, 0, 3)
    arrays["w_v"] = w_in[:, nt * P:]
    arrays["w_out"] = a["w_out"][0]
    wide = np.pad(a["na_rpb"][0], ((0, 0), (0, 0), (GRID_W - WIN_C, GRID_W - WIN_C)))
    arrays["rpb_t"] = np.stack([wide[:, :, GRID_W - 1 - q:2 * GRID_W - 1 - q] for q in range(GRID_W)], axis=1)
    q = np.arange(GRID_W)[:, None]
    k = np.arange(GRID_W)[None, :]
    first = np.clip(q - WIN_C // 2, 0, GRID_W - WIN_C)
    window = np.where((k >= first) & (k < first + WIN_C), 0.0, NEG).astype(np.float32)
    mask = np.tile(window[:, None, :], (2, BIAS_R, 1))
    mask[:GRID_W, T_ROWS + IN_ROWS - 1] = NEG
    mask[GRID_W:, T_ROWS] = NEG
    arrays["mask"] = mask.reshape(P, BIAS_R * GRID_W)
    arrays["ident"] = np.eye(P, dtype=np.float32)
    arrays["iota"] = np.tile(np.arange(PK, dtype=np.float32), (P, 1))
    arrays["wq_t"] = a["peer_wq"][0].reshape(KD, P, SUB, P).transpose(2, 1, 0, 3)
    arrays["keys_t"] = a["peer_keys"][0].reshape(SUB, PK, P).transpose(0, 2, 1)
    arrays["u_t"] = a["peer_u"][0].reshape(PK, PK, KD, P).transpose(0, 3, 2, 1).reshape(PK, P, D)
    arrays["v"] = a["peer_v"][0].reshape(PK, PK, D)
    return {name: np.ascontiguousarray(v) for name, v in arrays.items()}


def kernel(**inputs):
    import numpy as _np
    import concourse.bacc as _bacc
    from concourse import mybir as _mybir
    from concourse.bass_utils import run_bass_kernel_spmd as _run

    nc = _bacc.Bacc("TRN2", target_bir_lowering=False, num_devices=1)
    arrays = {f"in_{k}": v for k, v in lay_out({k: _np.asarray(v) for k, v in inputs.items()}).items()}
    io = {}
    for name, a in arrays.items():
        io[name[3:]] = nc.dram_tensor(name, a.shape, _mybir.dt.from_np(a.dtype), kind="ExternalInput").ap()
    io["out"] = nc.dram_tensor("out", (SEQ, D), F32, kind="ExternalOutput").ap()
    io["x2"] = nc.dram_tensor("x2", (SEQ, D), F32).ap()
    io["gates"] = nc.dram_tensor("gate_tables", (SEQ // SLOT, PK, PK, SLOT), F32).ap()
    build(nc, io)
    r = _run(nc, [arrays], core_ids=[0])
    return r.results[0]["out"].reshape(1, SEQ, D)
```

```python
from contextlib import ExitStack

import concourse.bass as bass
from concourse import mybir

F32 = mybir.dt.float32
BF16 = mybir.dt.bfloat16
U32 = mybir.dt.uint32
I32 = mybir.dt.int32
ALU = mybir.AluOpType
ACT = mybir.ActivationFunctionType
AX_X = mybir.AxisListType.X

P = 128
D = 1024
KD = D // P
SEQ = 1024
NT = SEQ // P
CTX = 256
CT = CTX // P
HALF = 512
NH = SEQ // HALF
N_MOD = 6
MODT = N_MOD * KD
D_CONV = 512
CC = D_CONV // P
TAPS = 31
PAD = TAPS // 2
HEADS = 8
HD = 64
D_NA = HEADS * HD
CA = D_NA // P
GRID_W = 64
ROWS = SEQ // GRID_W
WIN_R = 8
WIN_C = 16
PAIRS = ROWS // 2
EDGE_ROWS = [7, 5, 3, 1]
T_ROWS = 14
IN_ROWS = 9
BIAS_R = T_ROWS + IN_ROWS
EPS = 1e-6
NEG = -1e30
PH = 8
PK = 128
TOPK = 16
SUB = 2 * PH
EXPERTS = PK * PK
GROUP = 4
GROUPS = PK // GROUP

V_BADA = 0
V_GPRE1 = V_BADA + MODT
V_GPOST1 = V_GPRE1 + KD
V_GPRE2 = V_GPOST1 + KD
V_GPOST2 = V_GPRE2 + KD
V_CONVB = V_GPOST2 + KD
V_CNG = V_CONVB + CC
V_CNB = V_CNG + CC
V_CONVW = V_CNB + CC
V_COND = V_CONVW + CC * TAPS
V_END = V_COND + 2 * KD


PARTS = [(0, 0), (0, 1), (1, 0)]


class Count:

    def __init__(self, sem):
        self.sem, self.n = sem, 0

    def up(self, instruction):
        self.n += 1
        instruction.then_inc(self.sem, 1)
        return self.n

    def then_wait(self, engine, instruction):
        engine.wait_ge(self.sem, self.up(instruction))


def modulation(nc, io, keep):
    with ExitStack() as ctx:
        def sb(name, shape, dt=F32):
            return ctx.enter_context(nc.sbuf_tensor(f"modulation_{name}", shape, dt))

        def sem(name):
            return ctx.enter_context(nc.semaphore(f"modulation_{name}"))

        CH = 4
        NCH = MODT // CH
        RING = 3
        TT = NT + CT
        x_sb = sb("x_sb", [P, TT, D])
        w_sb = sb("w_ada_sb", [P, RING, KD, CH * P])
        silu_c = sb("silu_c", [P, KD, 2])
        square = sb("square", [P, 2, D])
        ssq = sb("ssq", [P, TT])
        std = sb("std", [P, TT])
        rstd = sb("rstd", [P, TT])
        gs1 = sb("gs1", [P, KD])
        cgs1 = sb("cgs1", [P, KD])
        cmod = sb("cmod", [P, 2 * KD])
        gate_col = sb("gate_col", [P, 2 * KD])
        diag = sb("diag", [P, 2 * KD, P])
        ones = sb("ones", [P, P])
        TEMPS = 4
        temp = sb("temp", [P, TEMPS, HALF])
        mod1_ps = ctx.enter_context(nc.psum_tensor("mod1_ps", [P, HALF], F32))
        mod2_ps = ctx.enter_context(nc.psum_tensor("mod2_ps", [P, HALF], F32))
        tr_ps = [ctx.enter_context(nc.psum_tensor(f"tr_ps{i}", [P, HALF], F32)) for i in range(4)]
        row_ps = [ctx.enter_context(nc.psum_tensor(f"row_ps{i}", [P, HALF], F32)) for i in range(2)]

        vec_in = sem("vec_in")
        x_in = [sem(f"x_in{t}") for t in range(TT)]
        w_in = [sem(f"w_ada_in{i}") for i in range(RING)]
        silu_done = sem("silu_done")
        ssq_done = sem("ssq_done")
        std_done = sem("std_done")
        xn_done = sem("xn_done")
        mod1_mm = sem("mod1_mm")
        chunk_used = sem("chunk_used")
        mod_done = sem("mod_done")
        dve = sem("dve")
        tr_done = sem("tr_done")
        modulated = sem("modulated")
        hi_done = sem("hi_done")
        lo_done = sem("lo_done")
        diag_done = sem("diag_done")
        row_mm = sem("row_mm")
        ones_set = sem("ones_set")
        row_out = sem("row_out")

        vec, ident, hp, hcp, mod, gs2, rows1, rows2 = (
            keep[n] for n in ("vec", "ident", "hp", "hcp", "mod", "gs2", "rows1", "rows2"))
        mod_src = io["w_ada"].rearrange("(k p) c -> p k c", p=P)
        turns = [("x", 4 * q, 4, k) for q in range(NT // 4) for k in range(KD)] + [("c", NT, CT, k) for k in range(KD)]

        def parts(n):
            which, t0, nt, k = turns[n]
            return (hp[:, k, :, t0 * P:(t0 + nt) * P] if which == "x" else hcp[:, k, :, :]), nt * P

        block = ctx.enter_context(nc.Block())

        @block.sync
        def _(sp):
            sp.dma_start(vec[:], io["vec"]).then_inc(vec_in, 16)
            sp.dma_start(ident[:], io["ident"]).then_inc(vec_in, 16)
            for n in range(NCH):
                if n >= RING:
                    sp.wait_ge(chunk_used, n - RING + 1)
                sp.dma_start(w_sb[:, n % RING], mod_src[:, :, n * CH * P:(n + 1) * CH * P]).then_inc(w_in[n % RING], 16)

        @block.scalar
        def _(act):
            for t in range(TT):
                src = io["x"][t * P:(t + 1) * P, :] if t < NT else io["ctx"][(t - NT) * P:(t - NT + 1) * P, :]
                act.dma_start(x_sb[:, t, :], src).then_inc(x_in[t], 16)
            act.wait_ge(vec_in, 32)
            nc.scalar.activation(silu_c[:].rearrange("p k c -> p (k c)"), vec[:, V_COND:V_END],
                                 ACT.Silu).then_inc(silu_done, 1)
            for t in range(TT):
                act.wait_ge(x_in[t], 16)
                if t >= 2:
                    act.wait_ge(ssq_done, t - 1)
                nc.scalar.activation(square[:, t % 2, :], x_sb[:, t, :], ACT.Square,
                                     accum_out=ssq[:, t:t + 1]).then_inc(ssq_done, 1)
            act.wait_ge(dve, 1)
            nc.scalar.activation(std[:], std[:], ACT.Sqrt).then_inc(std_done, 1)
            act.wait_ge(mod_done, 1)
            for n, (which, t0, nt, k) in enumerate(turns):
                act.wait_ge(tr_done, n + 1)
                if n >= TEMPS:
                    act.wait_ge(lo_done, n - TEMPS + 1)
                g, sh = (gs1, mod) if which == "x" else (cgs1, cmod)
                nc.scalar.activation(temp[:, n % TEMPS, 0:nt * P], tr_ps[n % 4][:, 0:nt * P], ACT.Identity,
                                     bias=sh[:, k:k + 1], scale=g[:, k:k + 1]).then_inc(modulated, 1)

        @block.gpsimd
        def _(pool):
            nc.gpsimd.memset(keep["eps"][:], EPS)
            nc.gpsimd.memset(ones[:], 1.0).then_inc(ones_set, 1)
            for n in range(len(turns)):
                dst, width = parts(n)
                pool.wait_ge(hi_done, n + 1)
                nc.gpsimd.tensor_tensor(dst[:, 1], temp[:, n % TEMPS, 0:width], dst[:, 0],
                                        ALU.subtract).then_inc(lo_done, 1)

        @block.tensor
        def _(pe):
            pe.wait_ge(silu_done, 1)

            def turn(n):
                which, t0, nt, k = turns[n]
                if n % 4 == 0:
                    pe.wait_ge(xn_done, t0 + nt)
                if n >= 4:
                    pe.wait_ge(modulated, n - 3)
                for j in range(nt):
                    last = nc.tensor.transpose(tr_ps[n % 4][:, j * P:(j + 1) * P], x_sb[:, t0 + j, k * P:(k + 1) * P],
                                               ident[:])
                last.then_inc(tr_done, 1)

            for n in range(NCH):
                pe.wait_ge(w_in[n % RING], 16 * (n // RING + 1))
                for c in range(CH):
                    m = n * CH + c
                    out = mod1_ps[:, 2 * m:2 * m + 2] if m < 2 * KD else mod2_ps[:, 2 * m:2 * m + 2]
                    for k in range(KD):
                        last = nc.tensor.matmul(out, w_sb[:, n % RING, k, c * P:(c + 1) * P], silu_c[:, k, :],
                                                start=(k == 0), stop=(k == KD - 1))
                last.then_inc(chunk_used, 1)
                if n >= 3:
                    for i in range(3 * (n - 3), min(3 * (n - 2), len(turns))):
                        turn(i)
            assert 3 * (NCH - 3) >= len(turns)
            pe.wait_ge(ones_set, 1)
            for g in range(4):
                pe.wait_ge(diag_done, 4 * g + 4)
                if g >= 2:
                    pe.wait_ge(row_out, g - 1)
                for j in range(4):
                    last = nc.tensor.matmul(row_ps[g % 2][:, j * P:(j + 1) * P], ones[:], diag[:, 4 * g + j, :],
                                            start=True, stop=True)
                last.then_inc(row_mm, 1)

        @block.vector
        def _(v):
            c = Count(dve)
            v.wait_ge(ssq_done, TT)
            c.up(nc.vector.tensor_scalar(std[:], ssq[:], 1.0 / D, EPS, ALU.mult, ALU.add))
            v.wait_ge(std_done, 1)
            c.then_wait(v, nc.vector.reciprocal(rstd[:], std[:]))
            for t in range(TT):
                nc.vector.tensor_scalar(x_sb[:, t, :], x_sb[:, t, :], rstd[:, t:t + 1], None,
                                        ALU.mult).then_inc(xn_done, 1)
            v.wait_ge(chunk_used, 2 * KD // CH)
            both = mod1_ps[:, 0:4 * KD].rearrange("p (m c) -> p m c", c=2)
            nc.vector.tensor_tensor(mod[:, 0:2 * KD], both[:, :, 0], vec[:, V_BADA:V_BADA + 2 * KD], ALU.add)
            c.then_wait(v, nc.vector.tensor_tensor(cmod[:], both[:, :, 1], vec[:, V_BADA:V_BADA + 2 * KD], ALU.add))
            g1 = vec[:, V_GPRE1:V_GPRE1 + KD]
            nc.vector.scalar_tensor_tensor(gs1[:], mod[:, KD:2 * KD], 1.0, g1, ALU.add, ALU.mult)
            nc.vector.scalar_tensor_tensor(cgs1[:], cmod[:, KD:2 * KD], 1.0, g1, ALU.add, ALU.mult).then_inc(mod_done, 1)
            v.wait_ge(mod_done, 1)
            for n in range(len(turns)):
                dst, width = parts(n)
                v.wait_ge(modulated, n + 1)
                nc.vector.tensor_copy(dst[:, 0], temp[:, n % TEMPS, 0:width]).then_inc(hi_done, 1)
            v.wait_ge(chunk_used, NCH)
            c.then_wait(v, nc.vector.tensor_tensor(
                mod[:, 2 * KD:], mod2_ps[:, 4 * KD:2 * MODT].rearrange("p (m c) -> p m c", c=2)[:, :, 0],
                vec[:, V_BADA + 2 * KD:V_BADA + MODT], ALU.add))
            nc.vector.scalar_tensor_tensor(gs2[:], mod[:, 4 * KD:5 * KD], 1.0, vec[:, V_GPRE2:V_GPRE2 + KD],
                                           ALU.add, ALU.mult)
            nc.vector.tensor_tensor(gate_col[:, 0:KD], mod[:, 2 * KD:3 * KD], vec[:, V_GPOST1:V_GPOST1 + KD], ALU.mult)
            c.then_wait(v, nc.vector.tensor_tensor(gate_col[:, KD:], mod[:, 5 * KD:6 * KD],
                                                   vec[:, V_GPOST2:V_GPOST2 + KD], ALU.mult))
            for k in range(2 * KD):
                nc.vector.tensor_scalar(diag[:, k, :], ident[:], gate_col[:, k:k + 1], None,
                                        ALU.mult).then_inc(diag_done, 1)
            for g in range(4):
                v.wait_ge(row_mm, g + 1)
                nc.vector.tensor_copy((rows1 if g < NH else rows2)[:, g % NH, :], row_ps[g % 2][:]).then_inc(row_out, 1)


def projection(nc, io, keep):
    with ExitStack() as ctx:
        def sb(name, shape, dt=F32):
            return ctx.enter_context(nc.sbuf_tensor(f"projection_{name}", shape, dt))

        def sem(name):
            return ctx.enter_context(nc.semaphore(f"projection_{name}"))

        vec, hp, hcp, conv, q_p, k_p, kc_p, v_p, vc_p = (
            keep[n] for n in ("vec", "hp", "hcp", "conv", "q_p", "k_p", "kc_p", "v_p", "vc_p"))
        RAWS = 2
        RING = 3
        w_raw = sb("w_raw", [P, RAWS, D])
        w_part = sb("w_part", [P, RING, 2, D], BF16)
        wv_part = sb("wv_part", [P, KD, 2, D_NA], BF16)
        TEMPS = 4
        temp = sb("temp", [P, TEMPS, HALF])
        glu = sb("glu", [P, 2, SEQ + 2 * PAD])
        odd = sb("odd", [P, SEQ])
        sig = sb("sig", [P, 2, SEQ])
        square = sig[:].rearrange("p a (b n) -> p (a b) n", n=HALF)
        mean_w = sb("mean_w", [P, P])
        rstd_row = sb("rstd_row", [P, SEQ])
        conv_p = conv[:].bitcast(BF16).rearrange("p c (s n) -> p c s n", s=2)
        BANKS = 8
        bank = [ctx.enter_context(nc.psum_tensor(f"proj_ps{i}", [P, HALF], F32)) for i in range(BANKS)]

        w_in = [sem(f"w_in{i}") for i in range(RAWS)]
        w_hi = sem("w_hi")
        w_lo = sem("w_lo")
        piece_mm = sem("piece_mm")
        act_read = sem("act_read")
        dve_read = sem("dve_read")
        lo_done = sem("lo_done")
        dve = sem("dve")
        glu_zero = sem("glu_zero")
        conv_done = sem("conv_done")
        sq_done = sem("sq_done")
        normed = sem("normed")
        swished = sem("swished")
        mean_set = sem("mean_set")

        order = [t for c in range(CC) for t in (CC + c, c)] + list(range(2 * CC, 2 * CC + 2 * CA))
        NW = len(order)
        NV = KD // 2
        kind_of = lambda t: "value" if t < CC else "gate" if t < 2 * CC else "q" if t < 2 * CC + CA else "k"
        pieces = []
        for t in order:
            pieces += [(kind_of(t), t % CC, h) for h in range(NH)]
            if kind_of(t) == "k":
                pieces.append(("kc", t % CC, 0))
        pieces += [("v", t, 0) for t in range(NT)] + [("vc", t, 0) for t in range(CT)]
        pieces += [("mean", 0, h) for h in range(NH)] + [("var", 0, h) for h in range(NH)]
        number = {p: n for n, p in enumerate(pieces)}
        by_dve = [p for p in pieces if p[0] in ("value", "mean")]
        by_act = [p for p in pieces if p not in by_dve]
        split = [p for p in pieces if p[0] in ("q", "k", "kc", "v", "vc")]

        def place(p):
            kind, i, h = p
            cols = slice(h * HALF, (h + 1) * HALF)
            return {"q": lambda: q_p[:, i, :, cols], "k": lambda: k_p[:, i, :, cols], "kc": lambda: kc_p[:, i],
                    "v": lambda: v_p[:, i], "vc": lambda: vc_p[:, i]}[kind]()

        def last_piece(t):
            return number[("kc", t % CC, 0) if kind_of(t) == "k" else (kind_of(t), t % CC, NH - 1)]

        def wait_read(eng, p):
            if p in by_dve:
                eng.wait_ge(dve_read, by_dve.index(p) + 1)
            else:
                eng.wait_ge(act_read, by_act.index(p) + 1)

        def weights(i):
            if i < NW:
                return w_part[:, i % RING]
            j = i - NW
            return wv_part[:, 2 * j:2 * j + 2].rearrange("p k s n -> p s k n")

        def raw(i):
            return w_raw[:, i % RAWS] if i < NW else w_raw[:, i % RAWS].rearrange("p (k n) -> p k n", k=2)

        block = ctx.enter_context(nc.Block())

        @block.sync
        def _(sp):
            for i in range(NW + NV):
                if i >= RAWS:
                    sp.wait_ge(w_lo, i - RAWS + 1)
                if i < NW:
                    src = io["w_in_t"][order[i]]
                else:
                    j = i - NW
                    src = io["w_v"][2 * j * P:(2 * j + 2) * P, :].rearrange("(k p) c -> p k c", p=P)
                sp.dma_start(raw(i), src).then_inc(w_in[i % RAWS], 16)

        @block.tensor
        def _(pe):
            def make(n, terms, width=HALF):
                if n >= BANKS:
                    wait_read(pe, pieces[n - BANKS])
                for i, (w, m) in enumerate(terms):
                    last = nc.tensor.matmul(bank[n % BANKS][:, 0:width], w, m, start=(i == 0), stop=(i == len(terms) - 1))
                last.then_inc(piece_mm, 1)

            for i, t in enumerate(order):
                pe.wait_ge(w_lo, i + 1)
                w = w_part[:, i % RING]
                for h in range(NH):
                    make(number[(kind_of(t), t % CC, h)],
                         [(w[:, a, k * P:(k + 1) * P], hp[:, k, b, h * HALF:(h + 1) * HALF])
                          for a, b in PARTS for k in range(KD)])
                if kind_of(t) == "k":
                    make(number[("kc", t % CC, 0)],
                         [(w[:, a, k * P:(k + 1) * P], hcp[:, k, b, :]) for a, b in PARTS for k in range(KD)], CTX)
            pe.wait_ge(w_lo, NW + NV)
            for t in range(NT):
                make(number[("v", t, 0)], [(hp[:, k, a, t * P:(t + 1) * P], wv_part[:, k, b, :])
                                           for a, b in PARTS for k in range(KD)])
            for t in range(CT):
                make(number[("vc", t, 0)], [(hcp[:, k, a, t * P:(t + 1) * P], wv_part[:, k, b, :])
                                            for a, b in PARTS for k in range(KD)])
            pe.wait_ge(mean_set, 1)
            pe.wait_ge(conv_done, CC)
            for h in range(NH):
                make(number[("mean", 0, h)], [(mean_w[:], conv[:, c, h * HALF:(h + 1) * HALF]) for c in range(CC)])
            for h in range(NH):
                pe.wait_ge(sq_done, CC * (h + 1))
                make(number[("var", 0, h)], [(mean_w[:], square[:, c, :]) for c in range(CC)])

        @block.scalar
        def _(act):
            def take(i):
                act.wait_ge(w_in[i % RAWS], 16 * (i // RAWS + 1))
                if RING <= i < NW:
                    act.wait_ge(piece_mm, last_piece(order[i - RING]) + 1)
                nc.scalar.copy(weights(i)[:, 0], raw(i)).then_inc(w_hi, 1)

            taken = 0
            for n, (kind, i, h) in enumerate(pieces):
                while taken < NW + NV and (taken < 2 or (taken < NW and last_piece(order[taken - 2]) <= n + 1) or
                                           (taken >= NW and n >= last_piece(order[NW - 4]))):
                    take(taken)
                    taken += 1
                cols = slice(h * HALF, (h + 1) * HALF)
                src = bank[n % BANKS][:]
                if (kind, i, h) in by_dve:
                    continue
                if kind == "var":
                    for c in range(CC):
                        act.wait_ge(dve_read, by_dve.index(("mean", 0, h)) + 1)
                        if h > 0:
                            act.wait_ge(piece_mm, number[("var", 0, h - 1)] + 1)
                        nc.scalar.activation(square[:, c, :], conv[:, c, cols], ACT.Square).then_inc(sq_done, 1)
                act.wait_ge(piece_mm, n + 1)
                if kind == "gate":
                    if i >= 2:
                        act.wait_ge(dve_read, by_dve.index(("value", i - 2, NH - 1)) + 1)
                    nc.scalar.activation(sig[:, i % 2, cols], src, ACT.Sigmoid).then_inc(act_read, 1)
                elif kind == "var":
                    nc.scalar.activation(rstd_row[:, cols], src, ACT.Sqrt, bias=keep["eps"][:, 0:1]).then_inc(act_read, 1)
                else:
                    m = split.index((kind, i, h))
                    width = CTX if kind == "kc" else HALF
                    scale = HD ** -0.5 if kind == "q" else 1.0
                    if m >= TEMPS:
                        act.wait_ge(lo_done, m - TEMPS + 1)
                    nc.scalar.activation(temp[:, m % TEMPS, 0:width], src[:, 0:width], ACT.Copy, scale=scale)
                    nc.scalar.activation(place((kind, i, h))[:, 0], src[:, 0:width], ACT.Copy,
                                         scale=scale).then_inc(act_read, 1)
            for c in range(CC):
                act.wait_ge(normed, c + 1)
                if c >= 2:
                    act.wait_ge(lo_done, len(split) + c - 1)
                nc.scalar.activation(sig[:, c % 2, :], conv[:, c, :], ACT.Silu, bias=vec[:, V_CNB + c:V_CNB + c + 1],
                                     scale=vec[:, V_CNG + c:V_CNG + c + 1]).then_inc(swished, 1)

        @block.gpsimd
        def _(pool):
            nc.gpsimd.memset(mean_w[:], 1.0 / D_CONV).then_inc(mean_set, 1)
            nc.gpsimd.memset(glu[:, :, 0:PAD], 0.0)
            nc.gpsimd.memset(glu[:, :, PAD + SEQ:], 0.0).then_inc(glu_zero, 1)

            def take(i):
                pool.wait_ge(w_hi, i + 1)
                nc.gpsimd.tensor_tensor(weights(i)[:, 1], raw(i), weights(i)[:, 0], ALU.subtract).then_inc(w_lo, 1)

            taken = 0
            for n, p in enumerate(pieces):
                while taken < NW + NV and (taken < 2 or (taken < NW and last_piece(order[taken - 2]) <= n + 1) or
                                           (taken >= NW and n >= last_piece(order[NW - 4]))):
                    take(taken)
                    taken += 1
                if p in split:
                    m = split.index(p)
                    width = CTX if p[0] == "kc" else HALF
                    pool.wait_ge(act_read, by_act.index(p) + 1)
                    nc.gpsimd.tensor_tensor(place(p)[:, 1], temp[:, m % TEMPS, 0:width], place(p)[:, 0],
                                            ALU.subtract).then_inc(lo_done, 1)
            for c in range(CC):
                pool.wait_ge(dve_read, len(by_dve) + c + 1)
                nc.gpsimd.tensor_tensor(conv_p[:, c, 1], sig[:, c % 2, :], conv_p[:, c, 0],
                                        ALU.subtract).then_inc(lo_done, 1)

        @block.vector
        def _(v):
            ch = Count(dve)
            v.wait_ge(glu_zero, 1)

            def gated(c):
                for h in range(NH):
                    v.wait_ge(piece_mm, number[("value", c, h)] + 1)
                    v.wait_ge(act_read, by_act.index(("gate", c, h)) + 1)
                    cols = slice(h * HALF, (h + 1) * HALF)
                    nc.vector.tensor_tensor(glu[:, c % 2, PAD + h * HALF:PAD + (h + 1) * HALF],
                                            bank[number[("value", c, h)] % BANKS][:], sig[:, c % 2, cols],
                                            ALU.mult).then_inc(dve_read, 1)

            def depthwise(c):
                v.wait_ge(dve_read, by_dve.index(("value", c, NH - 1)) + 1)
                made = []
                for tap in range(TAPS):
                    w = vec[:, V_CONVW + c * TAPS + tap:V_CONVW + c * TAPS + tap + 1]
                    src = glu[:, c % 2, tap:tap + SEQ]
                    acc = conv[:, c, :] if tap % 2 == 0 else odd[:]
                    if tap >= 2:
                        v.wait_ge(dve, made[tap - 2])
                    if tap == 1 and c >= 1:
                        v.wait_ge(conv_done, c)
                    if tap == 0:
                        ins = nc.vector.tensor_scalar(acc, src, w, vec[:, V_CONVB + c:V_CONVB + c + 1], ALU.mult, ALU.add)
                    elif tap == 1:
                        ins = nc.vector.tensor_scalar(acc, src, w, None, ALU.mult)
                    else:
                        ins = nc.vector.scalar_tensor_tensor(acc, src, w, acc, ALU.mult, ALU.add)
                    made.append(ch.up(ins))
                v.wait_ge(dve, made[-1])
                nc.vector.tensor_tensor(conv[:, c, :], conv[:, c, :], odd[:], ALU.add).then_inc(conv_done, 1)

            gated(0)
            gated(1)
            for c in range(CC):
                depthwise(c)
                if c + 2 < CC:
                    gated(c + 2)
            v.wait_ge(conv_done, CC)
            for h in range(NH):
                n = number[("mean", 0, h)]
                v.wait_ge(piece_mm, n + 1)
                for c in range(CC):
                    cols = slice(h * HALF, (h + 1) * HALF)
                    ins = nc.vector.tensor_tensor(conv[:, c, cols], conv[:, c, cols], bank[n % BANKS][:], ALU.subtract)
                ins.then_inc(dve_read, 1)
            v.wait_ge(act_read, len(by_act))
            ch.then_wait(v, nc.vector.reciprocal(rstd_row[:], rstd_row[:]))
            for c in range(CC):
                nc.vector.tensor_tensor(conv[:, c, :], conv[:, c, :], rstd_row[:], ALU.mult).then_inc(normed, 1)
            for c in range(CC):
                v.wait_ge(swished, c + 1)
                nc.vector.tensor_copy(conv_p[:, c, 0], sig[:, c % 2, :]).then_inc(dve_read, 1)


def attention(nc, io, keep):
    with ExitStack() as ctx:
        def sb(name, shape, dt=F32):
            return ctx.enter_context(nc.sbuf_tensor(f"attention_{name}", shape, dt))

        def sem(name):
            return ctx.enter_context(nc.semaphore(f"attention_{name}"))

        ident, q_p, k_p, kc_p, v_p, vc_p = (keep[n] for n in ("ident", "q_p", "k_p", "kc_p", "v_p", "vc_p"))
        att_p = q_p
        bias = sb("bias", [P, HEADS, BIAS_R * GRID_W])
        LAT = IN_ROWS * GRID_W
        KB = (LAT + P - 1) // P
        KEYS = LAT + CTX
        SLOTS = 4
        score = sb("score", [P, SLOTS, KEYS])
        prob_p = sb("prob_p", [P, 2, 2, (CT + KB) * P], BF16)
        mask = score[:].rearrange("p s k -> p (s k)")[:, 0:BIAS_R * GRID_W]
        zero = sb("zero", [P, 1])
        top = sb("top", [P, SLOTS, 2])
        neg_max = sb("neg_max", [P, SLOTS])
        sums = sb("sums", [P, SLOTS])
        rsum = sb("rsum", [P, SLOTS])
        heads_out = sb("heads_out", [P, 2, D_NA])
        temp = sb("temp", [P, HALF])
        s_ps = [ctx.enter_context(nc.psum_tensor(f"s_ps{i}", [P, 2 * HALF], F32)) for i in range(2)]
        pt_ps = ctx.enter_context(nc.psum_tensor("pt_ps", [P, 2 * HALF], F32))
        o_ps = ctx.enter_context(nc.psum_tensor("o_ps", [P, HALF], F32))
        ot_ps = ctx.enter_context(nc.psum_tensor("ot_ps", [P, HALF], F32))

        bias_in = [sem(f"bias_in{h}") for h in range(HEADS)]
        mask_in = sem("mask_in")
        zero_set = sem("zero_set")
        bias_done = sem("bias_done")
        scores_mm = sem("scores_mm")
        biased = sem("biased")
        neg_done = sem("neg_done")
        exp_done = sem("exp_done")
        prob_turned = sem("prob_turned")
        prob_hi = sem("prob_hi")
        prob_lo = sem("prob_lo")
        out_mm = sem("out_mm")
        out_done = sem("out_done")
        outT_mm = sem("outT_mm")
        outT_read = sem("outT_read")
        outT_done = sem("outT_done")
        dve = sem("dve")

        plan = []
        for j in range(PAIRS):
            lo = min(max(2 * j - WIN_R // 2, 0), ROWS - WIN_R)
            hi = min(max(2 * j + 1 - WIN_R // 2, 0), ROWS - WIN_R)
            if lo == hi:
                plan.append((lo, WIN_R, EDGE_ROWS[j if j < 2 else j - PAIRS + 4] - 1))
            else:
                plan.append((lo, IN_ROWS, T_ROWS))
            assert lo % 2 == 0
        units = [(j, h) for j in range(PAIRS) for h in range(HEADS)]

        block = ctx.enter_context(nc.Block())

        @block.sync
        def _(sp):
            sp.dma_start(mask, io["mask"]).then_inc(mask_in, 16)
            for h in range(HEADS):
                src = io["rpb_t"][h]
                edge, inner = T_ROWS * GRID_W, IN_ROWS * GRID_W
                sp.dma_start(bias[0:GRID_W, h, 0:edge], src[:, 1:1 + T_ROWS, :].rearrange("q r c -> q (r c)")).then_inc(bias_in[h], 16)
                sp.dma_start(bias[GRID_W:P, h, 0:edge], src[:, 0:T_ROWS, :].rearrange("q r c -> q (r c)")).then_inc(bias_in[h], 16)
                sp.dma_start(bias[0:GRID_W, h, edge:edge + inner], src[:, 3:3 + IN_ROWS, :].rearrange("q r c -> q (r c)")).then_inc(bias_in[h], 16)
                sp.dma_start(bias[GRID_W:P, h, edge:edge + inner], src[:, 2:2 + IN_ROWS, :].rearrange("q r c -> q (r c)")).then_inc(bias_in[h], 16)

        def key_blocks(u):
            j, h = units[u]
            r0, nr, _ = plan[j]
            cols = slice(h * HD, (h + 1) * HD)
            out = [(b * P, P, vc_p[:, b, :, cols]) for b in range(CT)]
            for b in range((nr * GRID_W + P - 1) // P):
                n = min(P, nr * GRID_W - b * P)
                out.append((CTX + b * P, n, v_p[0:n, r0 * GRID_W // P + b, :, cols]))
            return out

        def spans(u):
            nk = CTX + plan[units[u][0]][1] * GRID_W
            full = nk // P * P
            return [(P, slice(0, full))] + ([(nk - full, slice(full, full + P))] if nk > full else [])

        LAG = 2

        @block.tensor
        def _(pe):
            def scores(u):
                j, h = units[u]
                r0, nr, _ = plan[j]
                if u >= 2:
                    pe.wait_ge(biased, u - 1)
                part = slice(HD * (h % 2), HD * (h % 2) + HD)
                g = h // 2
                k0, nk = r0 * GRID_W, nr * GRID_W
                for dst, src in ((slice(0, CTX), lambda b: kc_p[part, g, b, :]),
                                 (slice(CTX, HALF), lambda b: k_p[part, g, b, k0:k0 + HALF - CTX]),
                                 (slice(HALF, CTX + nk), lambda b: k_p[part, g, b, k0 + HALF - CTX:k0 + nk])):
                    for i, (a, b) in enumerate(PARTS):
                        last = nc.tensor.matmul(s_ps[u % 2][:, dst], q_p[part, g, a, j * P:(j + 1) * P], src(b),
                                                start=(i == 0), stop=(i == len(PARTS) - 1))
                last.then_inc(scores_mm, 1)

            def turn(u):
                pe.wait_ge(exp_done, u + 1)
                if u >= 1:
                    pe.wait_ge(prob_lo, u)
                for b, (c, n, _) in enumerate(key_blocks(u)):
                    last = nc.tensor.transpose(pt_ps[0:n, b * P:(b + 1) * P], score[:, u % SLOTS, c:c + n], ident[:])
                last.then_inc(prob_turned, 1)

            def outputs(u):
                pe.wait_ge(prob_lo, u + 1)
                if u >= 1:
                    pe.wait_ge(out_done, u)
                terms = [(b, n, vals, x, y) for b, (c, n, vals) in enumerate(key_blocks(u)) for x, y in PARTS]
                for i, (b, n, vals, x, y) in enumerate(terms):
                    last = nc.tensor.matmul(o_ps[:, 0:HD], prob_p[0:n, u % 2, x, b * P:(b + 1) * P], vals[:, y],
                                            start=(i == 0), stop=(i == len(terms) - 1))
                last.then_inc(out_mm, 1)

            def turned(j):
                pe.wait_ge(out_done, HEADS * (j + 1))
                if j >= 1:
                    pe.wait_ge(outT_read, j)
                for c in range(CA):
                    last = nc.tensor.transpose(ot_ps[:, c * P:(c + 1) * P], heads_out[:, j % 2, c * P:(c + 1) * P], ident[:])
                last.then_inc(outT_mm, 1)

            for u in range(len(units) + LAG + 1):
                if u < len(units):
                    scores(u)
                if LAG <= u < len(units) + LAG:
                    turn(u - LAG)
                if u >= LAG + 1:
                    w = u - LAG - 1
                    outputs(w)
                    if w % HEADS == 0 and w > 0:
                        turned(w // HEADS - 1)
            turned(PAIRS - 1)

        @block.scalar
        def _(act):
            def probs(u):
                nk = CTX + plan[units[u][0]][1] * GRID_W
                s = u % SLOTS
                act.wait_ge(neg_done, u + 1)
                if u >= SLOTS:
                    act.wait_ge(out_done, u - SLOTS + 1)
                nc.scalar.activation(score[:, s, 0:nk], score[:, s, 0:nk], ACT.Exp, bias=neg_max[:, s:s + 1],
                                     accum_out=sums[:, s:s + 1]).then_inc(exp_done, 1)

            def round_probs(u):
                act.wait_ge(prob_turned, u + 1)
                if u >= 2:
                    act.wait_ge(out_mm, u - 1)
                for n, cols in spans(u):
                    ins = nc.scalar.copy(prob_p[0:n, u % 2, 0, cols], pt_ps[0:n, cols])
                ins.then_inc(prob_hi, 1)

            for u in range(len(units) + LAG):
                if u >= LAG:
                    round_probs(u - LAG)
                if u < len(units):
                    probs(u)

        @block.gpsimd
        def _(pool):
            for j in range(PAIRS):
                pool.wait_ge(outT_read, j + 1)
                cols = slice(j * P, (j + 1) * P)
                nc.gpsimd.tensor_tensor(att_p[:, :, 1, cols], temp[:].rearrange("p (c n) -> p c n", c=CA),
                                        att_p[:, :, 0, cols], ALU.subtract).then_inc(outT_done, 1)

        @block.vector
        def _(v):
            ch = Count(dve)
            nc.vector.memset(zero[:], 0.0).then_inc(zero_set, 1)
            v.wait_ge(mask_in, 16)
            for h in range(HEADS):
                v.wait_ge(bias_in[h], 64)
                nc.vector.tensor_tensor(bias[:, h, :], bias[:, h, :], mask, ALU.add).then_inc(bias_done, 1)
            v.wait_ge(bias_done, HEADS)
            v.wait_ge(zero_set, 1)

            def biased_scores(u):
                j, h = units[u]
                _, nr, t0 = plan[j]
                nk = nr * GRID_W
                s = u % SLOTS
                v.wait_ge(scores_mm, u + 1)
                if u >= SLOTS:
                    v.wait_ge(prob_turned, u - SLOTS + 1)
                nc.vector.tensor_tensor_reduce(score[:, s, 0:CTX], s_ps[u % 2][:, 0:CTX],
                                               zero[:].to_broadcast([P, CTX]), 1.0, NEG, ALU.add, ALU.max,
                                               top[:, s, 0:1])
                nc.vector.tensor_tensor_reduce(score[:, s, CTX:CTX + nk], s_ps[u % 2][:, CTX:CTX + nk],
                                               bias[:, h, t0 * GRID_W:t0 * GRID_W + nk], 1.0, NEG,
                                               ALU.add, ALU.max, top[:, s, 1:2]).then_inc(biased, 1)

            def maximum(u):
                s = u % SLOTS
                v.wait_ge(biased, u + 1)
                nc.vector.tensor_reduce(neg_max[:, s:s + 1], top[:, s, :], AX_X, ALU.max,
                                        negate=True).then_inc(neg_done, 1)

            def split_probs(u):
                v.wait_ge(prob_hi, u + 1)
                for n, cols in spans(u):
                    ins = nc.vector.tensor_tensor(prob_p[0:n, u % 2, 1, cols], pt_ps[0:n, cols],
                                                  prob_p[0:n, u % 2, 0, cols], ALU.subtract)
                ins.then_inc(prob_lo, 1)

            def invert(u):
                v.wait_ge(exp_done, u + 1)
                ch.up(nc.vector.reciprocal(rsum[:, u % SLOTS:u % SLOTS + 1], sums[:, u % SLOTS:u % SLOTS + 1]))

            def normalise(u):
                j, h = units[u]
                v.wait_ge(dve, u + 1)
                v.wait_ge(out_mm, u + 1)
                if h == 0 and j >= 2:
                    v.wait_ge(outT_mm, j - 1)
                nc.vector.tensor_scalar(heads_out[:, j % 2, h * HD:(h + 1) * HD], o_ps[:, 0:HD],
                                        rsum[:, u % SLOTS:u % SLOTS + 1], None, ALU.mult).then_inc(out_done, 1)

            def place(j):
                v.wait_ge(outT_mm, j + 1)
                if j >= 1:
                    v.wait_ge(outT_done, j)
                nc.vector.tensor_copy(temp[:], ot_ps[:])
                nc.vector.tensor_copy(att_p[:, :, 0, j * P:(j + 1) * P],
                                      ot_ps[:].rearrange("p (c n) -> p c n", c=CA)).then_inc(outT_read, 1)

            for u in range(len(units) + LAG + 1):
                if u < len(units):
                    biased_scores(u)
                if LAG <= u < len(units) + LAG:
                    split_probs(u - LAG)
                    invert(u - LAG)
                if u < len(units):
                    maximum(u)
                if u >= LAG + 1:
                    w = u - LAG - 1
                    if w % HEADS == 1 and w > HEADS:
                        place(w // HEADS - 1)
                    normalise(w)
            place(PAIRS - 1)


def output(nc, io, keep):
    with ExitStack() as ctx:
        def sb(name, shape, dt=F32):
            return ctx.enter_context(nc.sbuf_tensor(f"output_{name}", shape, dt))

        def sem(name):
            return ctx.enter_context(nc.semaphore(f"output_{name}"))

        ident, conv, att_p, hp, mod, gs2, rows1 = (
            keep[n] for n in ("ident", "conv", "q_p", "hp", "mod", "gs2", "rows1"))
        conv_p = conv[:].bitcast(BF16).rearrange("p c (s n) -> p c s n", s=2)
        w_raw = sb("w_raw", [P, 2, D])
        w_part = sb("w_part", [P, KD, 2, D], BF16)
        temp = sb("temp", [P, 2, KD, P])
        x_sb = sb("x_res", [P, NT, D])
        square = sb("square", [P, 2, D])
        work = sb("work", [P, 2, D])
        ssq = sb("ssq", [P, 2, NT])
        std = sb("std", [P, 2, NT])
        rstd = sb("rstd", [P, 2, NT])
        y_ps = [ctx.enter_context(nc.psum_tensor(f"y_ps{i}", [P, D], F32)) for i in range(2)]
        t_ps = [ctx.enter_context(nc.psum_tensor(f"t_ps{i}", [P, D], F32)) for i in range(2)]

        w_in = [sem(f"w_in{i}") for i in range(2)]
        w_hi = sem("w_hi")
        w_lo = sem("w_lo")
        h_hi = sem("h_hi")
        h_lo = sem("h_lo")
        x_in = [sem(f"x_res_in{t}") for t in range(NT)]
        y_mm = sem("y_mm")
        y_ssq = sem("y_ssq")
        y_ms = sem("y_ms")
        y_std = sem("y_std")
        x2_done = sem("x2_done")
        x2_out = sem("x2_out")
        x2_ssq = sem("x2_ssq")
        x2_ms = sem("x2_ms")
        x2_std = sem("x2_std")
        normed = sem("normed")
        t_mm = sem("t_mm")
        t_act = sem("t_act")
        t_dve = sem("t_dve")
        dve = sem("dve")

        block = ctx.enter_context(nc.Block())

        @block.sync
        def _(sp):
            for k in range(KD):
                if k >= 2:
                    sp.wait_ge(w_lo, k - 1)
                sp.dma_start(w_raw[:, k % 2, :], io["w_out"][k * P:(k + 1) * P, :]).then_inc(w_in[k % 2], 16)
            for t in range(NT):
                sp.dma_start(x_sb[:, t, :], io["x"][t * P:(t + 1) * P, :]).then_inc(x_in[t], 16)
            for t in range(NT):
                sp.wait_ge(x2_done, t + 1)
                sp.dma_start(io["x2"][t * P:(t + 1) * P, :], x_sb[:, t, :]).then_inc(x2_out, 16)
            sp.wait_ge(x2_out, 16 * NT)

        @block.tensor
        def _(pe):
            def product(t):
                if t >= 2:
                    pe.wait_ge(x2_done, t - 1)
                for k in range(KD):
                    if t == 0:
                        pe.wait_ge(w_lo, k + 1)
                    mix = conv_p[:, k] if k < CC else att_p[:, k - CC]
                    for h in range(NH):
                        for i, (a, b) in enumerate(PARTS):
                            last = nc.tensor.matmul(y_ps[t % 2][:, h * HALF:(h + 1) * HALF], mix[:, a, t * P:(t + 1) * P],
                                                    w_part[:, k, b, h * HALF:(h + 1) * HALF], start=(k == 0 and i == 0),
                                                    stop=(k == KD - 1 and i == len(PARTS) - 1))
                last.then_inc(y_mm, 1)

            def turn(t):
                pe.wait_ge(normed, t + 1)
                if t >= 2:
                    pe.wait_ge(t_act, t - 1)
                    pe.wait_ge(t_dve, t - 1)
                for k in range(KD):
                    last = nc.tensor.transpose(t_ps[t % 2][:, k * P:(k + 1) * P], work[:, t % 2, k * P:(k + 1) * P], ident[:])
                last.then_inc(t_mm, 1)

            for t in range(NT + 1):
                if t < NT:
                    product(t)
                if t >= 1:
                    turn(t - 1)

        @block.scalar
        def _(act):
            for k in range(KD):
                act.wait_ge(w_in[k % 2], 16 * (k // 2 + 1))
                nc.scalar.copy(w_part[:, k, 0, :], w_raw[:, k % 2, :]).then_inc(w_hi, 1)
            for t in range(NT):
                act.wait_ge(y_mm, t + 1)
                nc.scalar.activation(square[:, 0, :], y_ps[t % 2][:], ACT.Square,
                                     accum_out=ssq[:, 0, t:t + 1]).then_inc(y_ssq, 1)
                act.wait_ge(y_ms, t + 1)
                nc.scalar.activation(std[:, 0, t:t + 1], std[:, 0, t:t + 1], ACT.Sqrt).then_inc(y_std, 1)
                act.wait_ge(x2_done, t + 1)
                nc.scalar.activation(square[:, 1, :], x_sb[:, t, :], ACT.Square,
                                     accum_out=ssq[:, 1, t:t + 1]).then_inc(x2_ssq, 1)
                act.wait_ge(x2_ms, t + 1)
                nc.scalar.activation(std[:, 1, t:t + 1], std[:, 1, t:t + 1], ACT.Sqrt).then_inc(x2_std, 1)
                act.wait_ge(t_mm, t + 1)
                if t >= 2:
                    act.wait_ge(h_lo, t - 1)
                for k in range(KD // 2):
                    ins = nc.scalar.activation(temp[:, t % 2, k, :], t_ps[t % 2][:, k * P:(k + 1) * P],
                                               ACT.Identity, bias=mod[:, 3 * KD + k:3 * KD + k + 1], scale=gs2[:, k:k + 1])
                ins.then_inc(t_act, 1)

        @block.gpsimd
        def _(pool):
            for k in range(KD):
                pool.wait_ge(w_hi, k + 1)
                nc.gpsimd.tensor_tensor(w_part[:, k, 1, :], w_raw[:, k % 2, :], w_part[:, k, 0, :],
                                        ALU.subtract).then_inc(w_lo, 1)
            for t in range(NT):
                pool.wait_ge(h_hi, t + 1)
                nc.gpsimd.tensor_tensor(hp[:, :, 1, t * P:(t + 1) * P], temp[:, t % 2], hp[:, :, 0, t * P:(t + 1) * P],
                                        ALU.subtract).then_inc(h_lo, 1)

        @block.vector
        def _(v):
            ch = Count(dve)
            for t in range(NT):
                y = y_ps[t % 2]
                v.wait_ge(y_ssq, t + 1)
                nc.vector.tensor_scalar(std[:, 0, t:t + 1], ssq[:, 0, t:t + 1], 1.0 / D, EPS, ALU.mult,
                                        ALU.add).then_inc(y_ms, 1)
                v.wait_ge(y_std, t + 1)
                ch.then_wait(v, nc.vector.reciprocal(rstd[:, 0, t:t + 1], std[:, 0, t:t + 1]))
                if t >= 2:
                    v.wait_ge(t_mm, t - 1)
                ch.then_wait(v, nc.vector.scalar_tensor_tensor(work[:, t % 2, :], y[:], rstd[:, 0, t:t + 1],
                                                               rows1[:].rearrange("p a b -> p (a b)"),
                                                               ALU.mult, ALU.mult))
                v.wait_ge(x_in[t], 16)
                nc.vector.tensor_tensor(x_sb[:, t, :], x_sb[:, t, :], work[:, t % 2, :], ALU.add).then_inc(x2_done, 1)
                v.wait_ge(x2_ssq, t + 1)
                nc.vector.tensor_scalar(std[:, 1, t:t + 1], ssq[:, 1, t:t + 1], 1.0 / D, EPS, ALU.mult,
                                        ALU.add).then_inc(x2_ms, 1)
                v.wait_ge(x2_std, t + 1)
                ch.then_wait(v, nc.vector.reciprocal(rstd[:, 1, t:t + 1], std[:, 1, t:t + 1]))
                nc.vector.tensor_scalar(work[:, t % 2, :], x_sb[:, t, :], rstd[:, 1, t:t + 1], None,
                                        ALU.mult).then_inc(normed, 1)
                v.wait_ge(t_mm, t + 1)
                if t >= 2:
                    v.wait_ge(h_lo, t - 1)
                for k in range(KD // 2, KD):
                    ins = nc.vector.tensor_scalar(temp[:, t % 2, k, :], t_ps[t % 2][:, k * P:(k + 1) * P],
                                                  gs2[:, k:k + 1], mod[:, 3 * KD + k:3 * KD + k + 1], ALU.mult, ALU.add)
                ins.then_inc(t_dve, 1)
                v.wait_ge(t_dve, t + 1)
                v.wait_ge(t_act, t + 1)
                nc.vector.tensor_copy(hp[:, :, 0, t * P:(t + 1) * P], temp[:, t % 2]).then_inc(h_hi, 1)


A_ROWS = 4
B_COLS = 4
CAND_A = A_ROWS * TOPK
CAND = CAND_A + (TOPK - A_ROWS) * B_COLS
LOWEST = -3.0e38
ROUTE_STEPS = 143


def routing(nc, io, keep):
    with ExitStack() as ctx:
        def sb(name, shape, dt=F32):
            return ctx.enter_context(nc.sbuf_tensor(f"routing_{name}", shape, dt))

        def sem(name):
            return ctx.enter_context(nc.semaphore(f"routing_{name}"))

        hp, route = keep["hp"], keep["route"]
        wq_raw = sb("wq_raw", [P, 2, D])
        wq_part = sb("wq_part", [P, 2, 2, D], BF16)
        key_sb = sb("key_sb", [P, 2, PK])
        iota16 = sb("iota16", [P, TOPK])
        qh = sb("qh", [P, 2, SEQ])
        sc = sb("sc", [P, 2, NT, PK])
        rest = sb("rest", [P, 2, NT, PK])
        best = sb("best", [P, 2, NT, TOPK])
        at = sb("at", [P, 2, NT, TOPK], U32)
        atf = sb("atf", [P, 2, NT, TOPK])
        cand = sb("cand", [P, NT, CAND])
        cand_rest = sb("cand_rest", [P, NT, CAND])
        top = sb("top", [P, NT, TOPK])
        pos = sb("pos", [P, NT, TOPK], U32)
        shr = sb("shr", [P, 2, NT, TOPK], U32)
        low = sb("low", [P, 2, NT, TOPK], U32)
        late = sb("late", [P, NT, TOPK])
        diff = sb("diff", [P, 2, NT, TOPK])
        rank = sb("rank", [P, 2, NT, TOPK])
        hot = sb("hot", [P, 2, NT * TOPK, TOPK])
        gate = sb("gate", [P, NT, TOPK])
        gsum = sb("gsum", [P, NT])
        q_ps = [ctx.enter_context(nc.psum_tensor(f"q_ps{i}", [P, NH * HALF], F32)) for i in range(2)]
        s_ps = [ctx.enter_context(nc.psum_tensor(f"sc_ps{i}", [P, NT, PK], F32)) for i in range(2)]

        w_in = [sem(f"wq_in{i}") for i in range(2)]
        key_in = [sem(f"key_in{i}") for i in range(2)]
        iota_in = sem("iota_in")
        wq_hi = sem("wq_hi")
        wq_lo = sem("wq_lo")
        q_mm = sem("q_mm")
        q_out = sem("q_out")
        s_mm = sem("s_mm")
        s_out = sem("s_out")
        found = sem("found")
        shifted = sem("shifted")
        exp_done = sem("gate_exp")
        dve = sem("dve")

        block = ctx.enter_context(nc.Block())

        @block.sync
        def _(sp):
            sp.dma_start(iota16[:], io["iota"][:, 0:TOPK]).then_inc(iota_in, 16)
            for s in range(2):
                sp.dma_start(wq_raw[:, s], io["wq_t"][s]).then_inc(w_in[s], 16)
                sp.dma_start(key_sb[:, s], io["keys_t"][s]).then_inc(key_in[s], 16)
            with sp.Fori(1, PH) as h:
                for s in range(2):
                    sp.wait_ge(wq_lo, 2 * h + s - 1)
                    sp.dma_start(wq_raw[:, s], io["wq_t"][2 * h + s]).then_inc(w_in[s], 16)
                    sp.wait_ge(s_mm, 2 * h + s + 1)
                    sp.dma_start(key_sb[:, s], io["keys_t"][2 * h + s]).then_inc(key_in[s], 16)

        @block.tensor
        def _(pe):
            pe.sem_inc(q_out, 2)
            pe.sem_inc(s_out, 2)
            pe.sem_inc(s_mm, 2)
            pe.sem_inc(q_mm, 2)
            with pe.Fori(0, PH) as h:
                for s in range(2):
                    pe.wait_ge(wq_lo, 2 * h + s + 1)
                    pe.wait_ge(q_out, 2 * h + s + 1)
                    for half in range(NH):
                        terms = [(a, b, k) for a, b in PARTS for k in range(KD)]
                        for i, (a, b, k) in enumerate(terms):
                            last = nc.tensor.matmul(q_ps[s][:, half * HALF:(half + 1) * HALF],
                                                    wq_part[:, s, a, k * P:(k + 1) * P],
                                                    hp[:, k, b, half * HALF:(half + 1) * HALF], start=(i == 0),
                                                    stop=(i == len(terms) - 1))
                    last.then_inc(q_mm, 1)
                for s in range(2):
                    pe.wait_ge(q_out, 2 * h + s + 3)
                    pe.wait_ge(key_in[s], 16 * h + 16)
                    pe.wait_ge(s_out, 2 * h + s + 1)
                    for t in range(NT):
                        last = nc.tensor.matmul(s_ps[s][:, t, :], qh[:, s, t * P:(t + 1) * P], key_sb[:, s, :],
                                                start=True, stop=True)
                    last.then_inc(s_mm, 1)

        @block.scalar
        def _(act):
            with act.Fori(0, PH) as h:
                for s in range(2):
                    act.wait_ge(w_in[s], 16 * h + 16)
                    act.wait_ge(q_mm, 2 * h + s + 1)
                    nc.scalar.copy(wq_part[:, s, 0, :], wq_raw[:, s]).then_inc(wq_hi, 1)
                for s in range(2):
                    act.wait_ge(q_mm, 2 * h + s + 3)
                    act.wait_ge(s_mm, 2 * h + s + 1)
                    nc.scalar.copy(qh[:, s, :], q_ps[s][:]).then_inc(q_out, 1)
                for s in range(2):
                    act.wait_ge(s_mm, 2 * h + s + 3)
                    act.wait_ge(found, 2 * h + s + 1)
                    nc.scalar.copy(sc[:, s], s_ps[s][:]).then_inc(s_out, 1)
                act.wait_ge(shifted, h + 1)
                nc.scalar.activation(gate[:], gate[:], ACT.Exp).then_inc(exp_done, 1)

        @block.gpsimd
        def _(pool):
            with pool.Fori(0, PH) as h:
                for s in range(2):
                    pool.wait_ge(wq_hi, 2 * h + s + 1)
                    nc.gpsimd.tensor_tensor(wq_part[:, s, 1, :], wq_raw[:, s], wq_part[:, s, 0, :],
                                            ALU.subtract).then_inc(wq_lo, 1)

        @block.vector
        def _(v):
            v.wait_ge(iota_in, 16)
            v.sem_inc(found, 2)
            with v.Fori(0, PH) as h:
                c = Count(dve)

                def ready():
                    v.wait_ge(dve, ROUTE_STEPS * h + c.n)
                    v.nop(nofuse=True)

                for s in range(2):
                    v.wait_ge(s_out, 2 * h + s + 3)
                    v.nop(nofuse=True)
                    for t in range(NT):
                        c.up(nc.vector.max(best[:, s, t, 0:8], sc[:, s, t, :]))
                    ready()
                    for t in range(NT):
                        c.up(nc.vector.match_replace(rest[:, s, t, :], best[:, s, t, 0:8], sc[:, s, t, :], LOWEST))
                    for t in range(NT):
                        c.up(nc.vector.max_index(at[:, s, t, 0:8], best[:, s, t, 0:8], sc[:, s, t, :]))
                    ready()
                    v.sem_inc(found, 1)
                    for t in range(NT):
                        c.up(nc.vector.max(best[:, s, t, 8:16], rest[:, s, t, :]))
                    ready()
                    for t in range(NT):
                        c.up(nc.vector.max_index(at[:, s, t, 8:16], best[:, s, t, 8:16], rest[:, s, t, :]))
                ready()
                c.up(nc.vector.tensor_copy(atf[:], at[:]))
                a, b = best[:, 0], best[:, 1]
                c.up(nc.vector.tensor_tensor(
                    cand[:, :, 0:CAND_A].rearrange("p t (a b) -> p t a b", b=TOPK),
                    a[:, :, 0:A_ROWS].unsqueeze(3).to_broadcast([P, NT, A_ROWS, TOPK]),
                    b.unsqueeze(2).to_broadcast([P, NT, A_ROWS, TOPK]), ALU.add))
                c.up(nc.vector.tensor_tensor(
                    cand[:, :, CAND_A:].rearrange("p t (a b) -> p t a b", b=B_COLS),
                    a[:, :, A_ROWS:].unsqueeze(3).to_broadcast([P, NT, TOPK - A_ROWS, B_COLS]),
                    b[:, :, 0:B_COLS].unsqueeze(2).to_broadcast([P, NT, TOPK - A_ROWS, B_COLS]), ALU.add))
                ready()
                for t in range(NT):
                    c.up(nc.vector.max(top[:, t, 0:8], cand[:, t, :]))
                ready()
                for t in range(NT):
                    c.up(nc.vector.match_replace(cand_rest[:, t, :], top[:, t, 0:8], cand[:, t, :], LOWEST))
                for t in range(NT):
                    c.up(nc.vector.max_index(pos[:, t, 0:8], top[:, t, 0:8], cand[:, t, :]))
                ready()
                for t in range(NT):
                    c.up(nc.vector.max(top[:, t, 8:16], cand_rest[:, t, :]))
                ready()
                nc.vector.tensor_tensor(gate[:], top[:], top[:, :, 0:1].to_broadcast([P, NT, TOPK]),
                                        ALU.subtract).then_inc(shifted, 1)
                for t in range(NT):
                    c.up(nc.vector.max_index(pos[:, t, 8:16], top[:, t, 8:16], cand_rest[:, t, :]))
                ready()
                c.up(nc.vector.tensor_scalar(shr[:, 0], pos[:], 4, None, ALU.logical_shift_right))
                c.up(nc.vector.tensor_scalar(shr[:, 1], pos[:], 2, None, ALU.logical_shift_right))
                c.up(nc.vector.tensor_scalar(low[:, 0], pos[:], TOPK - 1, None, ALU.bitwise_and))
                c.up(nc.vector.tensor_scalar(low[:, 1], pos[:], B_COLS - 1, None, ALU.bitwise_and))
                c.up(nc.vector.tensor_scalar(late[:], pos[:], float(CAND_A), None, ALU.is_ge))
                ready()
                c.up(nc.vector.scalar_tensor_tensor(diff[:, 0], shr[:, 1], float(CAND_A // B_COLS - A_ROWS), shr[:, 0],
                                                    ALU.subtract, ALU.subtract))
                c.up(nc.vector.tensor_tensor(diff[:, 1], low[:, 1], low[:, 0], ALU.subtract))
                ready()
                for s in range(2):
                    c.up(nc.vector.tensor_tensor(diff[:, s], diff[:, s], late[:], ALU.mult))
                ready()
                c.up(nc.vector.tensor_tensor(rank[:, 0], diff[:, 0], shr[:, 0], ALU.add))
                c.up(nc.vector.tensor_tensor(rank[:, 1], diff[:, 1], low[:, 0], ALU.add))
                ready()
                flat = [P, NT * TOPK, TOPK]
                for s in range(2):
                    c.up(nc.vector.tensor_tensor(
                        hot[:, s], rank[:, s].rearrange("p t k -> p (t k)").unsqueeze(2).to_broadcast(flat),
                        iota16[:].unsqueeze(1).to_broadcast(flat), ALU.is_equal))
                ready()
                for s in range(2):
                    hs = hot[:, s].rearrange("p (t k) m -> p t k m", k=TOPK)
                    c.up(nc.vector.tensor_tensor(hs, hs, atf[:, s].unsqueeze(2).to_broadcast([P, NT, TOPK, TOPK]),
                                                 ALU.mult))
                ready()
                for s in range(2):
                    c.up(nc.vector.tensor_reduce(route[:, s, :, bass.ts(h, TOPK)],
                                                 hot[:, s].rearrange("p (t k) m -> p t k m", k=TOPK), AX_X, ALU.add))
                v.wait_ge(exp_done, h + 1)
                c.up(nc.vector.tensor_reduce(gsum[:], gate[:], AX_X, ALU.add))
                ready()
                c.up(nc.vector.reciprocal(gsum[:], gsum[:]))
                ready()
                c.up(nc.vector.tensor_tensor(route[:, 2, :, bass.ts(h, TOPK)], gate[:],
                                             gsum[:].unsqueeze(2).to_broadcast([P, NT, TOPK]), ALU.mult))
                ready()
                assert c.n == ROUTE_STEPS, c.n


SLOT = 64
PERG = HALF // PK
HOTS = 8


def gates(nc, io, keep):
    with ExitStack() as ctx:
        def sb(name, shape, dt=F32):
            return ctx.enter_context(nc.sbuf_tensor(f"gates_{name}", shape, dt))

        def sem(name):
            return ctx.enter_context(nc.semaphore(f"gates_{name}"))

        ident, route = keep["ident"], keep["route"]
        iota = sb("iota_sb", [P, PK])
        routeT = sb("routeT", [P, 3, SEQ])
        row_hot = sb("row_hot", [P, HOTS, PK])
        col_hot = sb("col_hot", [P, HOTS, PK])
        table = sb("table", [P, 2, PK, SLOT])
        t_ps = [ctx.enter_context(nc.psum_tensor(f"rt_ps{i}", [P, 4, P], F32)) for i in range(2)]
        g_ps = [ctx.enter_context(nc.psum_tensor(f"g_ps{i}", [P, PERG, PK], F32)) for i in range(4)]

        iota_in = sem("iota_in")
        turned = sem("turned")
        routeT_done = sem("routeT_done")
        hot_done = sem("hot_done")
        g_mm = sem("g_mm")
        g_out = sem("g_out")
        table_out = [sem(f"table_out{i}") for i in range(2)]

        ITER = 2 * SLOT
        TURNS = SEQ // ITER
        jobs = [(c, q) for c in range(3) for q in range(NT // 4)]

        block = ctx.enter_context(nc.Block())

        @block.sync
        def _(sp):
            sp.dma_start(iota[:], io["iota"]).then_inc(iota_in, 16)
            for s in range(2):
                sp.sem_inc(table_out[s], 16)
            with sp.Fori(0, TURNS) as i:
                for s in range(2):
                    sp.wait_ge(g_out, (2 * i + s + 1) * (SLOT // PERG) + 4)
                    sp.dma_start(io["gates"][2 * i + s], table[:, s]).then_inc(table_out[s], 16)
            for s in range(2):
                sp.wait_ge(table_out[s], 16 * (TURNS + 1))

        @block.tensor
        def _(pe):
            for n, (c, q) in enumerate(jobs):
                if n >= 2:
                    pe.wait_ge(routeT_done, n - 1)
                for j in range(4):
                    last = nc.tensor.transpose(t_ps[n % 2][:, j, :], route[:, c, 4 * q + j, :], ident[:])
                last.then_inc(turned, 1)
            pe.sem_inc(g_out, 4)
            pe.sem_inc(g_mm, HOTS // PERG)
            with pe.Fori(0, TURNS) as i:
                for b in range(ITER // PERG):
                    pe.wait_ge(g_out, i * (ITER // PERG) + b + 1)
                    for j in range(PERG):
                        n = b * PERG + j
                        pe.wait_ge(hot_done, 2 * (i * ITER + n) + 2)
                        last = nc.tensor.matmul(g_ps[b % 4][:, j, :], col_hot[:, n % HOTS, :], row_hot[:, n % HOTS, :],
                                                start=True, stop=True)
                    last.then_inc(g_mm, 1)

        @block.scalar
        def _(act):
            with act.Fori(0, TURNS) as i:
                for b in range(ITER // PERG):
                    s, n = divmod(b * PERG, SLOT)
                    if n == 0:
                        act.wait_ge(table_out[s], 16 * i + 16)
                    act.wait_ge(g_mm, i * (ITER // PERG) + b + 1 + HOTS // PERG)
                    nc.scalar.copy(table[:, s, :, n:n + PERG].rearrange("p i n -> p n i"),
                                   g_ps[b % 4][:]).then_inc(g_out, 1)

        @block.vector
        def _(v):
            for n, (c, q) in enumerate(jobs):
                v.wait_ge(turned, n + 1)
                nc.vector.tensor_copy(routeT[:, c, q * HALF:(q + 1) * HALF],
                                      t_ps[n % 2][:].rearrange("p a b -> p (a b)")).then_inc(routeT_done, 1)
            v.wait_ge(routeT_done, len(jobs))
            v.wait_ge(iota_in, 16)
            with v.Fori(0, TURNS) as i:
                for n in range(ITER):
                    tok = i * ITER + n
                    if n % PERG == 0:
                        v.wait_ge(g_mm, i * (ITER // PERG) + n // PERG + 1)
                    nc.vector.tensor_scalar(col_hot[:, n % HOTS, :], iota[:], routeT[:, 1, bass.ds(tok, 1)], None,
                                            ALU.is_equal).then_inc(hot_done, 1)
                    nc.vector.tensor_scalar(row_hot[:, n % HOTS, :], iota[:], routeT[:, 0, bass.ds(tok, 1)],
                                            routeT[:, 2, bass.ds(tok, 1)], ALU.is_equal, ALU.mult).then_inc(hot_done, 1)



def experts(nc, io, keep):
    with ExitStack() as ctx:
        def sb(name, shape, dt=F32):
            return ctx.enter_context(nc.sbuf_tensor(f"experts_{name}", shape, dt))

        def sem(name):
            return ctx.enter_context(nc.semaphore(f"experts_{name}"))

        hp, rows2 = keep["hp"], keep["rows2"]
        acc = sb("acc", [P, NT, NH, HALF])
        u_raw = sb("u_raw", [P, 2, D])
        v_raw = sb("v_raw", [P, D])
        u_part = sb("u_part", [P, GROUP, 2, D], BF16)
        v_part = sb("v_part", [P, 2, GROUP, 2, D], BF16)
        w_part = sb("w_part", [P, 2, GROUP, 2, SEQ], BF16)
        CHUNKS = SEQ // SLOT
        g_sb = sb("g_sb", [P, 2, CHUNKS, GROUP * SLOT])
        ACTS = 4
        act_sb = sb("act_sb", [P, ACTS, HALF])
        stat = sb("stat", [P, 3, NT])
        whole = acc[:].rearrange("p t h n -> p t (h n)")
        a_ps = [ctx.enter_context(nc.psum_tensor(f"a_ps{i}", [P, HALF], F32)) for i in range(4)]
        b_ps = [ctx.enter_context(nc.psum_tensor(f"b_ps{i}", [P, HALF], F32)) for i in range(4)]

        zero_done = sem("zero_done")
        u_in = [sem(f"u_in{i}") for i in range(2)]
        v_in = sem("v_in")
        g_in = [sem(f"g_in{i}") for i in range(2)]
        u_hi = sem("u_hi")
        u_lo = sem("u_lo")
        v_hi = sem("v_hi")
        v_lo = sem("v_lo")
        a_mm = sem("a_mm")
        gelu_done = sem("gelu_done")
        prod_done = sem("prod_done")
        w_hi = sem("w_hi")
        w_lo = sem("w_lo")
        b_mm = sem("b_mm")
        acc_done = sem("acc_done")
        f_ssq = sem("f_ssq")
        f_ms = sem("f_ms")
        f_std = sem("f_std")
        f_rstd = sem("f_rstd")
        f_norm = sem("f_norm")
        f_done = sem("f_done")
        out_done = sem("out_done")

        UA = 2 * GROUP
        UB = NH * NT

        def schedule(eng, a, b):
            a(0, 0)
            a(1, 1)
            b(0, 0)
            with eng.Fori(0, (GROUPS - 4) // 2) as it:
                for s in range(2):
                    a(2 * it + s + 2, s)
                    b(2 * it + s + 1, 1 - s)
            for g in range(GROUPS - 3, GROUPS - 1):
                a(g + 1, (g + 1) % 2)
                b(g, g % 2)
            b(GROUPS - 1, 1)

        def within(g, n):
            return isinstance(g, int) and g >= GROUPS - n

        def wait(eng, semaphore, value):
            if not isinstance(value, int) or value > 0:
                eng.wait_ge(semaphore, value)

        block = ctx.enter_context(nc.Block())

        @block.sync
        def _(sp):
            def load_g(g, s):
                wait(sp, w_lo, UA * (g - 1))
                sp.dma_start(g_sb[:, s], io["gates"][:, :, bass.ts(g, GROUP), :].rearrange("c j i n -> j c (i n)"))\
                  .then_inc(g_in[s], 16)

            def load_u(g, i):
                wait(sp, u_lo, GROUP * g + i - 1)
                sp.dma_start(u_raw[:, i % 2], io["u_t"][GROUP * g + i]).then_inc(u_in[i % 2], 16)

            def load_v(g):
                for i in range(GROUP):
                    wait(sp, v_lo, GROUP * g + i)
                    sp.dma_start(v_raw[:], io["v"][GROUP * g + i]).then_inc(v_in, 16)

            def a(g, s):
                if isinstance(g, int) and g == 0:
                    load_u(0, 0)
                    load_g(0, 0)
                for i in range(1, GROUP):
                    load_u(g, i)
                if isinstance(g, int) and g == 0:
                    load_u(1, 0)
                    load_g(1, 1)
                    load_v(0)

            def b(g, s):
                if not within(g, 2):
                    load_g(g + 2, s)
                if not within(g, 1):
                    load_v(g + 1)
                if not within(g, 2):
                    load_u(g + 2, 0)

            schedule(sp, a, b)
            for t in range(NT):
                if t == 0:
                    sp.wait_ge(u_lo, PK)
                if t >= 2:
                    sp.wait_ge(f_done, t - 1)
                    sp.wait_ge(out_done, 16 * (t - 1))
                sp.dma_start(u_raw[:, t % 2], io["x2"][t * P:(t + 1) * P, :]).then_inc(u_in[t % 2], 16)
                if t >= 1:
                    sp.wait_ge(f_done, t)
                    sp.dma_start(io["out"][(t - 1) * P:t * P, :], u_raw[:, (t - 1) % 2]).then_inc(out_done, 16)
            sp.wait_ge(f_done, NT)
            sp.dma_start(io["out"][(NT - 1) * P:NT * P, :], u_raw[:, (NT - 1) % 2]).then_inc(out_done, 16)
            sp.wait_ge(out_done, 16 * NT)

        @block.tensor
        def _(pe):
            def a(g, s):
                for i in range(GROUP):
                    pe.wait_ge(u_lo, GROUP * g + i + 1)
                    for h in range(NH):
                        n = NH * i + h
                        wait(pe, gelu_done, UA * g + n - 3)
                        terms = [(wp, mp, k) for wp, mp in PARTS for k in range(KD)]
                        for m, (wp, mp, k) in enumerate(terms):
                            last = nc.tensor.matmul(a_ps[n % 4][:], u_part[:, i, wp, k * P:(k + 1) * P],
                                                    hp[:, k, mp, h * HALF:(h + 1) * HALF], start=(m == 0),
                                                    stop=(m == len(terms) - 1))
                        last.then_inc(a_mm, 1)

            def b(g, s):
                pe.wait_ge(w_lo, UA * g + UA)
                pe.wait_ge(v_lo, GROUP * g + GROUP)
                for t in range(NT):
                    for h in range(NH):
                        n = NH * t + h
                        wait(pe, acc_done, UB * g + n - 3)
                        terms = [(i, wp, vp) for i in range(GROUP) for wp, vp in PARTS]
                        for m, (i, wp, vp) in enumerate(terms):
                            last = nc.tensor.matmul(b_ps[n % 4][:], w_part[:, s, i, wp, t * P:(t + 1) * P],
                                                    v_part[:, s, i, vp, h * HALF:(h + 1) * HALF], start=(m == 0),
                                                    stop=(m == len(terms) - 1))
                        last.then_inc(b_mm, 1)

            schedule(pe, a, b)

        @block.scalar
        def _(act):
            def take_u(g, i):
                e = GROUP * g + i
                act.wait_ge(u_in[i % 2], 2 * 16 * g + 16 * (i // 2 + 1))
                wait(act, a_mm, NH * (e - GROUP) + NH)
                nc.scalar.copy(u_part[:, i, 0, :], u_raw[:, i % 2]).then_inc(u_hi, 1)

            def take_v(g, s):
                wait(act, b_mm, UB * (g - 1))
                for i in range(GROUP):
                    act.wait_ge(v_in, 16 * (GROUP * g + i + 1))
                    nc.scalar.copy(v_part[:, s, i, 0, :], v_raw[:]).then_inc(v_hi, 1)

            def round_w(g, s, n):
                act.wait_ge(prod_done, UA * g + n + 1)
                if n == 0:
                    wait(act, b_mm, UB * (g - 1))
                i, h = divmod(n, NH)
                nc.scalar.copy(w_part[:, s, i, 0, h * HALF:(h + 1) * HALF], act_sb[:, n % ACTS, :]).then_inc(w_hi, 1)

            def a(g, s):
                if isinstance(g, int) and g == 0:
                    take_u(0, 0)
                for i in range(GROUP):
                    for h in range(NH):
                        n = NH * i + h
                        if h == 0 and i + 1 < GROUP:
                            take_u(g, i + 1)
                        act.wait_ge(a_mm, UA * g + n + 1)
                        wait(act, w_lo, UA * g + n - ACTS + 1)
                        nc.scalar.activation(act_sb[:, n % ACTS, :], a_ps[n % 4][:],
                                             ACT.Gelu_apprx_tanh).then_inc(gelu_done, 1)
                        if n >= 1:
                            round_w(g, s, n - 1)
                round_w(g, s, UA - 1)
                if isinstance(g, int) and g == 0:
                    take_u(1, 0)
                    take_v(0, 0)

            def b(g, s):
                if not within(g, 1):
                    take_v(g + 1, 1 - s)
                if not within(g, 2):
                    take_u(g + 2, 0)

            schedule(act, a, b)
            act.wait_ge(acc_done, GROUPS * UB)
            for t in range(NT):
                if t >= 1:
                    act.wait_ge(f_ssq, t)
                nc.scalar.activation(g_sb[:, 0, 0:4, :].rearrange("p a b -> p (a b)"),
                                     whole[:, t, :], ACT.Square,
                                     accum_out=stat[:, 0, t:t + 1]).then_inc(f_ssq, 1)
            act.wait_ge(f_ms, 1)
            nc.scalar.activation(stat[:, 1, :], stat[:, 1, :], ACT.Sqrt).then_inc(f_std, 1)

        @block.gpsimd
        def _(pool):
            def take_u(g, i):
                pool.wait_ge(u_hi, GROUP * g + i + 1)
                nc.gpsimd.tensor_tensor(u_part[:, i, 1, :], u_raw[:, i % 2], u_part[:, i, 0, :],
                                        ALU.subtract).then_inc(u_lo, 1)

            def take_v(g, s):
                for i in range(GROUP):
                    pool.wait_ge(v_hi, GROUP * g + i + 1)
                    nc.gpsimd.tensor_tensor(v_part[:, s, i, 1, :], v_raw[:], v_part[:, s, i, 0, :],
                                            ALU.subtract).then_inc(v_lo, 1)

            def a(g, s):
                if isinstance(g, int) and g == 0:
                    take_u(0, 0)
                for i in range(1, GROUP):
                    take_u(g, i)
                if isinstance(g, int) and g == 0:
                    take_u(1, 0)
                    take_v(0, 0)

            def b(g, s):
                if not within(g, 1):
                    take_v(g + 1, 1 - s)
                if not within(g, 2):
                    take_u(g + 2, 0)

            schedule(pool, a, b)

        @block.vector
        def _(v):
            nc.vector.memset(acc[:], 0.0).then_inc(zero_done, 1)
            v.wait_ge(zero_done, 1)

            def low_w(g, s, n):
                i, h = divmod(n, NH)
                v.wait_ge(w_hi, UA * g + n + 1)
                nc.vector.tensor_tensor(w_part[:, s, i, 1, h * HALF:(h + 1) * HALF], act_sb[:, n % ACTS, :],
                                        w_part[:, s, i, 0, h * HALF:(h + 1) * HALF], ALU.subtract).then_inc(w_lo, 1)

            def a(g, s):
                for n in range(UA):
                    i, h = divmod(n, NH)
                    v.wait_ge(gelu_done, UA * g + n + 1)
                    if n == 0:
                        v.wait_ge(g_in[s], 8 * (g - s) + 16)
                    cs = slice(h * CHUNKS // NH, (h + 1) * CHUNKS // NH)
                    nc.vector.tensor_tensor(act_sb[:, n % ACTS, :].rearrange("p (c n) -> p c n", n=SLOT),
                                            act_sb[:, n % ACTS, :].rearrange("p (c n) -> p c n", n=SLOT),
                                            g_sb[:, s, cs, i * SLOT:(i + 1) * SLOT], ALU.mult).then_inc(prod_done, 1)
                    if n >= 1:
                        low_w(g, s, n - 1)
                low_w(g, s, UA - 1)

            def b(g, s):
                for n in range(UB):
                    t, h = divmod(n, NH)
                    v.wait_ge(b_mm, UB * g + n + 1)
                    wait(v, acc_done, UB * g + n - UB + 1)
                    nc.vector.tensor_tensor(acc[:, t, h, :], acc[:, t, h, :], b_ps[n % 4][:], ALU.add)\
                        .then_inc(acc_done, 1)

            schedule(v, a, b)
            v.wait_ge(f_ssq, NT)
            nc.vector.tensor_scalar(stat[:, 1, :], stat[:, 0, :], 1.0 / D, EPS, ALU.mult, ALU.add).then_inc(f_ms, 1)
            v.wait_ge(f_std, 1)
            nc.vector.reciprocal(stat[:, 2, :], stat[:, 1, :]).then_inc(f_rstd, 1)
            v.wait_ge(f_rstd, 1)
            for t in range(NT):
                f = whole[:, t, :]
                nc.vector.scalar_tensor_tensor(f, f, stat[:, 2, t:t + 1], rows2[:].rearrange("p a b -> p (a b)"),
                                               ALU.mult, ALU.mult).then_inc(f_norm, 1)
                v.wait_ge(f_norm, t + 1)
                v.wait_ge(u_in[t % 2], 16 * (PK // 2 + t // 2 + 1))
                nc.vector.tensor_tensor(u_raw[:, t % 2], u_raw[:, t % 2], f, ALU.add).then_inc(f_done, 1)

def build(nc, io):
    with ExitStack() as ctx:
        def sb(stack, name, shape, dt=F32):
            return stack.enter_context(nc.sbuf_tensor(name, shape, dt))

        keep = {
            "vec": sb(ctx, "vec_sb", [P, V_END]),
            "ident": sb(ctx, "ident_sb", [P, P]),
            "mod": sb(ctx, "mod", [P, MODT]),
            "gs2": sb(ctx, "gs2", [P, KD]),
            "eps": sb(ctx, "eps", [P, 1]),
            "rows2": sb(ctx, "rows2", [P, NH, HALF]),
            "hp": sb(ctx, "hp", [P, KD, 2, SEQ], BF16),
        }
        with ExitStack() as mix:
            keep["rows1"] = sb(mix, "rows1", [P, NH, HALF])
            keep["conv"] = sb(mix, "conv", [P, CC, SEQ])
            keep["q_p"] = sb(mix, "q_p", [P, CA, 2, SEQ], BF16)
            with ExitStack() as heads:
                keep["hcp"] = sb(heads, "hcp", [P, KD, 2, CTX], BF16)
                modulation(nc, io, keep)
                for name, shape in (("k_p", [P, CA, 2, SEQ]), ("kc_p", [P, CA, 2, CTX]),
                                    ("v_p", [P, NT, 2, D_NA]), ("vc_p", [P, CT, 2, D_NA])):
                    keep[name] = sb(heads, name, shape, BF16)
                projection(nc, io, keep)
                attention(nc, io, keep)
            output(nc, io, keep)
        with ExitStack() as chosen:
            keep["route"] = sb(chosen, "route", [P, 3, NT, PH * TOPK])
            routing(nc, io, keep)
            gates(nc, io, keep)
        experts(nc, io, keep)


def lay_out(a):
    import numpy as np

    def cols(v):
        return np.ascontiguousarray(v).reshape(-1, P).T

    arrays = {}
    arrays["x"] = a["x"][0]
    arrays["ctx"] = a["ctx"][0]
    cond = np.stack([cols(a["c"][0]), cols(a["c_ctx"])], axis=-1).reshape(P, 2 * KD)
    taps = a["conv_w"][0].reshape(TAPS, CC, P).transpose(2, 1, 0).reshape(P, CC * TAPS)
    arrays["vec"] = np.concatenate(
        [cols(a["b_ada"][0]), cols(a["g_pre_mix"][0]), cols(a["g_post_mix"][0]), cols(a["g_pre_ffn"][0]),
         cols(a["g_post_ffn"][0]), cols(a["conv_b"][0]), cols(a["conv_norm_g"][0]), cols(a["conv_norm_b"][0]), taps,
         cond], axis=1)
    arrays["w_ada"] = a["w_ada"][0]
    w_in = a["w_in"][0]
    nt = 2 * CC + 2 * CA
    arrays["w_in_t"] = w_in[:, :nt * P].reshape(KD, P, nt, P).transpose(2, 1, 0, 3)
    arrays["w_v"] = w_in[:, nt * P:]
    arrays["w_out"] = a["w_out"][0]
    wide = np.pad(a["na_rpb"][0], ((0, 0), (0, 0), (GRID_W - WIN_C, GRID_W - WIN_C)))
    arrays["rpb_t"] = np.stack([wide[:, :, GRID_W - 1 - q:2 * GRID_W - 1 - q] for q in range(GRID_W)], axis=1)
    q = np.arange(GRID_W)[:, None]
    k = np.arange(GRID_W)[None, :]
    first = np.clip(q - WIN_C // 2, 0, GRID_W - WIN_C)
    window = np.where((k >= first) & (k < first + WIN_C), 0.0, NEG).astype(np.float32)
    mask = np.tile(window[:, None, :], (2, BIAS_R, 1))
    mask[:GRID_W, T_ROWS + IN_ROWS - 1] = NEG
    mask[GRID_W:, T_ROWS] = NEG
    arrays["mask"] = mask.reshape(P, BIAS_R * GRID_W)
    arrays["ident"] = np.eye(P, dtype=np.float32)
    arrays["iota"] = np.tile(np.arange(PK, dtype=np.float32), (P, 1))
    arrays["wq_t"] = a["peer_wq"][0].reshape(KD, P, SUB, P).transpose(2, 1, 0, 3)
    arrays["keys_t"] = a["peer_keys"][0].reshape(SUB, PK, P).transpose(0, 2, 1)
    arrays["u_t"] = a["peer_u"][0].reshape(PK, PK, KD, P).transpose(0, 3, 2, 1).reshape(PK, P, D)
    arrays["v"] = a["peer_v"][0].reshape(PK, PK, D)
    return {name: np.ascontiguousarray(v) for name, v in arrays.items()}


def kernel(**inputs):
    import numpy as _np
    import concourse.bacc as _bacc
    from concourse import mybir as _mybir
    from concourse.bass_utils import run_bass_kernel_spmd as _run

    nc = _bacc.Bacc("TRN2", target_bir_lowering=False, num_devices=1)
    arrays = {f"in_{k}": v for k, v in lay_out({k: _np.asarray(v) for k, v in inputs.items()}).items()}
    io = {}
    for name, a in arrays.items():
        io[name[3:]] = nc.dram_tensor(name, a.shape, _mybir.dt.from_np(a.dtype), kind="ExternalInput").ap()
    io["out"] = nc.dram_tensor("out", (SEQ, D), F32, kind="ExternalOutput").ap()
    io["x2"] = nc.dram_tensor("x2", (SEQ, D), F32).ap()
    io["gates"] = nc.dram_tensor("gate_tables", (SEQ // SLOT, PK, PK, SLOT), F32).ap()
    build(nc, io)
    r = _run(nc, [arrays], core_ids=[0])
    return r.results[0]["out"].reshape(1, SEQ, D)
```

```python
from contextlib import ExitStack

import concourse.bass as bass
from concourse import mybir

F32 = mybir.dt.float32
BF16 = mybir.dt.bfloat16
U32 = mybir.dt.uint32
ALU = mybir.AluOpType
ACT = mybir.ActivationFunctionType
AX_X = mybir.AxisListType.X

P = 128
D = 1024
KD = D // P
SEQ = 1024
NT = SEQ // P
CTX = 256
CT = CTX // P
HALF = 512
NH = SEQ // HALF
N_MOD = 6
MODT = N_MOD * KD
D_CONV = 512
CC = D_CONV // P
TAPS = 31
PAD = TAPS // 2
HEADS = 8
HD = 64
D_NA = HEADS * HD
CA = D_NA // P
GRID_W = 64
ROWS = SEQ // GRID_W
WIN_R = 8
WIN_C = 16
PAIRS = ROWS // 2
EDGE_ROWS = [7, 5, 3, 1]
T_ROWS = 14
IN_ROWS = 9
BIAS_R = T_ROWS + IN_ROWS
EPS = 1e-6
NEG = -1e30
PH = 8
PK = 128
TOPK = 16
SUB = 2 * PH
GROUP = 4
GROUPS = PK // GROUP

V_BADA = 0
V_GPRE1 = V_BADA + MODT
V_GPOST1 = V_GPRE1 + KD
V_GPRE2 = V_GPOST1 + KD
V_GPOST2 = V_GPRE2 + KD
V_CONVB = V_GPOST2 + KD
V_CNG = V_CONVB + CC
V_CNB = V_CNG + CC
V_CONVW = V_CNB + CC
V_COND = V_CONVW + CC * TAPS
V_END = V_COND + 2 * KD


PARTS = [(0, 0), (0, 1), (1, 0)]


class Count:

    def __init__(self, sem):
        self.sem, self.n = sem, 0

    def up(self, instruction):
        self.n += 1
        instruction.then_inc(self.sem, 1)
        return self.n

    def then_wait(self, engine, instruction):
        engine.wait_ge(self.sem, self.up(instruction))


class Signals:

    def __init__(self, nc):
        self.nc, self.all = nc, []

    def __enter__(self):
        return self

    def new(self, name):
        self.all.append(self.nc.alloc_semaphore(name))
        return self.all[-1]

    def __exit__(self, *error):
        if error[0] is None:
            self.nc.clear_and_free_semaphores(self.all)
            self.nc.all_engine_barrier()


def modulation(nc, io, keep):
    with ExitStack() as ctx:
        signals = ctx.enter_context(Signals(nc))

        def sb(name, shape, dt=F32):
            return ctx.enter_context(nc.sbuf_tensor(f"modulation_{name}", shape, dt))

        def sem(name):
            return signals.new(f"modulation_{name}")

        CH = HALF // P
        NCH = MODT // CH
        TT = NT + CT
        x_sb = sb("x_sb", [P, TT, D])
        w_sb = [keep[n][:].rearrange("p a b -> p (a b)").rearrange("p (k c) -> p k c", k=KD) for n in ("conv", "q", "k")]
        RING = len(w_sb)
        silu_c = sb("silu_c", [P, KD, 2])
        square = sb("square", [P, 2, D])
        ssq = sb("ssq", [P, TT])
        std = sb("std", [P, TT])
        rstd = sb("rstd", [P, TT])
        gs1 = sb("gs1", [P, KD])
        cgs1 = sb("cgs1", [P, KD])
        cmod = sb("cmod", [P, 2 * KD])
        gate_col = sb("gate_col", [P, 2 * KD])
        diag = sb("diag", [P, 2 * KD, P])
        ones = sb("ones", [P, P])
        chunk_rows = sb("chunk_rows", [2, 2, CH * P])
        mod1_ps = ctx.enter_context(nc.psum_tensor("mod1_ps", [P, HALF], F32))
        mod2_ps = ctx.enter_context(nc.psum_tensor("mod2_ps", [P, HALF], F32))
        tr_ps = [ctx.enter_context(nc.psum_tensor(f"tr_ps{i}", [P, HALF], F32)) for i in range(4)]
        row_ps = [ctx.enter_context(nc.psum_tensor(f"row_ps{i}", [P, HALF], F32)) for i in range(2)]

        vec_in = sem("vec_in")
        x_in = [sem(f"x_in{t}") for t in range(TT)]
        w_in = [sem(f"w_ada_in{i}") for i in range(RING)]
        silu_done = sem("silu_done")
        ssq_done = sem("ssq_done")
        std_done = sem("std_done")
        xn_done = sem("xn_done")
        chunk_used = sem("chunk_used")
        chunk_out = sem("chunk_out")
        chunk_turned = sem("chunk_turned")
        mod_done = sem("mod_done")
        dve = sem("dve")
        tr_done = sem("tr_done")
        modulated = sem("modulated")
        hi_done = sem("hi_done")
        lo_done = sem("lo_done")
        diag_done = sem("diag_done")
        row_mm = sem("row_mm")
        ones_set = sem("ones_set")
        row_out = sem("row_out")

        vec, ident, hw, hcw, hp, hcp, mod, gs2, rows1, rows2 = (
            keep[n] for n in ("vec", "ident", "hw", "hcw", "hp", "hcp", "mod", "gs2", "rows1", "rows2"))
        mod_src = io["w_ada"].rearrange("(k p) c -> p k c", p=P)
        turns = [("x", 4 * q, 4, k) for q in range(NT // 4) for k in range(KD)] + [("c", NT, CT, k) for k in range(KD)]

        FIRST = 2 * KD // CH
        assert 3 * (NCH - FIRST) == len(turns)

        def place(n):
            which, t0, nt, k = turns[n]
            if which == "c":
                return hcw[:, k, :], hcp[:, k]
            cols = slice(t0 * P, (t0 + nt) * P)
            return hw[:, k, cols], hp[:, k, :, cols]

        block = ctx.enter_context(nc.Block())

        @block.sync
        def _(sp):
            sp.dma_start(vec[:], io["vec"]).then_inc(vec_in, 16)
            sp.dma_start(ident[:], io["ident"]).then_inc(vec_in, 16)
            for n in range(NCH):
                if n >= RING:
                    sp.wait_ge(chunk_used, n - RING + 1)
                sp.dma_start(w_sb[n % RING], mod_src[:, :, n * CH * P:(n + 1) * CH * P]).then_inc(w_in[n % RING], 16)

        @block.scalar
        def _(act):
            for t in range(TT):
                src = io["x"][t * P:(t + 1) * P, :] if t < NT else io["ctx"][(t - NT) * P:(t - NT + 1) * P, :]
                act.dma_start(x_sb[:, t, :], src).then_inc(x_in[t], 16)
            act.wait_ge(vec_in, 32)
            nc.scalar.activation(silu_c[:].rearrange("p k c -> p (k c)"), vec[:, V_COND:V_END],
                                 ACT.Silu).then_inc(silu_done, 1)
            for t in range(TT):
                act.wait_ge(x_in[t], 16)
                if t >= 2:
                    act.wait_ge(ssq_done, t - 1)
                nc.scalar.activation(square[:, t % 2, :], x_sb[:, t, :], ACT.Square,
                                     accum_out=ssq[:, t:t + 1]).then_inc(ssq_done, 1)
            act.wait_ge(dve, 1)
            nc.scalar.activation(std[:], std[:], ACT.Sqrt).then_inc(std_done, 1)

            def modulate(n):
                which, t0, nt, k = turns[n]
                act.wait_ge(tr_done, n + 1)
                g, sh = (gs1, mod) if which == "x" else (cgs1, cmod)
                nc.scalar.activation(place(n)[0], tr_ps[n % 4][:, 0:nt * P], ACT.Identity,
                                     bias=sh[:, k:k + 1], scale=g[:, k:k + 1]).then_inc(modulated, 1)

            for n in range(NCH):
                act.wait_ge(chunk_used, n + 1)
                if n >= 2:
                    act.wait_ge(chunk_turned, n - 1)
                nc.scalar.copy(chunk_rows[:, n % 2, :], row_ps[n % 2][0:2, :]).then_inc(chunk_out, 1)
                if n == FIRST:
                    act.wait_ge(mod_done, 1)
                if n >= FIRST:
                    for i in range(3 * (n - FIRST), 3 * (n - FIRST + 1)):
                        modulate(i)

        @block.gpsimd
        def _(pool):
            nc.gpsimd.memset(keep["eps"][:], EPS)
            nc.gpsimd.memset(ones[:], 1.0).then_inc(ones_set, 1)
            for n in range(len(turns)):
                whole, parts = place(n)
                pool.wait_ge(hi_done, n + 1)
                nc.gpsimd.tensor_tensor(parts[:, 1], whole, parts[:, 0], ALU.subtract).then_inc(lo_done, 1)

        @block.tensor
        def _(pe):
            pe.wait_ge(silu_done, 1)

            def turn(n):
                which, t0, nt, k = turns[n]
                if n % 4 == 0:
                    pe.wait_ge(xn_done, t0 + nt)
                if n >= 4:
                    pe.wait_ge(modulated, n - 3)
                for j in range(nt):
                    last = nc.tensor.transpose(tr_ps[n % 4][:, j * P:(j + 1) * P], x_sb[:, t0 + j, k * P:(k + 1) * P],
                                               ident[:])
                last.then_inc(tr_done, 1)

            def turn_chunk(n):
                pe.wait_ge(chunk_out, n + 1)
                for c in range(CH):
                    m = n * CH + c
                    out = mod1_ps[:, 2 * m:2 * m + 2] if m < 2 * KD else mod2_ps[:, 2 * m:2 * m + 2]
                    last = nc.tensor.transpose(out, chunk_rows[:, n % 2, c * P:(c + 1) * P], ident[0:2, 0:2])
                last.then_inc(chunk_turned, 1)

            for n in range(NCH):
                pe.wait_ge(w_in[n % RING], 16 * (n // RING + 1))
                if n >= 2:
                    pe.wait_ge(chunk_out, n - 1)
                for k in range(KD):
                    last = nc.tensor.matmul(row_ps[n % 2][0:2, :], silu_c[:, k, :], w_sb[n % RING][:, k, :],
                                            start=(k == 0), stop=(k == KD - 1))
                last.then_inc(chunk_used, 1)
                if n >= 1:
                    turn_chunk(n - 1)
                if n >= FIRST:
                    for i in range(3 * (n - FIRST), 3 * (n - FIRST + 1)):
                        turn(i)
            turn_chunk(NCH - 1)
            pe.wait_ge(ones_set, 1)
            for g in range(4):
                pe.wait_ge(diag_done, 4 * g + 4)
                if g >= 2:
                    pe.wait_ge(row_out, g - 1)
                for j in range(4):
                    last = nc.tensor.matmul(row_ps[g % 2][:, j * P:(j + 1) * P], ones[:], diag[:, 4 * g + j, :],
                                            start=True, stop=True)
                last.then_inc(row_mm, 1)

        @block.vector
        def _(v):
            c = Count(dve)
            v.wait_ge(ssq_done, TT)
            c.up(nc.vector.tensor_scalar(std[:], ssq[:], 1.0 / D, EPS, ALU.mult, ALU.add))
            v.wait_ge(std_done, 1)
            c.then_wait(v, nc.vector.reciprocal(rstd[:], std[:]))
            for t in range(TT):
                nc.vector.tensor_scalar(x_sb[:, t, :], x_sb[:, t, :], rstd[:, t:t + 1], None,
                                        ALU.mult).then_inc(xn_done, 1)
            v.wait_ge(chunk_turned, FIRST)
            both = mod1_ps[:, 0:4 * KD].rearrange("p (m c) -> p m c", c=2)
            nc.vector.tensor_tensor(mod[:, 0:2 * KD], both[:, :, 0], vec[:, V_BADA:V_BADA + 2 * KD], ALU.add)
            c.then_wait(v, nc.vector.tensor_tensor(cmod[:], both[:, :, 1], vec[:, V_BADA:V_BADA + 2 * KD], ALU.add))
            g1 = vec[:, V_GPRE1:V_GPRE1 + KD]
            nc.vector.scalar_tensor_tensor(gs1[:], mod[:, KD:2 * KD], 1.0, g1, ALU.add, ALU.mult)
            nc.vector.scalar_tensor_tensor(cgs1[:], cmod[:, KD:2 * KD], 1.0, g1, ALU.add, ALU.mult).then_inc(mod_done, 1)
            for n in range(len(turns)):
                whole, parts = place(n)
                v.wait_ge(modulated, n + 1)
                nc.vector.tensor_copy(parts[:, 0], whole).then_inc(hi_done, 1)
            v.wait_ge(chunk_turned, NCH)
            c.then_wait(v, nc.vector.tensor_tensor(
                mod[:, 2 * KD:], mod2_ps[:, 4 * KD:2 * MODT].rearrange("p (m c) -> p m c", c=2)[:, :, 0],
                vec[:, V_BADA + 2 * KD:V_BADA + MODT], ALU.add))
            nc.vector.scalar_tensor_tensor(gs2[:], mod[:, 4 * KD:5 * KD], 1.0, vec[:, V_GPRE2:V_GPRE2 + KD],
                                           ALU.add, ALU.mult)
            nc.vector.tensor_tensor(gate_col[:, 0:KD], mod[:, 2 * KD:3 * KD], vec[:, V_GPOST1:V_GPOST1 + KD], ALU.mult)
            c.then_wait(v, nc.vector.tensor_tensor(gate_col[:, KD:], mod[:, 5 * KD:6 * KD],
                                                   vec[:, V_GPOST2:V_GPOST2 + KD], ALU.mult))
            for k in range(2 * KD):
                nc.vector.tensor_scalar(diag[:, k, :], ident[:], gate_col[:, k:k + 1], None,
                                        ALU.mult).then_inc(diag_done, 1)
            for g in range(4):
                v.wait_ge(row_mm, g + 1)
                nc.vector.tensor_copy((rows1 if g < NH else rows2)[:, g % NH, :], row_ps[g % 2][:]).then_inc(row_out, 1)


def projection(nc, io, keep):
    with ExitStack() as ctx:
        signals = ctx.enter_context(Signals(nc))

        def sb(name, shape, dt=F32):
            return ctx.enter_context(nc.sbuf_tensor(f"projection_{name}", shape, dt))

        def sem(name):
            return signals.new(f"projection_{name}")

        vec, hp, hw, hcw, conv, rstd_row, q, k_sb, kc = (
            keep[n] for n in ("vec", "hp", "hw", "hcw", "conv", "rstd_row", "q", "k", "kc"))
        RAWS = 3
        RING = 3
        w_raw = sb("w_raw", [P, RAWS, D])
        w_part = sb("w_part", [P, RING, 2, D], BF16)
        glu = sb("glu", [P, 2, SEQ + 2 * PAD])
        odd = sb("odd", [P, SEQ])
        sig = sb("sig", [P, 2, SEQ])
        square = sig[:].rearrange("p a (b n) -> p (a b) n", n=HALF)
        mean_w = sb("mean_w", [P, P])
        BANKS = 8
        bank = [ctx.enter_context(nc.psum_tensor(f"proj_ps{i}", [P, HALF], F32)) for i in range(BANKS)]

        w_in = [sem(f"w_in{i}") for i in range(RAWS)]
        w_hi = sem("w_hi")
        w_lo = sem("w_lo")
        piece_mm = sem("piece_mm")
        act_read = sem("act_read")
        dve_read = sem("dve_read")
        dve = sem("dve")
        glu_zero = sem("glu_zero")
        conv_done = sem("conv_done")
        sq_done = sem("sq_done")
        mean_set = sem("mean_set")

        order = [t for c in range(CC) for t in (CC + c, c)] + list(range(2 * CC, 2 * CC + 2 * CA))
        NC = 2 * CC
        kind_of = lambda t: "value" if t < CC else "gate" if t < 2 * CC else "q" if t < 2 * CC + CA else "k"
        pieces = []
        for t in order:
            pieces += [(kind_of(t), t % CC, h) for h in range(NH)]
            if kind_of(t) == "k":
                pieces.append(("kc", t % CC, 0))
        pieces += [("mean", 0, h) for h in range(NH)] + [("var", 0, h) for h in range(NH)]
        number = {p: n for n, p in enumerate(pieces)}
        by_dve = [p for p in pieces if p[0] in ("value", "mean")]
        by_act = [p for p in pieces if p not in by_dve]

        def place(p):
            kind, i, h = p
            cols = slice(h * HALF, (h + 1) * HALF)
            return kc[:, i] if kind == "kc" else (q if kind == "q" else k_sb)[:, i, cols]

        def last_piece(t):
            return number[("kc", t % CC, 0) if kind_of(t) == "k" else (kind_of(t), t % CC, NH - 1)]

        def wait_read(eng, p):
            if p in by_dve:
                eng.wait_ge(dve_read, by_dve.index(p) + 1)
            else:
                eng.wait_ge(act_read, by_act.index(p) + 1)

        block = ctx.enter_context(nc.Block())

        @block.sync
        def _(sp):
            for i, t in enumerate(order):
                if RAWS <= i < NC + RAWS:
                    sp.wait_ge(w_lo, i - RAWS + 1)
                elif i >= RAWS:
                    sp.wait_ge(piece_mm, last_piece(order[i - RAWS]) + 1)
                sp.dma_start(w_raw[:, i % RAWS], io["w_in_t"][t]).then_inc(w_in[i % RAWS], 16)

        @block.tensor
        def _(pe):
            def make(n, terms, width=HALF):
                if n >= BANKS:
                    wait_read(pe, pieces[n - BANKS])
                for i, (w, m) in enumerate(terms):
                    last = nc.tensor.matmul(bank[n % BANKS][:, 0:width], w, m, start=(i == 0), stop=(i == len(terms) - 1))
                last.then_inc(piece_mm, 1)

            for i, t in enumerate(order[:NC]):
                pe.wait_ge(w_lo, i + 1)
                w = w_part[:, i % RING]
                for h in range(NH):
                    make(number[(kind_of(t), t % CC, h)],
                         [(w[:, a, k * P:(k + 1) * P], hp[:, k, b, h * HALF:(h + 1) * HALF])
                          for a, b in PARTS for k in range(KD)])
            for i, t in enumerate(order[NC:], NC):
                pe.wait_ge(w_in[i % RAWS], 16 * (i // RAWS + 1))
                w = w_raw[:, i % RAWS]
                for h in range(NH):
                    make(number[(kind_of(t), t % CC, h)],
                         [(w[:, k * P:(k + 1) * P], hw[:, k, h * HALF:(h + 1) * HALF]) for k in range(KD)])
                if kind_of(t) == "k":
                    make(number[("kc", t % CC, 0)], [(w[:, k * P:(k + 1) * P], hcw[:, k, :]) for k in range(KD)], CTX)
            pe.wait_ge(mean_set, 1)
            pe.wait_ge(conv_done, CC)
            for h in range(NH):
                make(number[("mean", 0, h)], [(mean_w[:], conv[:, c, h * HALF:(h + 1) * HALF]) for c in range(CC)])
            for h in range(NH):
                pe.wait_ge(sq_done, CC * (h + 1))
                make(number[("var", 0, h)], [(mean_w[:], square[:, c, :]) for c in range(CC)])

        @block.scalar
        def _(act):
            def take(i):
                act.wait_ge(w_in[i % RAWS], 16 * (i // RAWS + 1))
                if i >= RING:
                    act.wait_ge(piece_mm, last_piece(order[i - RING]) + 1)
                nc.scalar.copy(w_part[:, i % RING, 0], w_raw[:, i % RAWS]).then_inc(w_hi, 1)

            taken = 0
            for n, (kind, i, h) in enumerate(pieces):
                while taken < NC and (taken < 2 or last_piece(order[taken - 2]) <= n + 1):
                    take(taken)
                    taken += 1
                cols = slice(h * HALF, (h + 1) * HALF)
                src = bank[n % BANKS][:]
                if (kind, i, h) in by_dve:
                    continue
                if kind == "var":
                    for c in range(CC):
                        act.wait_ge(dve_read, by_dve.index(("mean", 0, h)) + 1)
                        if h > 0:
                            act.wait_ge(piece_mm, number[("var", 0, h - 1)] + 1)
                        nc.scalar.activation(square[:, c, :], conv[:, c, cols], ACT.Square).then_inc(sq_done, 1)
                act.wait_ge(piece_mm, n + 1)
                if kind == "gate":
                    if i >= 2:
                        act.wait_ge(dve_read, by_dve.index(("value", i - 2, NH - 1)) + 1)
                    nc.scalar.activation(sig[:, i % 2, cols], src, ACT.Sigmoid).then_inc(act_read, 1)
                elif kind == "var":
                    nc.scalar.activation(rstd_row[:, cols], src, ACT.Sqrt, bias=keep["eps"][:, 0:1]).then_inc(act_read, 1)
                else:
                    width = CTX if kind == "kc" else HALF
                    scale = HD ** -0.5 if kind == "q" else 1.0
                    nc.scalar.activation(place((kind, i, h)), src[:, 0:width], ACT.Copy, scale=scale).then_inc(act_read, 1)

        @block.gpsimd
        def _(pool):
            nc.gpsimd.memset(mean_w[:], 1.0 / D_CONV).then_inc(mean_set, 1)
            nc.gpsimd.memset(glu[:, :, 0:PAD], 0.0)
            nc.gpsimd.memset(glu[:, :, PAD + SEQ:], 0.0).then_inc(glu_zero, 1)

            for i in range(NC):
                pool.wait_ge(w_hi, i + 1)
                nc.gpsimd.tensor_tensor(w_part[:, i % RING, 1], w_raw[:, i % RAWS], w_part[:, i % RING, 0],
                                        ALU.subtract).then_inc(w_lo, 1)

        @block.vector
        def _(v):
            ch = Count(dve)
            v.wait_ge(glu_zero, 1)

            def gated(c):
                for h in range(NH):
                    v.wait_ge(piece_mm, number[("value", c, h)] + 1)
                    v.wait_ge(act_read, by_act.index(("gate", c, h)) + 1)
                    cols = slice(h * HALF, (h + 1) * HALF)
                    nc.vector.tensor_tensor(glu[:, c % 2, PAD + h * HALF:PAD + (h + 1) * HALF],
                                            bank[number[("value", c, h)] % BANKS][:], sig[:, c % 2, cols],
                                            ALU.mult).then_inc(dve_read, 1)

            def depthwise(c):
                v.wait_ge(dve_read, by_dve.index(("value", c, NH - 1)) + 1)
                made = []
                for tap in range(TAPS):
                    w = vec[:, V_CONVW + c * TAPS + tap:V_CONVW + c * TAPS + tap + 1]
                    src = glu[:, c % 2, tap:tap + SEQ]
                    acc = conv[:, c, :] if tap % 2 == 0 else odd[:]
                    if tap >= 2:
                        v.wait_ge(dve, made[tap - 2])
                    if tap == 1 and c >= 1:
                        v.wait_ge(conv_done, c)
                    if tap == 0:
                        ins = nc.vector.tensor_scalar(acc, src, w, vec[:, V_CONVB + c:V_CONVB + c + 1], ALU.mult, ALU.add)
                    elif tap == 1:
                        ins = nc.vector.tensor_scalar(acc, src, w, None, ALU.mult)
                    else:
                        ins = nc.vector.scalar_tensor_tensor(acc, src, w, acc, ALU.mult, ALU.add)
                    made.append(ch.up(ins))
                v.wait_ge(dve, made[-1])
                nc.vector.tensor_tensor(conv[:, c, :], conv[:, c, :], odd[:], ALU.add).then_inc(conv_done, 1)

            gated(0)
            gated(1)
            for c in range(CC):
                depthwise(c)
                if c + 2 < CC:
                    gated(c + 2)
            v.wait_ge(conv_done, CC)
            for h in range(NH):
                n = number[("mean", 0, h)]
                v.wait_ge(piece_mm, n + 1)
                for c in range(CC):
                    cols = slice(h * HALF, (h + 1) * HALF)
                    ins = nc.vector.tensor_tensor(conv[:, c, cols], conv[:, c, cols], bank[n % BANKS][:], ALU.subtract)
                ins.then_inc(dve_read, 1)
            v.wait_ge(act_read, len(by_act))
            ch.then_wait(v, nc.vector.reciprocal(rstd_row[:], rstd_row[:]))

def values(nc, io, keep):
    with ExitStack() as ctx:
        signals = ctx.enter_context(Signals(nc))

        def sb(name, shape, dt=F32):
            return ctx.enter_context(nc.sbuf_tensor(f"values_{name}", shape, dt))

        def sem(name):
            return signals.new(f"values_{name}")

        vec, hp, hcp, conv, rstd_row, v_p, vc_p = (
            keep[n] for n in ("vec", "hp", "hcp", "conv", "rstd_row", "v_p", "vc_p"))
        conv_p = conv[:].bitcast(BF16).rearrange("p c (s n) -> p c s n", s=2)
        w_raw = sb("w_raw", [P, KD, D_NA])
        w_part = sb("w_part", [P, KD, 2, D_NA], BF16)
        TEMPS = 4
        temp = sb("temp", [P, TEMPS, HALF])
        swish = sb("swish", [P, CC, SEQ])
        TT = NT + CT
        BANKS = 8
        bank = [ctx.enter_context(nc.psum_tensor(f"v_bank{i}", [P, HALF], F32)) for i in range(BANKS)]
        tokens = lambda t, k, s: hp[:, k, s, t * P:(t + 1) * P] if t < NT else hcp[:, k, s, (t - NT) * P:(t - NT + 1) * P]
        place = lambda t: v_p[:, t] if t < NT else vc_p[:, t - NT]

        w_in = [sem(f"w_in{k}") for k in range(KD)]
        w_hi = sem("w_hi")
        w_lo = sem("w_lo")
        v_mm = sem("v_mm")
        v_hi = sem("v_hi")
        v_lo = sem("v_lo")
        normed = sem("normed")
        swished = sem("swished")
        conv_hi = sem("conv_hi")
        conv_lo = sem("conv_lo")

        block = ctx.enter_context(nc.Block())

        @block.sync
        def _(sp):
            for k in range(KD):
                sp.dma_start(w_raw[:, k], io["w_v"][k * P:(k + 1) * P, :]).then_inc(w_in[k], 16)

        @block.tensor
        def _(pe):
            def product(t, k):
                for i, (a, b) in enumerate(PARTS):
                    last = nc.tensor.matmul(bank[t % BANKS][:], tokens(t, k, a), w_part[:, k, b],
                                            start=(k == 0 and i == 0), stop=(k == KD - 1 and i == len(PARTS) - 1))
                return last

            for k in range(KD):
                pe.wait_ge(w_lo, k + 1)
                for t in range(TT - 6):
                    last = product(t, k)
                    if k == KD - 1:
                        last.then_inc(v_mm, 1)
            for t in range(TT - 6, TT):
                if t >= BANKS:
                    pe.wait_ge(v_hi, t - BANKS + 1)
                for k in range(KD):
                    last = product(t, k)
                last.then_inc(v_mm, 1)

        @block.scalar
        def _(act):
            for k in range(KD):
                act.wait_ge(w_in[k], 16)
                nc.scalar.copy(w_part[:, k, 0], w_raw[:, k]).then_inc(w_hi, 1)
            for c in range(CC):
                act.wait_ge(normed, c + 1)
                nc.scalar.activation(swish[:, c, :], conv[:, c, :], ACT.Silu, bias=vec[:, V_CNB + c:V_CNB + c + 1],
                                     scale=vec[:, V_CNG + c:V_CNG + c + 1]).then_inc(swished, 1)
            for t in range(TT):
                act.wait_ge(v_mm, t + 1)
                if t >= TEMPS:
                    act.wait_ge(v_lo, t - TEMPS + 1)
                nc.scalar.copy(temp[:, t % TEMPS], bank[t % BANKS][:])
                nc.scalar.copy(place(t)[:, 0], bank[t % BANKS][:]).then_inc(v_hi, 1)

        @block.vector
        def _(v):
            for k in range(KD):
                v.wait_ge(w_hi, k + 1)
                nc.vector.tensor_tensor(w_part[:, k, 1], w_raw[:, k], w_part[:, k, 0], ALU.subtract).then_inc(w_lo, 1)
                if k % 2 == 1:
                    c = k // 2
                    nc.vector.tensor_tensor(conv[:, c, :], conv[:, c, :], rstd_row[:], ALU.mult).then_inc(normed, 1)
            for c in range(CC):
                v.wait_ge(swished, c + 1)
                nc.vector.tensor_copy(conv_p[:, c, 0], swish[:, c]).then_inc(conv_hi, 1)
                v.wait_ge(conv_hi, c + 1)
                nc.vector.tensor_tensor(conv_p[:, c, 1], swish[:, c], conv_p[:, c, 0], ALU.subtract).then_inc(conv_lo, 1)

        @block.gpsimd
        def _(pool):
            for t in range(TT):
                pool.wait_ge(v_hi, t + 1)
                nc.gpsimd.tensor_tensor(place(t)[:, 1], temp[:, t % TEMPS], place(t)[:, 0], ALU.subtract).then_inc(v_lo, 1)


def attention(nc, io, keep):
    with ExitStack() as ctx:
        signals = ctx.enter_context(Signals(nc))

        def sb(name, shape, dt=F32):
            return ctx.enter_context(nc.sbuf_tensor(f"attention_{name}", shape, dt))

        def sem(name):
            return signals.new(f"attention_{name}")

        ident, q, k_sb, kc, v_p, vc_p, att_p = (
            keep[n] for n in ("ident", "q", "k", "kc", "v_p", "vc_p", "att_p"))
        bias = sb("bias", [P, HEADS, BIAS_R * GRID_W])
        LAT = IN_ROWS * GRID_W
        KB = (LAT + P - 1) // P
        KEYS = LAT + CTX
        SLOTS = 4
        score = sb("score", [P, SLOTS, KEYS])
        PROBS = 3
        prob_p = sb("prob_p", [P, PROBS, 2, (CT + KB) * P], BF16)
        mask = sb("mask", [P, BIAS_R * GRID_W])
        zero = sb("zero", [P, 1])
        STATS = 8
        top = sb("top", [P, STATS, 2])
        neg_max = sb("neg_max", [P, STATS])
        sums = sb("sums", [P, STATS])
        rsum = sb("rsum", [P, STATS])
        heads_out = sb("heads_out", [P, 2, D_NA])
        temp = sb("temp", [P, HALF])
        s_ps = ctx.enter_context(nc.psum_tensor("s_ps", [P, 2 * HALF], F32))
        pt_ps = [ctx.enter_context(nc.psum_tensor(f"pt_ps{i}", [P, 2 * HALF], F32)) for i in range(2)]
        o_ps = ctx.enter_context(nc.psum_tensor("o_ps", [P, HALF], F32))
        ot_ps = ctx.enter_context(nc.psum_tensor("ot_ps", [P, HALF], F32))

        bias_in = [sem(f"bias_in{h}") for h in range(HEADS)]
        mask_in = sem("mask_in")
        zero_set = sem("zero_set")
        bias_done = sem("bias_done")
        scores_mm = sem("scores_mm")
        biased = sem("biased")
        neg_done = sem("neg_done")
        exp_done = sem("exp_done")
        prob_turned = sem("prob_turned")
        prob_hi = sem("prob_hi")
        prob_lo = sem("prob_lo")
        out_mm = sem("out_mm")
        out_done = sem("out_done")
        outT_mm = sem("outT_mm")
        outT_read = sem("outT_read")
        outT_done = sem("outT_done")
        dve = sem("dve")

        plan = []
        for j in range(PAIRS):
            lo = min(max(2 * j - WIN_R // 2, 0), ROWS - WIN_R)
            hi = min(max(2 * j + 1 - WIN_R // 2, 0), ROWS - WIN_R)
            if lo == hi:
                plan.append((lo, WIN_R, EDGE_ROWS[j if j < 2 else j - PAIRS + 4] - 1))
            else:
                plan.append((lo, IN_ROWS, T_ROWS))
            assert lo % 2 == 0
        units = [(j, h) for j in range(PAIRS) for h in range(HEADS)]

        block = ctx.enter_context(nc.Block())

        @block.sync
        def _(sp):
            sp.dma_start(mask[:], io["mask"]).then_inc(mask_in, 16)
            for h in range(HEADS):
                src = io["rpb_t"][h]
                edge, inner = T_ROWS * GRID_W, IN_ROWS * GRID_W
                sp.dma_start(bias[0:GRID_W, h, 0:edge], src[:, 1:1 + T_ROWS, :].rearrange("q r c -> q (r c)")).then_inc(bias_in[h], 16)
                sp.dma_start(bias[GRID_W:P, h, 0:edge], src[:, 0:T_ROWS, :].rearrange("q r c -> q (r c)")).then_inc(bias_in[h], 16)
                sp.dma_start(bias[0:GRID_W, h, edge:edge + inner], src[:, 3:3 + IN_ROWS, :].rearrange("q r c -> q (r c)")).then_inc(bias_in[h], 16)
                sp.dma_start(bias[GRID_W:P, h, edge:edge + inner], src[:, 2:2 + IN_ROWS, :].rearrange("q r c -> q (r c)")).then_inc(bias_in[h], 16)

        def key_blocks(u):
            j, h = units[u]
            r0, nr, _ = plan[j]
            cols = slice(h * HD, (h + 1) * HD)
            out = [(b * P, P, vc_p[:, b, :, cols]) for b in range(CT)]
            for b in range((nr * GRID_W + P - 1) // P):
                n = min(P, nr * GRID_W - b * P)
                out.append((CTX + b * P, n, v_p[0:n, r0 * GRID_W // P + b, :, cols]))
            return out

        def spans(u):
            nk = CTX + plan[units[u][0]][1] * GRID_W
            full = nk // P * P
            return [(P, slice(0, full))] + ([(nk - full, slice(full, full + P))] if nk > full else [])

        TURN_LAG = 2
        SPLIT_LAG = 3
        OUT_LAG = 4

        @block.tensor
        def _(pe):
            def scores(u):
                j, h = units[u]
                r0, nr, _ = plan[j]
                if u >= 1:
                    pe.wait_ge(biased, u)
                part = slice(HD * (h % 2), HD * (h % 2) + HD)
                g = h // 2
                k0, nk = r0 * GRID_W, nr * GRID_W
                for dst, keys in ((slice(0, CTX), kc[part, g, :]),
                                  (slice(CTX, HALF), k_sb[part, g, k0:k0 + HALF - CTX]),
                                  (slice(HALF, CTX + nk), k_sb[part, g, k0 + HALF - CTX:k0 + nk])):
                    last = nc.tensor.matmul(s_ps[:, dst], q[part, g, j * P:(j + 1) * P], keys,
                                            start=True, stop=True)
                last.then_inc(scores_mm, 1)

            def turn(u):
                pe.wait_ge(exp_done, u + 1)
                if u >= 2:
                    pe.wait_ge(prob_lo, u - 1)
                for b, (c, n, _) in enumerate(key_blocks(u)):
                    last = nc.tensor.transpose(pt_ps[u % 2][0:n, b * P:(b + 1) * P], score[:, u % SLOTS, c:c + n], ident[:])
                last.then_inc(prob_turned, 1)

            def outputs(u):
                pe.wait_ge(prob_lo, u + 1)
                if u >= 1:
                    pe.wait_ge(out_done, u)
                terms = [(b, n, vals, x, y) for b, (c, n, vals) in enumerate(key_blocks(u)) for x, y in PARTS]
                for i, (b, n, vals, x, y) in enumerate(terms):
                    last = nc.tensor.matmul(o_ps[:, 0:HD], prob_p[0:n, u % PROBS, x, b * P:(b + 1) * P], vals[:, y],
                                            start=(i == 0), stop=(i == len(terms) - 1))
                last.then_inc(out_mm, 1)

            def turned(j):
                pe.wait_ge(out_done, HEADS * (j + 1))
                if j >= 1:
                    pe.wait_ge(outT_read, j)
                for c in range(CA):
                    last = nc.tensor.transpose(ot_ps[:, c * P:(c + 1) * P], heads_out[:, j % 2, c * P:(c + 1) * P], ident[:])
                last.then_inc(outT_mm, 1)

            for u in range(len(units) + OUT_LAG):
                if u < len(units):
                    scores(u)
                if TURN_LAG <= u < len(units) + TURN_LAG:
                    turn(u - TURN_LAG)
                if u >= OUT_LAG:
                    w = u - OUT_LAG
                    outputs(w)
                    if w % HEADS == 0 and w > 0:
                        turned(w // HEADS - 1)
            turned(PAIRS - 1)

        @block.scalar
        def _(act):
            def probs(u):
                nk = CTX + plan[units[u][0]][1] * GRID_W
                s, m = u % SLOTS, u % STATS
                act.wait_ge(neg_done, u + 1)
                if u >= STATS:
                    act.wait_ge(out_done, u - STATS + 1)
                nc.scalar.activation(score[:, s, 0:nk], score[:, s, 0:nk], ACT.Exp, bias=neg_max[:, m:m + 1],
                                     accum_out=sums[:, m:m + 1]).then_inc(exp_done, 1)

            def round_probs(u):
                act.wait_ge(prob_turned, u + 1)
                if u >= PROBS:
                    act.wait_ge(out_mm, u - PROBS + 1)
                for n, cols in spans(u):
                    ins = nc.scalar.copy(prob_p[0:n, u % PROBS, 0, cols], pt_ps[u % 2][0:n, cols])
                ins.then_inc(prob_hi, 1)

            for u in range(len(units) + TURN_LAG):
                if u >= TURN_LAG:
                    round_probs(u - TURN_LAG)
                if u < len(units):
                    probs(u)

        @block.gpsimd
        def _(pool):
            for j in range(PAIRS):
                pool.wait_ge(outT_read, j + 1)
                nc.gpsimd.tensor_tensor(att_p[:, :, j, 1], temp[:].rearrange("p (c n) -> p c n", c=CA),
                                        att_p[:, :, j, 0], ALU.subtract).then_inc(outT_done, 1)

        @block.vector
        def _(v):
            ch = Count(dve)
            nc.vector.memset(zero[:], 0.0).then_inc(zero_set, 1)
            v.wait_ge(mask_in, 16)
            v.wait_ge(zero_set, 1)

            def masked_bias(h):
                v.wait_ge(bias_in[h], 64)
                nc.vector.tensor_tensor(bias[:, h, :], bias[:, h, :], mask[:], ALU.add).then_inc(bias_done, 1)
                v.wait_ge(bias_done, h + 1)

            def biased_scores(u):
                j, h = units[u]
                _, nr, t0 = plan[j]
                nk = nr * GRID_W
                s = u % SLOTS
                if j == 0:
                    masked_bias(h)
                v.wait_ge(scores_mm, u + 1)
                if u >= SLOTS:
                    v.wait_ge(prob_turned, u - SLOTS + 1)
                nc.vector.tensor_tensor_reduce(score[:, s, 0:CTX], s_ps[:, 0:CTX],
                                               zero[:].to_broadcast([P, CTX]), 1.0, NEG, ALU.add, ALU.max,
                                               top[:, u % STATS, 0:1])
                nc.vector.tensor_tensor_reduce(score[:, s, CTX:CTX + nk], s_ps[:, CTX:CTX + nk],
                                               bias[:, h, t0 * GRID_W:t0 * GRID_W + nk], 1.0, NEG,
                                               ALU.add, ALU.max, top[:, u % STATS, 1:2]).then_inc(biased, 1)

            def maximum(u):
                s = u % STATS
                v.wait_ge(biased, u + 1)
                nc.vector.tensor_reduce(neg_max[:, s:s + 1], top[:, s, :], AX_X, ALU.max,
                                        negate=True).then_inc(neg_done, 1)

            def split_probs(u):
                v.wait_ge(prob_hi, u + 1)
                for n, cols in spans(u):
                    ins = nc.vector.tensor_tensor(prob_p[0:n, u % PROBS, 1, cols], pt_ps[u % 2][0:n, cols],
                                                  prob_p[0:n, u % PROBS, 0, cols], ALU.subtract)
                ins.then_inc(prob_lo, 1)

            def invert(u):
                v.wait_ge(exp_done, u + 1)
                ch.up(nc.vector.reciprocal(rsum[:, u % STATS:u % STATS + 1], sums[:, u % STATS:u % STATS + 1]))

            def normalise(u):
                j, h = units[u]
                v.wait_ge(dve, u + 1)
                v.wait_ge(out_mm, u + 1)
                if h == 0 and j >= 2:
                    v.wait_ge(outT_mm, j - 1)
                nc.vector.tensor_scalar(heads_out[:, j % 2, h * HD:(h + 1) * HD], o_ps[:, 0:HD],
                                        rsum[:, u % STATS:u % STATS + 1], None, ALU.mult).then_inc(out_done, 1)

            def place(j):
                v.wait_ge(outT_mm, j + 1)
                if j >= 1:
                    v.wait_ge(outT_done, j)
                nc.vector.tensor_copy(temp[:], ot_ps[:])
                nc.vector.tensor_copy(att_p[:, :, j, 0],
                                      ot_ps[:].rearrange("p (c n) -> p c n", c=CA)).then_inc(outT_read, 1)

            for u in range(len(units) + OUT_LAG):
                if u < len(units):
                    biased_scores(u)
                    maximum(u)
                if SPLIT_LAG <= u < len(units) + SPLIT_LAG:
                    split_probs(u - SPLIT_LAG)
                    invert(u - SPLIT_LAG)
                if u >= OUT_LAG:
                    w = u - OUT_LAG
                    if w % HEADS == 1 and w > HEADS:
                        place(w // HEADS - 1)
                    normalise(w)
            place(PAIRS - 1)


def output(nc, io, keep):
    with ExitStack() as ctx:
        signals = ctx.enter_context(Signals(nc))

        def sb(name, shape, dt=F32):
            return ctx.enter_context(nc.sbuf_tensor(f"output_{name}", shape, dt))

        def sem(name):
            return signals.new(f"output_{name}")

        ident, conv, att_p, hp, mod, gs2, rows1 = (
            keep[n] for n in ("ident", "conv", "att_p", "hp", "mod", "gs2", "rows1"))
        conv_p = conv[:].bitcast(BF16).rearrange("p c (s n) -> p c s n", s=2)
        w_raw = sb("w_raw", [P, 2, D])
        w_part = sb("w_part", [P, KD, 2, D], BF16)
        temp = sb("temp", [P, 2, KD, P])
        x_sb = sb("x_res", [P, NT, D])
        square = sb("square", [P, 2, D])
        work = sb("work", [P, 2, D])
        ssq = sb("ssq", [P, 2, NT])
        std = sb("std", [P, 2, NT])
        rstd = sb("rstd", [P, 2, NT])
        y_ps = [ctx.enter_context(nc.psum_tensor(f"y_ps{i}", [P, D], F32)) for i in range(2)]
        t_ps = [ctx.enter_context(nc.psum_tensor(f"t_ps{i}", [P, D], F32)) for i in range(2)]

        w_in = [sem(f"w_in{i}") for i in range(2)]
        w_hi = sem("w_hi")
        w_lo = sem("w_lo")
        h_hi = sem("h_hi")
        h_lo = sem("h_lo")
        x_in = [sem(f"x_res_in{t}") for t in range(NT)]
        y_mm = sem("y_mm")
        y_ssq = sem("y_ssq")
        y_ms = sem("y_ms")
        y_std = sem("y_std")
        x2_done = sem("x2_done")
        x2_out = sem("x2_out")
        x2_ssq = sem("x2_ssq")
        x2_ms = sem("x2_ms")
        x2_std = sem("x2_std")
        normed = sem("normed")
        t_mm = sem("t_mm")
        t_act = sem("t_act")
        t_dve = sem("t_dve")
        dve = sem("dve")

        block = ctx.enter_context(nc.Block())

        @block.sync
        def _(sp):
            for k in range(KD):
                if k >= 2:
                    sp.wait_ge(w_lo, k - 1)
                sp.dma_start(w_raw[:, k % 2, :], io["w_out"][k * P:(k + 1) * P, :]).then_inc(w_in[k % 2], 16)
            for t in range(NT):
                sp.dma_start(x_sb[:, t, :], io["x"][t * P:(t + 1) * P, :]).then_inc(x_in[t], 16)
            for t in range(NT):
                sp.wait_ge(x2_done, t + 1)
                sp.dma_start(io["x2"][t * P:(t + 1) * P, :], x_sb[:, t, :]).then_inc(x2_out, 16)
            sp.wait_ge(x2_out, 16 * NT)

        @block.tensor
        def _(pe):
            def product(t):
                if t >= 2:
                    pe.wait_ge(x2_done, t - 1)
                for k in range(KD):
                    if t == 0:
                        pe.wait_ge(w_lo, k + 1)
                    mix = conv_p[:, k, :, t * P:(t + 1) * P] if k < CC else att_p[:, k - CC, t]
                    for h in range(NH):
                        for i, (a, b) in enumerate(PARTS):
                            last = nc.tensor.matmul(y_ps[t % 2][:, h * HALF:(h + 1) * HALF], mix[:, a],
                                                    w_part[:, k, b, h * HALF:(h + 1) * HALF], start=(k == 0 and i == 0),
                                                    stop=(k == KD - 1 and i == len(PARTS) - 1))
                last.then_inc(y_mm, 1)

            def turn(t):
                pe.wait_ge(normed, t + 1)
                if t >= 2:
                    pe.wait_ge(t_act, t - 1)
                    pe.wait_ge(t_dve, t - 1)
                for k in range(KD):
                    last = nc.tensor.transpose(t_ps[t % 2][:, k * P:(k + 1) * P], work[:, t % 2, k * P:(k + 1) * P], ident[:])
                last.then_inc(t_mm, 1)

            for t in range(NT + 1):
                if t < NT:
                    product(t)
                if t >= 1:
                    turn(t - 1)

        @block.scalar
        def _(act):
            for k in range(KD):
                act.wait_ge(w_in[k % 2], 16 * (k // 2 + 1))
                nc.scalar.copy(w_part[:, k, 0, :], w_raw[:, k % 2, :]).then_inc(w_hi, 1)
            for t in range(NT):
                act.wait_ge(y_mm, t + 1)
                nc.scalar.activation(square[:, 0, :], y_ps[t % 2][:], ACT.Square,
                                     accum_out=ssq[:, 0, t:t + 1]).then_inc(y_ssq, 1)
                act.wait_ge(y_ms, t + 1)
                nc.scalar.activation(std[:, 0, t:t + 1], std[:, 0, t:t + 1], ACT.Sqrt).then_inc(y_std, 1)
                act.wait_ge(x2_done, t + 1)
                nc.scalar.activation(square[:, 1, :], x_sb[:, t, :], ACT.Square,
                                     accum_out=ssq[:, 1, t:t + 1]).then_inc(x2_ssq, 1)
                act.wait_ge(x2_ms, t + 1)
                nc.scalar.activation(std[:, 1, t:t + 1], std[:, 1, t:t + 1], ACT.Sqrt).then_inc(x2_std, 1)
                act.wait_ge(t_mm, t + 1)
                if t >= 2:
                    act.wait_ge(h_lo, t - 1)
                for k in range(KD // 2):
                    ins = nc.scalar.activation(temp[:, t % 2, k, :], t_ps[t % 2][:, k * P:(k + 1) * P],
                                               ACT.Identity, bias=mod[:, 3 * KD + k:3 * KD + k + 1], scale=gs2[:, k:k + 1])
                ins.then_inc(t_act, 1)

        @block.gpsimd
        def _(pool):
            for k in range(KD):
                pool.wait_ge(w_hi, k + 1)
                nc.gpsimd.tensor_tensor(w_part[:, k, 1, :], w_raw[:, k % 2, :], w_part[:, k, 0, :],
                                        ALU.subtract).then_inc(w_lo, 1)
            for t in range(NT):
                pool.wait_ge(h_hi, t + 1)
                nc.gpsimd.tensor_tensor(hp[:, :, 1, t * P:(t + 1) * P], temp[:, t % 2], hp[:, :, 0, t * P:(t + 1) * P],
                                        ALU.subtract).then_inc(h_lo, 1)

        @block.vector
        def _(v):
            ch = Count(dve)
            for t in range(NT):
                y = y_ps[t % 2]
                v.wait_ge(y_ssq, t + 1)
                nc.vector.tensor_scalar(std[:, 0, t:t + 1], ssq[:, 0, t:t + 1], 1.0 / D, EPS, ALU.mult,
                                        ALU.add).then_inc(y_ms, 1)
                v.wait_ge(y_std, t + 1)
                ch.then_wait(v, nc.vector.reciprocal(rstd[:, 0, t:t + 1], std[:, 0, t:t + 1]))
                if t >= 2:
                    v.wait_ge(t_mm, t - 1)
                ch.then_wait(v, nc.vector.scalar_tensor_tensor(work[:, t % 2, :], y[:], rstd[:, 0, t:t + 1],
                                                               rows1[:].rearrange("p a b -> p (a b)"),
                                                               ALU.mult, ALU.mult))
                v.wait_ge(x_in[t], 16)
                nc.vector.tensor_tensor(x_sb[:, t, :], x_sb[:, t, :], work[:, t % 2, :], ALU.add).then_inc(x2_done, 1)
                v.wait_ge(x2_ssq, t + 1)
                nc.vector.tensor_scalar(std[:, 1, t:t + 1], ssq[:, 1, t:t + 1], 1.0 / D, EPS, ALU.mult,
                                        ALU.add).then_inc(x2_ms, 1)
                v.wait_ge(x2_std, t + 1)
                ch.then_wait(v, nc.vector.reciprocal(rstd[:, 1, t:t + 1], std[:, 1, t:t + 1]))
                nc.vector.tensor_scalar(work[:, t % 2, :], x_sb[:, t, :], rstd[:, 1, t:t + 1], None,
                                        ALU.mult).then_inc(normed, 1)
                v.wait_ge(t_mm, t + 1)
                if t >= 2:
                    v.wait_ge(h_lo, t - 1)
                for k in range(KD // 2, KD):
                    ins = nc.vector.tensor_scalar(temp[:, t % 2, k, :], t_ps[t % 2][:, k * P:(k + 1) * P],
                                                  gs2[:, k:k + 1], mod[:, 3 * KD + k:3 * KD + k + 1], ALU.mult, ALU.add)
                ins.then_inc(t_dve, 1)
                v.wait_ge(t_dve, t + 1)
                v.wait_ge(t_act, t + 1)
                nc.vector.tensor_copy(hp[:, :, 0, t * P:(t + 1) * P], temp[:, t % 2]).then_inc(h_hi, 1)


A_ROWS = 4
B_COLS = 4
CAND_A = A_ROWS * TOPK
CAND = CAND_A + (TOPK - A_ROWS) * B_COLS
LOWEST = -3.0e38
ROUTE_STEPS = 141


def routing(nc, io, keep):
    with ExitStack() as ctx:
        signals = ctx.enter_context(Signals(nc))

        def sb(name, shape, dt=F32):
            return ctx.enter_context(nc.sbuf_tensor(f"routing_{name}", shape, dt))

        def sem(name):
            return signals.new(f"routing_{name}")

        hp, route, acc = keep["hp"], keep["route"], keep["acc"]
        u_raw = sb("u_raw", [P, GROUP, D])
        u_part = sb("u_part", [P, GROUP, 2, D], BF16)
        wq_raw = sb("wq_raw", [P, 2, D])
        wq_part = sb("wq_part", [P, 2, 2, D], BF16)
        key_sb = sb("key_sb", [P, 2, PK])
        iota16 = sb("iota16", [P, TOPK])
        qh = sb("qh", [P, 2, SEQ])
        sc = sb("sc", [P, 2, NT, PK])
        rest = sb("rest", [P, 2, NT, PK])
        best = sb("best", [P, 2, NT, TOPK])
        at = sb("at", [P, 2, NT, TOPK], U32)
        atf = sb("atf", [P, 2, NT, TOPK])
        cand = sb("cand", [P, NT, CAND])
        cand_rest = sb("cand_rest", [P, NT, CAND])
        top = sb("top", [P, NT, TOPK])
        pos = sb("pos", [P, NT, TOPK], U32)
        shr = sb("shr", [P, 2, NT, TOPK], U32)
        low = sb("low", [P, 2, NT, TOPK], U32)
        late = sb("late", [P, NT, TOPK])
        diff = sb("diff", [P, 2, NT, TOPK])
        rank = sb("rank", [P, 2, NT, TOPK])
        hot = sb("hot", [P, 2, NT * TOPK, TOPK])
        gate = sb("gate", [P, NT, TOPK])
        gsum = sb("gsum", [P, NT])
        q_ps = [ctx.enter_context(nc.psum_tensor(f"q_ps{i}", [P, NH * HALF], F32)) for i in range(2)]
        s_ps = [ctx.enter_context(nc.psum_tensor(f"sc_ps{i}", [P, NT, PK], F32)) for i in range(2)]

        w_in = [sem(f"wq_in{i}") for i in range(2)]
        key_in = [sem(f"key_in{i}") for i in range(2)]
        iota_in = sem("iota_in")
        u_in = sem("u_in")
        u_hi = sem("u_hi")
        u_lo = sem("u_lo")
        a_mm = sem("a_mm")
        gelu_done = sem("gelu_done")
        wq_hi = sem("wq_hi")
        wq_lo = sem("wq_lo")
        q_mm = sem("q_mm")
        q_out = sem("q_out")
        s_mm = sem("s_mm")
        s_out = sem("s_out")
        found = sem("found")
        shifted = sem("shifted")
        exp_done = sem("gate_exp")
        marked = sem("marked")
        picked = sem("picked")
        dve = sem("dve")

        block = ctx.enter_context(nc.Block())

        @block.sync
        def _(sp):
            sp.dma_start(iota16[:], io["iota"][:, 0:TOPK]).then_inc(iota_in, 16)
            for s in range(2):
                sp.dma_start(wq_raw[:, s], io["wq_t"][s]).then_inc(w_in[s], 16)
                sp.dma_start(key_sb[:, s], io["keys_t"][s]).then_inc(key_in[s], 16)
            sp.dma_start(u_raw[:], io["u_t"][0:GROUP].rearrange("i p n -> p i n")).then_inc(u_in, 16)
            with sp.Fori(1, PH) as h:
                for s in range(2):
                    sp.wait_ge(wq_lo, 2 * h + s - 1)
                    sp.dma_start(wq_raw[:, s], io["wq_t"][2 * h + s]).then_inc(w_in[s], 16)
                for s in range(2):
                    sp.wait_ge(s_mm, 2 * h + s + 1)
                    sp.dma_start(key_sb[:, s], io["keys_t"][2 * h + s]).then_inc(key_in[s], 16)

        @block.tensor
        def _(pe):
            pe.sem_inc(q_out, 2)
            pe.sem_inc(s_out, 2)
            pe.sem_inc(s_mm, 2)
            pe.sem_inc(q_mm, 2)

            def queries(h, s):
                pe.wait_ge(wq_lo, 2 * h + s + 1)
                pe.wait_ge(q_out, 2 * h + s + 1)
                for half in range(NH):
                    terms = [(a, b, k) for a, b in PARTS for k in range(KD)]
                    for i, (a, b, k) in enumerate(terms):
                        last = nc.tensor.matmul(q_ps[s][:, half * HALF:(half + 1) * HALF],
                                                wq_part[:, s, a, k * P:(k + 1) * P],
                                                hp[:, k, b, half * HALF:(half + 1) * HALF], start=(i == 0),
                                                stop=(i == len(terms) - 1))
                last.then_inc(q_mm, 1)

            def scores(h, s):
                pe.wait_ge(q_out, 2 * h + s + 3)
                pe.wait_ge(key_in[s], 16 * h + 16)
                pe.wait_ge(s_out, 2 * h + s + 1)
                for t in range(NT):
                    last = nc.tensor.matmul(s_ps[s][:, t, :], qh[:, s, t * P:(t + 1) * P], key_sb[:, s, :],
                                            start=True, stop=True)
                last.then_inc(s_mm, 1)

            for s in range(2):
                queries(0, s)
                scores(0, s)
            with pe.Fori(1, PH) as h:
                for s in range(2):
                    queries(h, s)
                for s in range(2):
                    scores(h, s)
            pe.wait_ge(u_lo, GROUP)
            pe.wait_ge(q_out, 2 * PH + 2)
            for n in range(NH * GROUP):
                i, half = divmod(n, NH)
                if n >= 2 * NH:
                    pe.wait_ge(gelu_done, n - 2 * NH + 1)
                terms = [(a, b, k) for a, b in PARTS for k in range(KD)]
                for m, (a, b, k) in enumerate(terms):
                    last = nc.tensor.matmul(q_ps[i % 2][:, half * HALF:(half + 1) * HALF],
                                            u_part[:, i, a, k * P:(k + 1) * P],
                                            hp[:, k, b, half * HALF:(half + 1) * HALF], start=(m == 0),
                                            stop=(m == len(terms) - 1))
                last.then_inc(a_mm, 1)

        @block.scalar
        def _(act):
            def take_weights(h):
                for s in range(2):
                    act.wait_ge(w_in[s], 16 * h + 16)
                    act.wait_ge(q_mm, 2 * h + s + 1)
                    nc.scalar.copy(wq_part[:, s, 0, :], wq_raw[:, s]).then_inc(wq_hi, 1)

            def copy_queries(h, s):
                act.wait_ge(q_mm, 2 * h + s + 3)
                act.wait_ge(s_mm, 2 * h + s + 1)
                nc.scalar.copy(qh[:, s, :], q_ps[s][:]).then_inc(q_out, 1)

            def copy_scores(h, s):
                act.wait_ge(s_mm, 2 * h + s + 3)
                act.wait_ge(found, 2 * h + s + 1)
                nc.scalar.copy(sc[:, s], s_ps[s][:]).then_inc(s_out, 1)

            def head(h, first=False, last=False):
                if first:
                    for s in range(2):
                        copy_queries(h, s)
                        copy_scores(h, s)
                else:
                    for s in range(2):
                        copy_queries(h, s)
                    for s in range(2):
                        copy_scores(h, s)
                if not last:
                    take_weights(h + 1)
                act.wait_ge(shifted, h + 1)
                nc.scalar.activation(gate[:], gate[:], ACT.Exp).then_inc(exp_done, 1)

            take_weights(0)
            act.wait_ge(u_in, 16)
            for i in range(GROUP):
                nc.scalar.copy(u_part[:, i, 0, :], u_raw[:, i]).then_inc(u_hi, 1)
            head(0, first=True)
            with act.Fori(1, PH - 1) as h:
                head(h)
            head(PH - 1, last=True)
            for n in range(NH * GROUP):
                i, half = divmod(n, NH)
                act.wait_ge(a_mm, n + 1)
                nc.scalar.activation(acc[:, i, half, :], q_ps[i % 2][:, half * HALF:(half + 1) * HALF],
                                     ACT.Gelu_apprx_tanh).then_inc(gelu_done, 1)

        @block.gpsimd
        def _(pool):
            def split_weights(h):
                for s in range(2):
                    pool.wait_ge(wq_hi, 2 * h + s + 1)
                    nc.gpsimd.tensor_tensor(wq_part[:, s, 1, :], wq_raw[:, s], wq_part[:, s, 0, :],
                                            ALU.subtract).then_inc(wq_lo, 1)

            def pick(h):
                pool.wait_ge(marked, h + 1)
                for s in range(2):
                    hs = hot[:, s].rearrange("p (t k) m -> p t k m", k=TOPK)
                    nc.gpsimd.tensor_tensor(hs, hs, atf[:, s].unsqueeze(2).to_broadcast([P, NT, TOPK, TOPK]),
                                            ALU.mult).then_inc(picked, 1)

            split_weights(0)
            for i in range(GROUP):
                pool.wait_ge(u_hi, i + 1)
                nc.gpsimd.tensor_tensor(u_part[:, i, 1, :], u_raw[:, i], u_part[:, i, 0, :],
                                        ALU.subtract).then_inc(u_lo, 1)
            split_weights(1)
            with pool.Fori(0, PH - 2) as h:
                split_weights(h + 2)
                pick(h)
            for h in range(PH - 2, PH):
                pick(h)

        @block.vector
        def _(v):
            v.wait_ge(iota_in, 16)
            v.sem_inc(found, 2)

            def sum_picks(h, up):
                v.wait_ge(picked, 2 * h + 2)
                for s in range(2):
                    up(nc.vector.tensor_reduce(route[:, s, :, bass.ts(h, TOPK)],
                                               hot[:, s].rearrange("p (t k) m -> p t k m", k=TOPK), AX_X, ALU.add))

            def head(h, first):
                c = Count(dve)

                def ready():
                    v.wait_ge(dve, ROUTE_STEPS * h + c.n)
                    v.nop(nofuse=True)

                for s in range(2):
                    v.wait_ge(s_out, 2 * h + s + 3)
                    v.nop(nofuse=True)
                    for t in range(NT):
                        c.up(nc.vector.max(best[:, s, t, 0:8], sc[:, s, t, :]))
                    ready()
                    for t in range(NT):
                        c.up(nc.vector.match_replace(rest[:, s, t, :], best[:, s, t, 0:8], sc[:, s, t, :], LOWEST))
                    for t in range(NT):
                        c.up(nc.vector.max_index(at[:, s, t, 0:8], best[:, s, t, 0:8], sc[:, s, t, :]))
                    ready()
                    v.sem_inc(found, 1)
                    for t in range(NT):
                        c.up(nc.vector.max(best[:, s, t, 8:16], rest[:, s, t, :]))
                    ready()
                    for t in range(NT):
                        c.up(nc.vector.max_index(at[:, s, t, 8:16], best[:, s, t, 8:16], rest[:, s, t, :]))
                if first:
                    v.sem_inc(dve, 2)
                    c.n += 2
                else:
                    sum_picks(h - 1, c.up)
                ready()
                c.up(nc.vector.tensor_copy(atf[:], at[:]))
                a, b = best[:, 0], best[:, 1]
                c.up(nc.vector.tensor_tensor(
                    cand[:, :, 0:CAND_A].rearrange("p t (a b) -> p t a b", b=TOPK),
                    a[:, :, 0:A_ROWS].unsqueeze(3).to_broadcast([P, NT, A_ROWS, TOPK]),
                    b.unsqueeze(2).to_broadcast([P, NT, A_ROWS, TOPK]), ALU.add))
                c.up(nc.vector.tensor_tensor(
                    cand[:, :, CAND_A:].rearrange("p t (a b) -> p t a b", b=B_COLS),
                    a[:, :, A_ROWS:].unsqueeze(3).to_broadcast([P, NT, TOPK - A_ROWS, B_COLS]),
                    b[:, :, 0:B_COLS].unsqueeze(2).to_broadcast([P, NT, TOPK - A_ROWS, B_COLS]), ALU.add))
                ready()
                for t in range(NT):
                    c.up(nc.vector.max(top[:, t, 0:8], cand[:, t, :]))
                ready()
                for t in range(NT):
                    c.up(nc.vector.match_replace(cand_rest[:, t, :], top[:, t, 0:8], cand[:, t, :], LOWEST))
                for t in range(NT):
                    c.up(nc.vector.max_index(pos[:, t, 0:8], top[:, t, 0:8], cand[:, t, :]))
                ready()
                for t in range(NT):
                    c.up(nc.vector.max(top[:, t, 8:16], cand_rest[:, t, :]))
                ready()
                nc.vector.tensor_tensor(gate[:], top[:], top[:, :, 0:1].to_broadcast([P, NT, TOPK]),
                                        ALU.subtract).then_inc(shifted, 1)
                for t in range(NT):
                    c.up(nc.vector.max_index(pos[:, t, 8:16], top[:, t, 8:16], cand_rest[:, t, :]))
                ready()
                c.up(nc.vector.tensor_scalar(shr[:, 0], pos[:], 4, None, ALU.logical_shift_right))
                c.up(nc.vector.tensor_scalar(shr[:, 1], pos[:], 2, None, ALU.logical_shift_right))
                c.up(nc.vector.tensor_scalar(low[:, 0], pos[:], TOPK - 1, None, ALU.bitwise_and))
                c.up(nc.vector.tensor_scalar(low[:, 1], pos[:], B_COLS - 1, None, ALU.bitwise_and))
                c.up(nc.vector.tensor_scalar(late[:], pos[:], float(CAND_A), None, ALU.is_ge))
                ready()
                c.up(nc.vector.scalar_tensor_tensor(diff[:, 0], shr[:, 1], float(CAND_A // B_COLS - A_ROWS), shr[:, 0],
                                                    ALU.subtract, ALU.subtract))
                c.up(nc.vector.tensor_tensor(diff[:, 1], low[:, 1], low[:, 0], ALU.subtract))
                ready()
                for s in range(2):
                    c.up(nc.vector.tensor_tensor(diff[:, s], diff[:, s], late[:], ALU.mult))
                ready()
                c.up(nc.vector.tensor_tensor(rank[:, 0], diff[:, 0], shr[:, 0], ALU.add))
                c.up(nc.vector.tensor_tensor(rank[:, 1], diff[:, 1], low[:, 0], ALU.add))
                ready()
                flat = [P, NT * TOPK, TOPK]
                for s in range(2):
                    c.up(nc.vector.tensor_tensor(
                        hot[:, s], rank[:, s].rearrange("p t k -> p (t k)").unsqueeze(2).to_broadcast(flat),
                        iota16[:].unsqueeze(1).to_broadcast(flat), ALU.is_equal))
                ready()
                v.sem_inc(marked, 1)
                v.wait_ge(exp_done, h + 1)
                c.up(nc.vector.tensor_reduce(gsum[:], gate[:], AX_X, ALU.add))
                ready()
                c.up(nc.vector.reciprocal(gsum[:], gsum[:]))
                ready()
                c.up(nc.vector.tensor_tensor(route[:, 2, :, bass.ts(h, TOPK)], gate[:],
                                             gsum[:].unsqueeze(2).to_broadcast([P, NT, TOPK]), ALU.mult))
                ready()
                assert c.n == ROUTE_STEPS, c.n

            head(0, True)
            with v.Fori(1, PH) as h:
                head(h, False)
            c = Count(dve)
            sum_picks(PH - 1, c.up)


SLOT = 64
ITER = 2 * SLOT
TURNS = SEQ // ITER
PERG = HALF // PK
BATCH = 8


def gates(nc, io, keep):
    with ExitStack() as ctx:
        signals = ctx.enter_context(Signals(nc))

        def sb(name, shape, dt=F32):
            return ctx.enter_context(nc.sbuf_tensor(f"gates_{name}", shape, dt))

        def sem(name):
            return signals.new(f"gates_{name}")

        ident, route = keep["ident"], keep["route"]
        iota = sb("iota_sb", [P, PK])
        routeT = sb("routeT", [P, 3, SEQ])
        HOTS = 4
        MARKS = 2
        col_hot = sb("col_hot", [P, HOTS, BATCH, PK])
        row_mark = sb("row_mark", [P, MARKS, BATCH, PK])
        SHARE = 4
        act_mark = route
        one = sb("one", [P, 1])
        row_hot = sb("row_hot", [P, HOTS, BATCH, PK])
        table = sb("table", [P, 2, PK, SLOT])
        t_ps = [ctx.enter_context(nc.psum_tensor(f"rt_ps{i}", [P, 4, P], F32)) for i in range(2)]
        g_ps = [ctx.enter_context(nc.psum_tensor(f"g_ps{i}", [P, PERG, PK], F32)) for i in range(4)]

        iota_in = sem("iota_in")
        turned = sem("turned")
        routeT_done = sem("routeT_done")
        col_done = sem("col_done")
        mark_done = sem("mark_done")
        act_far = sem("act_far")
        act_marked = sem("act_marked")
        one_set = sem("one_set")
        row_done = sem("row_done")
        g_mm = sem("g_mm")
        g_out = sem("g_out")
        table_out = keep["table_out"]
        NB = ITER // BATCH
        BANKS_B = BATCH // PERG
        assert NB % (2 * SHARE) == 0
        NA = NB // SHARE
        CREDIT = 2 * SHARE
        by_dve = [n for n in range(NB) if n % SHARE < SHARE - 1]
        jobs = [(c, q) for c in range(3) for q in range(NT // 4)]

        def of_tokens(c, b):
            return routeT[:, c, bass.ds(b * BATCH, BATCH)].unsqueeze(2).to_broadcast([P, BATCH, PK])

        block = ctx.enter_context(nc.Block())

        @block.sync
        def _(sp):
            sp.dma_start(iota[:], io["iota"]).then_inc(iota_in, 16)
            for i in range(2):
                sp.dma_start(keep["u_raw"][:, i], io["u_t"][GROUP + i]).then_inc(keep["u_in"][i], 16)
            for s in range(2):
                sp.sem_inc(table_out[s], 16)
            with sp.Fori(0, TURNS) as i:
                for s in range(2):
                    sp.wait_ge(g_out, (2 * i + s + 1) * (SLOT // PERG) + 4)
                    sp.dma_start(io["gates"][2 * i + s], table[:, s]).then_inc(table_out[s], 16)

        @block.tensor
        def _(pe):
            for n, (c, q) in enumerate(jobs):
                if n >= 2:
                    pe.wait_ge(routeT_done, n - 1)
                for j in range(4):
                    last = nc.tensor.transpose(t_ps[n % 2][:, j, :], route[:, c, 4 * q + j, :], ident[:])
                last.then_inc(turned, 1)
            pe.sem_inc(g_out, 4)
            pe.sem_inc(g_mm, HOTS * BANKS_B)
            with pe.Fori(0, TURNS) as i:
                for m in range(ITER // PERG):
                    n, part = divmod(m, BANKS_B)
                    if part == 0:
                        pe.wait_ge(col_done, i * NB + n + 1)
                        pe.wait_ge(row_done, i * NB + n + 1 + CREDIT)
                    pe.wait_ge(g_out, i * (ITER // PERG) + m + 1)
                    for j in range(PERG):
                        last = nc.tensor.matmul(g_ps[m % 4][:, j, :], col_hot[:, n % HOTS, part * PERG + j, :],
                                                row_hot[:, n % HOTS, part * PERG + j, :], start=True, stop=True)
                    last.then_inc(g_mm, 1)

        @block.scalar
        def _(act):
            def mark(i, q):
                n = SHARE * q + SHARE - 1
                b = i * NB + n
                act.wait_ge(row_done, b - 2 * SHARE + 1 + CREDIT)
                for k in range(BATCH):
                    nc.scalar.activation(act_mark[:, q % 2, k, :], iota[:], ACT.Abs, scale=-1.0,
                                         bias=routeT[:, 0, bass.ds(b * BATCH + k, 1)]).then_inc(act_far, 1)
                act.wait_ge(act_far, (i * NA + q + 1) * BATCH)
                nc.scalar.activation(act_mark[:, q % 2], act_mark[:, q % 2], ACT.Relu, scale=-1.0,
                                     bias=one[:, 0:1]).then_inc(act_marked, 1)

            act.wait_ge(iota_in, 16)
            act.wait_ge(one_set, 1)
            act.wait_ge(turned, len(jobs))
            act.wait_ge(routeT_done, len(jobs))
            with act.Fori(0, TURNS) as i:
                for b in range(ITER // PERG):
                    if b % (BANKS_B * SHARE) == 0:
                        mark(i, b // (BANKS_B * SHARE))
                    s, n = divmod(b * PERG, SLOT)
                    if n == 0:
                        act.wait_ge(table_out[s], 16 * i + 16)
                    act.wait_ge(g_mm, i * (ITER // PERG) + b + 1 + HOTS * BANKS_B)
                    nc.scalar.copy(table[:, s, :, n:n + PERG].rearrange("p i n -> p n i"),
                                   g_ps[b % 4][:]).then_inc(g_out, 1)

        @block.vector
        def _(v):
            for n, (c, q) in enumerate(jobs):
                v.wait_ge(turned, n + 1)
                nc.vector.tensor_copy(routeT[:, c, q * HALF:(q + 1) * HALF],
                                      t_ps[n % 2][:].rearrange("p a b -> p (a b)")).then_inc(routeT_done, 1)
            v.wait_ge(routeT_done, len(jobs))
            v.wait_ge(iota_in, 16)
            iotas = iota[:].unsqueeze(1).to_broadcast([P, BATCH, PK])
            with v.Fori(0, TURNS) as i:
                for n in range(NB):
                    b = i * NB + n
                    v.wait_ge(g_mm, b * BANKS_B + BANKS_B)
                    nc.vector.tensor_tensor(col_hot[:, n % HOTS], iotas, of_tokens(1, b), ALU.is_equal).then_inc(col_done, 1)
                    if n not in by_dve:
                        continue
                    d = by_dve.index(n)
                    last = by_dve[d - MARKS] - (NB if d < MARKS else 0)
                    v.wait_ge(row_done, i * NB + last + 1 + CREDIT)
                    nc.vector.tensor_tensor(row_mark[:, d % MARKS], iotas, of_tokens(0, b),
                                            ALU.is_equal).then_inc(mark_done, 1)

        @block.gpsimd
        def _(pool):
            nc.gpsimd.memset(one[:], 1.0).then_inc(one_set, 1)
            pool.sem_inc(row_done, CREDIT)
            with pool.Fori(0, TURNS) as i:
                for n in range(NB):
                    b = i * NB + n
                    pool.wait_ge(g_mm, b * BANKS_B + BANKS_B)
                    if n in by_dve:
                        d = by_dve.index(n)
                        pool.wait_ge(mark_done, i * len(by_dve) + d + 1)
                        marks = row_mark[:, d % MARKS]
                    else:
                        q = n // SHARE
                        pool.wait_ge(act_marked, i * NA + q + 1)
                        marks = act_mark[:, q % 2]
                    nc.gpsimd.tensor_tensor(row_hot[:, n % HOTS], marks, of_tokens(2, b), ALU.mult).then_inc(row_done, 1)


def experts(nc, io, keep):
    with ExitStack() as ctx:
        signals = ctx.enter_context(Signals(nc))

        def sb(name, shape, dt=F32):
            return ctx.enter_context(nc.sbuf_tensor(f"experts_{name}", shape, dt))

        def sem(name):
            return signals.new(f"experts_{name}")

        hp, rows2, acc, table_out, u_raw, u_in = (
            keep[n] for n in ("hp", "rows2", "acc", "table_out", "u_raw", "u_in"))
        v_raw = sb("v_raw", [P, D])
        u_part = sb("u_part", [P, GROUP, 2, D], BF16)
        v_part = sb("v_part", [P, 2, GROUP, 2, D], BF16)
        w_part = sb("w_part", [P, 2, GROUP, 2, SEQ], BF16)
        CHUNKS = SEQ // SLOT
        g_sb = sb("g_sb", [P, 2, CHUNKS, GROUP * SLOT])
        ACTS = 4
        act_sb = sb("act_sb", [P, ACTS, HALF])
        stat = sb("stat", [P, 3, NT])
        whole = acc[:].rearrange("p t h n -> p t (h n)")
        a_ps = [ctx.enter_context(nc.psum_tensor(f"a_ps{i}", [P, HALF], F32)) for i in range(4)]
        b_ps = [ctx.enter_context(nc.psum_tensor(f"b_ps{i}", [P, HALF], F32)) for i in range(4)]

        v_in = sem("v_in")
        g_in = [sem(f"g_in{i}") for i in range(2)]
        u_hi = sem("u_hi")
        u_lo = sem("u_lo")
        v_hi = sem("v_hi")
        v_lo = sem("v_lo")
        a_mm = sem("a_mm")
        gelu_done = sem("gelu_done")
        prod_done = sem("prod_done")
        w_hi = sem("w_hi")
        w_lo = sem("w_lo")
        b_mm = sem("b_mm")
        acc_done = sem("acc_done")
        f_ssq = sem("f_ssq")
        f_std = sem("f_std")
        f_rstd = sem("f_rstd")
        f_norm = sem("f_norm")
        f_done = sem("f_done")
        out_done = sem("out_done")

        UA = 2 * GROUP
        UB = NH * NT

        def schedule(eng, a, b):
            a(0, 0)
            a(1, 1)
            b(0, 0)
            with eng.Fori(0, (GROUPS - 4) // 2) as it:
                for s in range(2):
                    a(2 * it + s + 2, s)
                    b(2 * it + s + 1, 1 - s)
            for g in range(GROUPS - 3, GROUPS - 1):
                a(g + 1, (g + 1) % 2)
                b(g, g % 2)
            b(GROUPS - 1, 1)

        def within(g, n):
            return isinstance(g, int) and g >= GROUPS - n

        def wait(eng, semaphore, value):
            if not isinstance(value, int) or value > 0:
                eng.wait_ge(semaphore, value)

        block = ctx.enter_context(nc.Block())

        @block.sync
        def _(sp):
            def load_g(g, s):
                wait(sp, w_lo, UA * (g - 1))
                sp.dma_start(g_sb[:, s], io["gates"][:, :, bass.ts(g, GROUP), :].rearrange("c j i n -> j c (i n)"))\
                  .then_inc(g_in[s], 16)

            def load_u(g, i):
                wait(sp, u_lo, GROUP * g + i - 1)
                sp.dma_start(u_raw[:, i % 2], io["u_t"][GROUP * g + i]).then_inc(u_in[i % 2], 16)

            def load_v(g):
                for i in range(GROUP):
                    wait(sp, v_lo, GROUP * g + i)
                    sp.dma_start(v_raw[:], io["v"][GROUP * g + i]).then_inc(v_in, 16)

            def a(g, s):
                if isinstance(g, int) and g == 0:
                    for i in range(2):
                        sp.sem_inc(u_in[i], 16 * GROUP // 2)
                    for i in range(2, GROUP):
                        load_u(1, i)
                    for i in range(2):
                        sp.wait_ge(table_out[i], 16 * (TURNS + 1))
                    load_g(0, 0)
                    load_v(0)
                    load_g(1, 1)
                elif not isinstance(g, int) or g > 1:
                    for i in range(1, GROUP):
                        load_u(g, i)

            def b(g, s):
                if not within(g, 2):
                    load_g(g + 2, s)
                if not within(g, 1):
                    load_v(g + 1)
                if not within(g, 2):
                    load_u(g + 2, 0)

            schedule(sp, a, b)
            for t in range(NT):
                if t == 0:
                    sp.wait_ge(u_lo, PK)
                if t >= 2:
                    sp.wait_ge(f_done, t - 1)
                    sp.wait_ge(out_done, 16 * (t - 1))
                sp.dma_start(u_raw[:, t % 2], io["x2"][t * P:(t + 1) * P, :]).then_inc(u_in[t % 2], 16)
                if t >= 1:
                    sp.wait_ge(u_in[(t - 1) % 2], 16 * (PK // 2 + (t - 1) // 2 + 1))
                    sp.wait_ge(f_done, t)
                    sp.dma_start(io["out"][(t - 1) * P:t * P, :], u_raw[:, (t - 1) % 2]).then_inc(out_done, 16)
            sp.wait_ge(u_in[(NT - 1) % 2], 16 * (PK // 2 + NT // 2))
            sp.wait_ge(f_done, NT)
            sp.dma_start(io["out"][(NT - 1) * P:NT * P, :], u_raw[:, (NT - 1) % 2]).then_inc(out_done, 16)
            sp.wait_ge(out_done, 16 * NT)

        @block.tensor
        def _(pe):
            def a(g, s):
                if isinstance(g, int) and g == 0:
                    pe.sem_inc(a_mm, UA)
                    return
                for i in range(GROUP):
                    pe.wait_ge(u_lo, GROUP * g + i + 1)
                    for h in range(NH):
                        n = NH * i + h
                        wait(pe, gelu_done, UA * g + n - 3)
                        terms = [(wp, mp, k) for wp, mp in PARTS for k in range(KD)]
                        for m, (wp, mp, k) in enumerate(terms):
                            last = nc.tensor.matmul(a_ps[n % 4][:], u_part[:, i, wp, k * P:(k + 1) * P],
                                                    hp[:, k, mp, h * HALF:(h + 1) * HALF], start=(m == 0),
                                                    stop=(m == len(terms) - 1))
                        last.then_inc(a_mm, 1)

            def b(g, s):
                pe.wait_ge(w_lo, UA * g + UA)
                pe.wait_ge(v_lo, GROUP * g + GROUP)
                for t in range(NT):
                    for h in range(NH):
                        n = NH * t + h
                        wait(pe, acc_done, UB * g + n - 3)
                        terms = [(i, wp, vp) for i in range(GROUP) for wp, vp in PARTS]
                        for m, (i, wp, vp) in enumerate(terms):
                            last = nc.tensor.matmul(b_ps[n % 4][:], w_part[:, s, i, wp, t * P:(t + 1) * P],
                                                    v_part[:, s, i, vp, h * HALF:(h + 1) * HALF], start=(m == 0),
                                                    stop=(m == len(terms) - 1))
                        last.then_inc(b_mm, 1)

            schedule(pe, a, b)

        @block.scalar
        def _(act):
            def take_u(g, i):
                e = GROUP * g + i
                act.wait_ge(u_in[i % 2], 2 * 16 * g + 16 * (i // 2 + 1))
                wait(act, a_mm, NH * (e - GROUP) + NH)
                nc.scalar.copy(u_part[:, i, 0, :], u_raw[:, i % 2]).then_inc(u_hi, 1)

            def take_v(g, s, tiles=range(GROUP)):
                wait(act, b_mm, UB * (g - 1))
                for i in tiles:
                    act.wait_ge(v_in, 16 * (GROUP * g + i + 1))
                    nc.scalar.copy(v_part[:, s, i, 0, :], v_raw[:]).then_inc(v_hi, 1)

            def round_w(g, s, n):
                act.wait_ge(prod_done, UA * g + n + 1)
                if n == 0:
                    wait(act, b_mm, UB * (g - 1))
                i, h = divmod(n, NH)
                nc.scalar.copy(w_part[:, s, i, 0, h * HALF:(h + 1) * HALF], act_sb[:, n % ACTS, :]).then_inc(w_hi, 1)

            def a(g, s):
                if isinstance(g, int) and g == 0:
                    act.sem_inc(u_hi, GROUP)
                    act.sem_inc(gelu_done, UA)
                    for i in range(GROUP):
                        take_u(1, i)
                    for n in range(UA):
                        act.wait_ge(a_mm, UA + n + 1)
                        nc.scalar.activation(acc[:, GROUP + n // NH, n % NH, :], a_ps[n % 4][:],
                                             ACT.Gelu_apprx_tanh).then_inc(gelu_done, 1)
                        if n == 2:
                            for i in range(2):
                                act.wait_ge(table_out[i], 16 * (TURNS + 1))
                        if 2 <= n < 2 + GROUP:
                            take_v(0, 0, [n - 2])
                        if n >= UA // 2:
                            round_w(0, 0, 2 * n - UA)
                            round_w(0, 0, 2 * n - UA + 1)
                    return
                for i in range(GROUP):
                    for h in range(NH):
                        n = NH * i + h
                        if isinstance(g, int) and g == 1:
                            round_w(g, s, n)
                            continue
                        if h == 0 and i + 1 < GROUP:
                            take_u(g, i + 1)
                        act.wait_ge(a_mm, UA * g + n + 1)
                        wait(act, w_lo, UA * g + n - ACTS + 1)
                        nc.scalar.activation(act_sb[:, n % ACTS, :], a_ps[n % 4][:],
                                             ACT.Gelu_apprx_tanh).then_inc(gelu_done, 1)
                        if n >= 1:
                            round_w(g, s, n - 1)
                if not isinstance(g, int) or g > 1:
                    round_w(g, s, UA - 1)

            def b(g, s):
                if not within(g, 1):
                    take_v(g + 1, 1 - s)
                if not within(g, 2):
                    take_u(g + 2, 0)

            schedule(act, a, b)
            for t in range(NT):
                act.wait_ge(acc_done, (GROUPS - 1) * UB + NH * (t + 1))
                if t >= 1:
                    act.wait_ge(f_ssq, t)
                nc.scalar.activation(g_sb[:, 0, 0:4, :].rearrange("p a b -> p (a b)"),
                                     whole[:, t, :], ACT.Square,
                                     accum_out=stat[:, 0, t:t + 1]).then_inc(f_ssq, 1)
                act.wait_ge(f_ssq, t + 1)
                nc.scalar.activation(stat[:, 1, t:t + 1], stat[:, 0, t:t + 1], ACT.Sqrt, bias=keep["eps"][:, 0:1],
                                     scale=1.0 / D).then_inc(f_std, 1)

        @block.gpsimd
        def _(pool):
            def take_u(g, i):
                pool.wait_ge(u_hi, GROUP * g + i + 1)
                nc.gpsimd.tensor_tensor(u_part[:, i, 1, :], u_raw[:, i % 2], u_part[:, i, 0, :],
                                        ALU.subtract).then_inc(u_lo, 1)

            def take_v(g, s):
                for i in range(GROUP):
                    pool.wait_ge(v_hi, GROUP * g + i + 1)
                    nc.gpsimd.tensor_tensor(v_part[:, s, i, 1, :], v_raw[:], v_part[:, s, i, 0, :],
                                            ALU.subtract).then_inc(v_lo, 1)

            def a(g, s):
                if isinstance(g, int) and g == 0:
                    pool.sem_inc(u_lo, GROUP)
                    for i in range(GROUP):
                        take_u(1, i)
                    take_v(0, 0)
                elif not isinstance(g, int) or g > 1:
                    for i in range(1, GROUP):
                        take_u(g, i)

            def b(g, s):
                if not within(g, 1):
                    take_v(g + 1, 1 - s)
                if not within(g, 2):
                    take_u(g + 2, 0)

            schedule(pool, a, b)

        @block.vector
        def _(v):
            def low_w(g, s, n):
                i, h = divmod(n, NH)
                v.wait_ge(w_hi, UA * g + n + 1)
                nc.vector.tensor_tensor(w_part[:, s, i, 1, h * HALF:(h + 1) * HALF], act_sb[:, n % ACTS, :],
                                        w_part[:, s, i, 0, h * HALF:(h + 1) * HALF], ALU.subtract).then_inc(w_lo, 1)

            def a(g, s):
                for n in range(UA):
                    i, h = divmod(n, NH)
                    v.wait_ge(gelu_done, UA * g + n + 1)
                    if n == 0:
                        v.wait_ge(g_in[s], 8 * (g - s) + 16)
                    cs = slice(h * CHUNKS // NH, (h + 1) * CHUNKS // NH)
                    gelu = act_sb[:, n % ACTS, :]
                    if isinstance(g, int) and g <= 1:
                        gelu = acc[:, GROUP * g + i, h, :]
                        wait(v, w_lo, UA * g + n - ACTS + 1)
                    nc.vector.tensor_tensor(act_sb[:, n % ACTS, :].rearrange("p (c n) -> p c n", n=SLOT),
                                            gelu.rearrange("p (c n) -> p c n", n=SLOT),
                                            g_sb[:, s, cs, i * SLOT:(i + 1) * SLOT], ALU.mult).then_inc(prod_done, 1)
                    if n >= 1:
                        low_w(g, s, n - 1)
                low_w(g, s, UA - 1)

            def b(g, s):
                for n in range(UB):
                    t, h = divmod(n, NH)
                    v.wait_ge(b_mm, UB * g + n + 1)
                    if isinstance(g, int) and g == 0:
                        if n == 0:
                            v.wait_ge(prod_done, 2 * UA)
                        nc.vector.tensor_copy(acc[:, t, h, :], b_ps[n % 4][:]).then_inc(acc_done, 1)
                    else:
                        v.wait_ge(acc_done, UB * g + n - UB + 1)
                        nc.vector.tensor_tensor(acc[:, t, h, :], acc[:, t, h, :], b_ps[n % 4][:], ALU.add)\
                            .then_inc(acc_done, 1)
                    if within(g, 1) and h == NH - 1 and t >= 1:
                        finish(t - 1)

            def finish(t):
                f = whole[:, t, :]
                v.wait_ge(f_std, t + 1)
                nc.vector.reciprocal(stat[:, 2, t:t + 1], stat[:, 1, t:t + 1]).then_inc(f_rstd, 1)
                v.wait_ge(f_rstd, t + 1)
                nc.vector.scalar_tensor_tensor(f, f, stat[:, 2, t:t + 1], rows2[:].rearrange("p a b -> p (a b)"),
                                               ALU.mult, ALU.mult).then_inc(f_norm, 1)
                v.wait_ge(f_norm, t + 1)
                v.wait_ge(u_in[t % 2], 16 * (PK // 2 + t // 2 + 1))
                nc.vector.tensor_tensor(u_raw[:, t % 2], u_raw[:, t % 2], f, ALU.add).then_inc(f_done, 1)

            schedule(v, a, b)
            finish(NT - 1)


def build(nc, io):
    with ExitStack() as ctx:
        def sb(stack, name, shape, dt=F32):
            return stack.enter_context(nc.sbuf_tensor(name, shape, dt))

        keep = {
            "vec": sb(ctx, "vec_sb", [P, V_END]),
            "ident": sb(ctx, "ident_sb", [P, P]),
            "mod": sb(ctx, "mod", [P, MODT]),
            "gs2": sb(ctx, "gs2", [P, KD]),
            "eps": sb(ctx, "eps", [P, 1]),
            "rows2": sb(ctx, "rows2", [P, NH, HALF]),
            "hp": sb(ctx, "hp", [P, KD, 2, SEQ], BF16),
        }
        with ExitStack() as mix:
            keep["rows1"] = sb(mix, "rows1", [P, NH, HALF])
            keep["conv"] = sb(mix, "conv", [P, CC, SEQ])
            keep["q"] = sb(mix, "q", [P, CA, SEQ])
            keep["att_p"] = keep["q"][:].bitcast(BF16).rearrange("p c (j s n) -> p c j s n", s=2, n=P)
            with ExitStack() as heads:
                keep["k"] = sb(heads, "k", [P, CA, SEQ])
                keep["kc"] = sb(heads, "kc", [P, CA, CTX])
                keep["hcp"] = sb(heads, "hcp", [P, KD, 2, CTX], BF16)
                keep["rstd_row"] = sb(heads, "rstd_row", [P, SEQ])
                with ExitStack() as whole:
                    keep["hw"] = sb(whole, "hw", [P, KD, SEQ])
                    keep["hcw"] = sb(whole, "hcw", [P, KD, CTX])
                    modulation(nc, io, keep)
                    projection(nc, io, keep)
                keep["v_p"] = sb(heads, "v_p", [P, NT, 2, D_NA], BF16)
                keep["vc_p"] = sb(heads, "vc_p", [P, CT, 2, D_NA], BF16)
                values(nc, io, keep)
                attention(nc, io, keep)
            output(nc, io, keep)
        keep["acc"] = sb(ctx, "acc", [P, NT, NH, HALF])
        signals = ctx.enter_context(Signals(nc))
        keep["table_out"] = [signals.new(f"table_out{i}") for i in range(2)]
        keep["u_raw"] = sb(ctx, "u_raw", [P, 2, D])
        keep["u_in"] = [signals.new(f"u_in{i}") for i in range(2)]
        with ExitStack() as chosen:
            keep["route"] = sb(chosen, "route", [P, 3, NT, PH * TOPK])
            routing(nc, io, keep)
            gates(nc, io, keep)
        experts(nc, io, keep)


def lay_out(a):
    import numpy as np

    def cols(v):
        return np.ascontiguousarray(v).reshape(-1, P).T

    arrays = {}
    arrays["x"] = a["x"][0]
    arrays["ctx"] = a["ctx"][0]
    cond = np.stack([cols(a["c"][0]), cols(a["c_ctx"])], axis=-1).reshape(P, 2 * KD)
    taps = a["conv_w"][0].reshape(TAPS, CC, P).transpose(2, 1, 0).reshape(P, CC * TAPS)
    arrays["vec"] = np.concatenate(
        [cols(a["b_ada"][0]), cols(a["g_pre_mix"][0]), cols(a["g_post_mix"][0]), cols(a["g_pre_ffn"][0]),
         cols(a["g_post_ffn"][0]), cols(a["conv_b"][0]), cols(a["conv_norm_g"][0]), cols(a["conv_norm_b"][0]), taps,
         cond], axis=1)
    arrays["w_ada"] = a["w_ada"][0]
    w_in = a["w_in"][0]
    nt = 2 * CC + 2 * CA
    arrays["w_in_t"] = w_in[:, :nt * P].reshape(KD, P, nt, P).transpose(2, 1, 0, 3)
    arrays["w_v"] = w_in[:, nt * P:]
    arrays["w_out"] = a["w_out"][0]
    wide = np.pad(a["na_rpb"][0], ((0, 0), (0, 0), (GRID_W - WIN_C, GRID_W - WIN_C)))
    arrays["rpb_t"] = np.stack([wide[:, :, GRID_W - 1 - q:2 * GRID_W - 1 - q] for q in range(GRID_W)], axis=1)
    q = np.arange(GRID_W)[:, None]
    k = np.arange(GRID_W)[None, :]
    first = np.clip(q - WIN_C // 2, 0, GRID_W - WIN_C)
    window = np.where((k >= first) & (k < first + WIN_C), 0.0, NEG).astype(np.float32)
    mask = np.tile(window[:, None, :], (2, BIAS_R, 1))
    mask[:GRID_W, T_ROWS + IN_ROWS - 1] = NEG
    mask[GRID_W:, T_ROWS] = NEG
    arrays["mask"] = mask.reshape(P, BIAS_R * GRID_W)
    arrays["ident"] = np.eye(P, dtype=np.float32)
    arrays["iota"] = np.tile(np.arange(PK, dtype=np.float32), (P, 1))
    arrays["wq_t"] = a["peer_wq"][0].reshape(KD, P, SUB, P).transpose(2, 1, 0, 3)
    arrays["keys_t"] = a["peer_keys"][0].reshape(SUB, PK, P).transpose(0, 2, 1)
    arrays["u_t"] = a["peer_u"][0].reshape(PK, PK, KD, P).transpose(0, 3, 2, 1).reshape(PK, P, D)
    arrays["v"] = a["peer_v"][0].reshape(PK, PK, D)
    return {name: np.ascontiguousarray(v) for name, v in arrays.items()}


def kernel(**inputs):
    import numpy as _np
    import concourse.bacc as _bacc
    from concourse import mybir as _mybir
    from concourse.bass_utils import run_bass_kernel_spmd as _run

    nc = _bacc.Bacc("TRN2", target_bir_lowering=False, num_devices=1)
    arrays = {f"in_{k}": v for k, v in lay_out({k: _np.asarray(v) for k, v in inputs.items()}).items()}
    io = {}
    for name, a in arrays.items():
        io[name[3:]] = nc.dram_tensor(name, a.shape, _mybir.dt.from_np(a.dtype), kind="ExternalInput").ap()
    io["out"] = nc.dram_tensor("out", (SEQ, D), F32, kind="ExternalOutput").ap()
    io["x2"] = nc.dram_tensor("x2", (SEQ, D), F32).ap()
    io["gates"] = nc.dram_tensor("gate_tables", (SEQ // SLOT, PK, PK, SLOT), F32).ap()
    build(nc, io)
    r = _run(nc, [arrays], core_ids=[0])
    return r.results[0]["out"].reshape(1, SEQ, D)
```
